# Optimizing a Trainium2 kernel written in Bass

```python
import math
import jax, jax.numpy as jnp
from jax import lax
import numpy as np

D_MODEL = 1024
BATCH = 1
SEQ = 256
DEPTH = 1

NSA_HEADS = 8
NSA_KV_GROUPS = 2
NSA_HPG = NSA_HEADS // NSA_KV_GROUPS
NSA_HEAD_DIM = 64
CMP_BLOCK = 32
CMP_STRIDE = 16
CMP_HIDDEN = 256
SLC_BLOCK = 64
SLC_COUNT = 16
WINDOW = 512
Q_BLOCK = 128
ROPE_THETA = 500000.0
ROPE_DIM = NSA_HEAD_DIM // 4
RET_HEADS = 4
RET_HEAD_DIM = 128
RET_CHUNK = 128
RET_ROT_BASE = 10000.0
MLP_HIDDEN = 4 * D_MODEL
NORM_EPS = 1e-6
NEG = -1e30
BIG = 1e30

NSA_Q_W = NSA_HEADS * NSA_HEAD_DIM
NSA_KV_W = NSA_KV_GROUPS * NSA_HEAD_DIM
RET_W = RET_HEADS * RET_HEAD_DIM
IN_SIZES = (NSA_Q_W, NSA_KV_W, NSA_KV_W, NSA_KV_W, NSA_KV_W, NSA_KV_W, NSA_KV_W, 3 * NSA_HEADS,
            RET_W, RET_W, RET_W, RET_W, D_MODEL, D_MODEL)
IN_WIDTH = sum(IN_SIZES)


def rmsnorm(x, g):
    xf = x.astype(jnp.float32)
    y = xf * lax.rsqrt(jnp.mean(xf * xf, axis=-1, keepdims=True) + NORM_EPS) * g.astype(jnp.float32)
    return y.astype(x.dtype)

def rotary(x, pos, rot_dim, base):
    half = rot_dim // 2
    inv = jnp.exp(-math.log(base) * jnp.arange(half, dtype=jnp.float32) * 2.0 / rot_dim)
    ang = pos.astype(jnp.float32)[..., None] * inv
    cos, sin = jnp.cos(ang)[:, :, None, :], jnp.sin(ang)[:, :, None, :]
    xf = x.astype(jnp.float32)
    x1, x2 = xf[..., :half], xf[..., half:rot_dim]
    out = jnp.concatenate([x1 * cos - x2 * sin, x1 * sin + x2 * cos, xf[..., rot_dim:]], axis=-1)
    return out.astype(x.dtype)

def nsa_mixer(q, kc, vc, ks, vs, kw, vw, gates, pe_k, pe_v, ck_w1, ck_w2, cv_w1, cv_w2):
    S = q.shape[0]
    dt = q.dtype
    G, HPG, dh = NSA_KV_GROUPS, NSA_HPG, NSA_HEAD_DIM
    n_cmp = (S - CMP_BLOCK) // CMP_STRIDE + 1
    n_slc = S // SLC_BLOCK
    n_sel = min(SLC_COUNT, n_slc)
    n_qb = S // Q_BLOCK
    scale = dh ** -0.5

    cmp_idx = jnp.arange(n_cmp)[:, None] * CMP_STRIDE + jnp.arange(CMP_BLOCK)[None, :]

    def compress(k, pe, w1, w2):
        blk = k[cmp_idx] + pe[None, :, None, :]
        blk = blk.transpose(0, 2, 1, 3).reshape(n_cmp, G, CMP_BLOCK * dh)
        return jax.nn.silu(blk @ w1) @ w2

    k_cmp = compress(kc, pe_k, ck_w1, ck_w2)
    v_cmp = compress(vc, pe_v, cv_w1, cv_w2)
    cmp_start = cmp_idx[:, 0]
    cmp_end = cmp_idx[:, -1]
    slc_start = jnp.arange(n_slc) * SLC_BLOCK
    overlap = jnp.clip(jnp.minimum(cmp_start[:, None] + CMP_BLOCK, slc_start[None, :] + SLC_BLOCK)
                       - jnp.maximum(cmp_start[:, None], slc_start[None, :]), 0, None)
    overlap = overlap.astype(jnp.float32) / CMP_BLOCK

    ks_b = ks.reshape(n_slc, SLC_BLOCK, G, dh).transpose(2, 0, 1, 3)
    vs_b = vs.reshape(n_slc, SLC_BLOCK, G, dh).transpose(2, 0, 1, 3)
    kw_pad = jnp.pad(kw, ((WINDOW, 0), (0, 0), (0, 0)))
    vw_pad = jnp.pad(vw, ((WINDOW, 0), (0, 0), (0, 0)))

    qg = q.reshape(S, G, HPG, dh)
    gg = jax.nn.sigmoid(gates.astype(jnp.float32)).reshape(S, G, HPG, 3)
    g_idx = jnp.arange(G)[:, None, None]
    blk_j = jnp.arange(n_slc)

    def block(b):
        s0 = b * Q_BLOCK
        qi = lax.dynamic_slice_in_dim(qg, s0, Q_BLOCK, 0)
        gi = lax.dynamic_slice_in_dim(gg, s0, Q_BLOCK, 0)
        t = s0 + jnp.arange(Q_BLOCK)

        sc = jnp.einsum('qghd,cgd->gqhc', qi, k_cmp).astype(jnp.float32) * scale
        valid = cmp_end[None, :] <= t[:, None]
        p_c = jax.nn.softmax(jnp.where(valid[None, :, None, :], sc, NEG), axis=-1)
        p_c = p_c * jnp.any(valid, axis=-1)[None, :, None, None].astype(jnp.float32)
        o_c = jnp.einsum('gqhc,cgd->qghd', p_c.astype(dt), v_cmp)

        imp = jnp.einsum('gqhc,cj->gqj', p_c, overlap)
        cur = t // SLC_BLOCK
        forced = (blk_j[None] == 0) | (blk_j[None] == cur[:, None]) | (blk_j[None] == cur[:, None] - 1)
        future = blk_j[None] > cur[:, None]
        imp = jnp.where(forced[None], BIG, jnp.where(future[None], NEG, imp))
        _, sel = lax.top_k(imp, n_sel)

        k_sel = ks_b[g_idx, sel].reshape(G, Q_BLOCK, n_sel * SLC_BLOCK, dh)
        v_sel = vs_b[g_idx, sel].reshape(G, Q_BLOCK, n_sel * SLC_BLOCK, dh)
        k_pos = (sel[..., None] * SLC_BLOCK + jnp.arange(SLC_BLOCK)).reshape(G, Q_BLOCK, n_sel * SLC_BLOCK)
        ss = jnp.einsum('qghd,gqkd->gqhk', qi, k_sel).astype(jnp.float32) * scale
        smask = (k_pos <= t[None, :, None])[:, :, None, :]
        p_s = jax.nn.softmax(jnp.where(smask, ss, NEG), axis=-1)
        o_s = jnp.einsum('gqhk,gqkd->qghd', p_s.astype(dt), v_sel)

        k_win = lax.dynamic_slice_in_dim(kw_pad, s0, WINDOW + Q_BLOCK, 0)
        v_win = lax.dynamic_slice_in_dim(vw_pad, s0, WINDOW + Q_BLOCK, 0)
        w_pos = s0 - WINDOW + jnp.arange(WINDOW + Q_BLOCK)
        wmask = (w_pos[None] <= t[:, None]) & (w_pos[None] > t[:, None] - WINDOW) & (w_pos[None] >= 0)
        sw = jnp.einsum('qghd,kgd->gqhk', qi, k_win).astype(jnp.float32) * scale
        p_w = jax.nn.softmax(jnp.where(wmask[None, :, None, :], sw, NEG), axis=-1)
        o_w = jnp.einsum('gqhk,kgd->qghd', p_w.astype(dt), v_win)

        o = gi[..., 0:1] * o_c + gi[..., 1:2] * o_s + gi[..., 2:3] * o_w
        return o.reshape(Q_BLOCK, NSA_HEADS * dh).astype(dt)

    out = lax.map(block, jnp.arange(n_qb))
    return out.reshape(S, NSA_HEADS * dh)

def retention(q, k, v, pos):
    B, S = q.shape[0], q.shape[1]
    H, d, C = RET_HEADS, RET_HEAD_DIM, RET_CHUNK
    q = rotary(q, pos, d, RET_ROT_BASE).astype(jnp.float32)
    k = rotary(k, pos, d, RET_ROT_BASE).astype(jnp.float32) * (d ** -0.5)
    v = v.astype(jnp.float32)
    n_c = S // C

    def chunks(a):
        return a.reshape(B, n_c, C, H, d).transpose(1, 0, 3, 2, 4)

    log_g = jnp.log(1.0 - jnp.exp2(-5.0 - jnp.arange(H, dtype=jnp.float32)))
    n = jnp.arange(C, dtype=jnp.float32)
    rel = n[:, None] - n[None, :]
    dmat = jnp.where(rel >= 0, jnp.exp(log_g[:, None, None] * jnp.maximum(rel, 0.0)), 0.0)
    xi = jnp.exp(log_g[:, None] * (n + 1.0))
    zeta = jnp.exp(log_g[:, None] * (C - 1.0 - n))
    chunk_decay = jnp.exp(log_g * C)

    def step(state, inp):
        qc, kc, vc = inp
        inner = jnp.einsum('bhnm,bhme->bhne', jnp.einsum('bhnd,bhmd->bhnm', qc, kc) * dmat, vc)
        cross = jnp.einsum('bhnd,bhde->bhne', qc, state) * xi[None, :, :, None]
        state = chunk_decay[None, :, None, None] * state + jnp.einsum(
            'bhmd,bhme->bhde', kc * zeta[None, :, :, None], vc)
        return state, inner + cross

    state0 = jnp.zeros((B, H, d, d), jnp.float32)
    _, o = lax.scan(step, state0, (chunks(q), chunks(k), chunks(v)))
    o = o.transpose(1, 0, 3, 2, 4).reshape(B, S, H, d)
    return o * lax.rsqrt(jnp.mean(o * o, axis=-1, keepdims=True) + NORM_EPS)

def first_inputs(seed: int = 0) -> dict:
    key = jax.random.key(seed)
    ks = jax.random.split(key, 20)
    f32 = jnp.float32
    nrm = lambda k, shape, s: jax.random.normal(k, shape, f32) * s
    L = DEPTH
    x = jax.random.normal(ks[0], (BATCH, SEQ, D_MODEL), f32)
    offset = jax.random.randint(ks[1], (BATCH, 1), 0, 4096, dtype=jnp.int32)
    positions = (offset + jnp.arange(SEQ, dtype=jnp.int32)[None, :]).astype(jnp.int32)
    return {
        "x": x,
        "positions": positions,
        "norm_mix": 1.0 + nrm(ks[2], (L, D_MODEL), 0.02),
        "w_in": nrm(ks[3], (L, D_MODEL, IN_WIDTH), D_MODEL ** -0.5),
        "cmp_pos_k": nrm(ks[4], (L, CMP_BLOCK, NSA_HEAD_DIM), 0.1),
        "cmp_pos_v": nrm(ks[5], (L, CMP_BLOCK, NSA_HEAD_DIM), 0.1),
        "cmp_k_w1": nrm(ks[6], (L, CMP_BLOCK * NSA_HEAD_DIM, CMP_HIDDEN), (CMP_BLOCK * NSA_HEAD_DIM) ** -0.5),
        "cmp_k_w2": nrm(ks[7], (L, CMP_HIDDEN, NSA_HEAD_DIM), CMP_HIDDEN ** -0.5),
        "cmp_v_w1": nrm(ks[8], (L, CMP_BLOCK * NSA_HEAD_DIM, CMP_HIDDEN), (CMP_BLOCK * NSA_HEAD_DIM) ** -0.5),
        "cmp_v_w2": nrm(ks[9], (L, CMP_HIDDEN, NSA_HEAD_DIM), CMP_HIDDEN ** -0.5),
        "w_proj_a": nrm(ks[10], (L, NSA_Q_W, D_MODEL), NSA_Q_W ** -0.5),
        "w_proj_b": nrm(ks[11], (L, RET_W, D_MODEL), RET_W ** -0.5),
        "w_out": nrm(ks[12], (L, D_MODEL, D_MODEL), D_MODEL ** -0.5),
        "norm_mlp": 1.0 + nrm(ks[13], (L, D_MODEL), 0.02),
        "w_up": nrm(ks[14], (L, D_MODEL, MLP_HIDDEN), D_MODEL ** -0.5),
        "w_down": nrm(ks[15], (L, MLP_HIDDEN, D_MODEL), MLP_HIDDEN ** -0.5),
        "norm_final": 1.0 + nrm(ks[16], (D_MODEL,), 0.02),
    }

def first_block(x, positions, norm_mix, w_in, cmp_pos_k, cmp_pos_v, cmp_k_w1, cmp_k_w2, cmp_v_w1, cmp_v_w2,
              w_proj_a, w_proj_b, w_out, norm_mlp, w_up, w_down, norm_final):
    B, S, _ = x.shape
    offsets = np.cumsum(IN_SIZES)[:-1].tolist()
    nsa_batched = jax.vmap(nsa_mixer, in_axes=(0,) * 8 + (None,) * 6)
    for layer in range(DEPTH):
        h = rmsnorm(x, norm_mix[layer])
        (q, kc, vc, ks, vs, kw, vw, nsa_g, rq, rk, rv, rg, gate_a, gate_b) = jnp.split(
            h @ w_in[layer], offsets, axis=-1)
        heads = lambda a, n_h, d: a.reshape(B, S, n_h, d)
        q = rotary(heads(q, NSA_HEADS, NSA_HEAD_DIM), positions, ROPE_DIM, ROPE_THETA)
        kc = rotary(heads(kc, NSA_KV_GROUPS, NSA_HEAD_DIM), positions, ROPE_DIM, ROPE_THETA)
        ks = rotary(heads(ks, NSA_KV_GROUPS, NSA_HEAD_DIM), positions, ROPE_DIM, ROPE_THETA)
        kw = rotary(heads(kw, NSA_KV_GROUPS, NSA_HEAD_DIM), positions, ROPE_DIM, ROPE_THETA)
        vc = heads(vc, NSA_KV_GROUPS, NSA_HEAD_DIM)
        vs = heads(vs, NSA_KV_GROUPS, NSA_HEAD_DIM)
        vw = heads(vw, NSA_KV_GROUPS, NSA_HEAD_DIM)
        nsa_out = nsa_batched(q, kc, vc, ks, vs, kw, vw, nsa_g.reshape(B, S, NSA_HEADS, 3),
                              cmp_pos_k[layer], cmp_pos_v[layer], cmp_k_w1[layer], cmp_k_w2[layer],
                              cmp_v_w1[layer], cmp_v_w2[layer])
        ret = retention(heads(rq, RET_HEADS, RET_HEAD_DIM), heads(rk, RET_HEADS, RET_HEAD_DIM),
                        heads(rv, RET_HEADS, RET_HEAD_DIM), positions)
        ret_out = (jax.nn.silu(rg.astype(jnp.float32)) * ret.reshape(B, S, RET_W)).astype(x.dtype)
        mix = (jax.nn.sigmoid(gate_a) * (nsa_out @ w_proj_a[layer])
               + jax.nn.sigmoid(gate_b) * (ret_out @ w_proj_b[layer]))
        x = x + mix @ w_out[layer]
        h = rmsnorm(x, norm_mlp[layer])
        x = x + jnp.square(jax.nn.relu(h @ w_up[layer])) @ w_down[layer]
    return rmsnorm(x, norm_final)


MEM_LEN = 256
EPS = 1e-6
CHUNK = 64

SSD_D_INNER = D_MODEL
SSD_HEAD_DIM = 64
SSD_HEADS = SSD_D_INNER // SSD_HEAD_DIM
SSD_GROUPS = 2
SSD_STATE = 128
SSD_CONV = 4
SSD_CONV_CH = SSD_D_INNER + 2 * SSD_GROUPS * SSD_STATE
DT_MIN = 1e-3
DT_MAX = 1e-1

GLA_HEADS = 4
GLA_DK = D_MODEL // 2
GLA_DV = D_MODEL
GLA_HEAD_K = GLA_DK // GLA_HEADS
GLA_HEAD_V = GLA_DV // GLA_HEADS
GLA_GATE_RANK = 16
GLA_TAU = 16.0

XATTN_HEADS = 4
XATTN_HEAD_DIM = D_MODEL // XATTN_HEADS

D_FF = -((-8 * D_MODEL) // (3 * 256)) * 256

IN_SIZES_2 = (SSD_D_INNER, SSD_CONV_CH, SSD_HEADS,
            GLA_DK, GLA_DK, GLA_DV, GLA_DV, GLA_GATE_RANK,
            D_MODEL, D_MODEL)
IN_WIDTH_2 = sum(IN_SIZES_2)


def rmsnorm_2(x, g):
    xf = x.astype(jnp.float32)
    y = xf * lax.rsqrt(jnp.mean(xf * xf, axis=-1, keepdims=True) + EPS)
    return (y * g.astype(jnp.float32)).astype(x.dtype)

def causal_dwconv(x, w, b):
    y = lax.conv_general_dilated(x, w, window_strides=(1,), padding=[(SSD_CONV - 1, 0)],
                                 dimension_numbers=('NWC', 'WIO', 'NWC'),
                                 feature_group_count=x.shape[-1])
    return y + b

def segsum_exp(a):
    L = a.shape[-1]
    cs = jnp.cumsum(a, axis=-1)
    mask = jnp.tril(jnp.ones((L, L), dtype=bool))
    diff = cs[..., :, None] - cs[..., None, :]
    return jnp.where(mask, jnp.exp(jnp.where(mask, diff, 0.0)), 0.0)

def ssd_mixer(z, xBC, dt_raw, conv_w, conv_b, dt_bias, A_log, D_skip, norm_g):
    Bsz, S, _ = z.shape
    nc = S // CHUNK
    G, R, P, N = SSD_GROUPS, SSD_HEADS // SSD_GROUPS, SSD_HEAD_DIM, SSD_STATE
    xBC = jax.nn.silu(causal_dwconv(xBC, conv_w, conv_b)).astype(jnp.float32)
    xs, Bm, Cm = jnp.split(xBC, [SSD_D_INNER, SSD_D_INNER + G * N], axis=-1)
    dt = jax.nn.softplus(dt_raw.astype(jnp.float32) + dt_bias.astype(jnp.float32))
    A = -jnp.exp(A_log.astype(jnp.float32))
    x_heads = xs.reshape(Bsz, S, SSD_HEADS, P)
    X = (x_heads * dt[..., None]).reshape(Bsz, nc, CHUNK, G, R, P)
    a = (dt * A).reshape(Bsz, nc, CHUNK, G, R).transpose(0, 3, 4, 1, 2)
    Bc = Bm.reshape(Bsz, nc, CHUNK, G, N)
    Cc = Cm.reshape(Bsz, nc, CHUNK, G, N)
    a_cs = jnp.cumsum(a, axis=-1)
    Lmat = segsum_exp(a)
    CB = jnp.einsum('bclgn,bcsgn->bcgls', Cc, Bc)
    y_diag = jnp.einsum('bcgls,bgrcls,bcsgrp->bclgrp', CB, Lmat, X)
    decay_states = jnp.exp(a_cs[..., -1:] - a_cs)
    states = jnp.einsum('bclgn,bgrcl,bclgrp->bcgrpn', Bc, decay_states, X)
    chunk_decay = jnp.exp(a_cs[..., -1])

    def chunk_step(state, inp):
        st_c, dec_c = inp
        return state * dec_c[..., None, None] + st_c, state

    init = jnp.zeros((Bsz, G, R, P, N), jnp.float32)
    _, prev = lax.scan(chunk_step, init, (jnp.moveaxis(states, 1, 0), jnp.moveaxis(chunk_decay, 3, 0)))
    prev = jnp.moveaxis(prev, 0, 1)
    y_off = jnp.einsum('bclgn,bcgrpn,bgrcl->bclgrp', Cc, prev, jnp.exp(a_cs))
    y = (y_diag + y_off).reshape(Bsz, S, SSD_HEADS, P) + D_skip.astype(jnp.float32)[:, None] * x_heads
    y = y.reshape(Bsz, S, SSD_D_INNER) * jax.nn.silu(z.astype(jnp.float32))
    y = rmsnorm_2(y.reshape(Bsz, S, G, SSD_D_INNER // G), norm_g.reshape(G, SSD_D_INNER // G))
    return y.reshape(Bsz, S, SSD_D_INNER).astype(z.dtype)

def gla_mixer(q, k, v, r, a1, w_a2, b_a, norm_g):
    Bsz, S, _ = q.shape
    nc = S // CHUNK
    H, dk, dv = GLA_HEADS, GLA_HEAD_K, GLA_HEAD_V
    log_alpha = jax.nn.log_sigmoid((a1 @ w_a2 + b_a).astype(jnp.float32)) / GLA_TAU
    qc = q.astype(jnp.float32).reshape(Bsz, nc, CHUNK, H, dk) * (dk ** -0.5)
    kc = k.astype(jnp.float32).reshape(Bsz, nc, CHUNK, H, dk)
    vc = v.astype(jnp.float32).reshape(Bsz, nc, CHUNK, H, dv)
    bcum = jnp.cumsum(log_alpha.reshape(Bsz, nc, CHUNK, H, dk), axis=2)
    b_last = bcum[:, :, -1:]
    q_t = qc * jnp.exp(bcum)
    k_t = kc * jnp.exp(-bcum)
    k_h = kc * jnp.exp(b_last - bcum)
    mask = jnp.tril(jnp.ones((CHUNK, CHUNK), dtype=bool))
    att = jnp.where(mask, jnp.einsum('bclhd,bcshd->bchls', q_t, k_t), 0.0)
    o_intra = jnp.einsum('bchls,bcshv->bclhv', att, vc)
    U = jnp.einsum('bclhd,bclhv->bchdv', k_h, vc)
    dec = jnp.exp(b_last[:, :, 0])

    def chunk_step(state, inp):
        u_c, d_c = inp
        return state * d_c[..., None] + u_c, state

    init = jnp.zeros((Bsz, H, dk, dv), jnp.float32)
    _, prev = lax.scan(chunk_step, init, (jnp.moveaxis(U, 1, 0), jnp.moveaxis(dec, 1, 0)))
    prev = jnp.moveaxis(prev, 0, 1)
    o_inter = jnp.einsum('bclhd,bchdv->bclhv', q_t, prev)
    o = (o_intra + o_inter).reshape(Bsz, S, H, dv)
    o = rmsnorm_2(o, norm_g).reshape(Bsz, S, GLA_DV)
    return (o * jax.nn.silu(r.astype(jnp.float32))).astype(q.dtype)

def hybrid_mixer(n, w_in, conv_w, conv_b, dt_bias, A_log, D_skip, ssd_norm,
                 gla_w_a2, gla_b_a, gla_norm, w_up_ssd, w_up_gla, w_o):
    proj = n @ w_in
    idx = np.cumsum(IN_SIZES_2)[:-1].tolist()
    z, xBC, dt_raw, q, k, v, r, a1, g_ssd, g_gla = jnp.split(proj, idx, axis=-1)
    y_ssd = ssd_mixer(z, xBC, dt_raw, conv_w, conv_b, dt_bias, A_log, D_skip, ssd_norm)
    y_gla = gla_mixer(q, k, v, r, a1, gla_w_a2, gla_b_a, gla_norm)
    merged = jax.nn.sigmoid(g_ssd) * (y_ssd @ w_up_ssd) + jax.nn.sigmoid(g_gla) * (y_gla @ w_up_gla)
    return merged @ w_o

def mem_cross_attention(n, m, w_xq, w_xkv, w_xo):
    Bsz, S, _ = n.shape
    q = (n @ w_xq).reshape(Bsz, S, XATTN_HEADS, XATTN_HEAD_DIM)
    k, v = jnp.split(m @ w_xkv, 2, axis=-1)
    k = k.reshape(Bsz, -1, XATTN_HEADS, XATTN_HEAD_DIM)
    v = v.reshape(Bsz, -1, XATTN_HEADS, XATTN_HEAD_DIM)
    s = jnp.einsum('bshd,bmhd->bhsm', q, k).astype(jnp.float32) * (XATTN_HEAD_DIM ** -0.5)
    p = jax.nn.softmax(s, axis=-1).astype(v.dtype)
    o = jnp.einsum('bhsm,bmhd->bshd', p, v).reshape(Bsz, S, D_MODEL)
    return o @ w_xo

def swiglu(n, w_ffn_in, w_ffn_out):
    g, u = jnp.split(n @ w_ffn_in, 2, axis=-1)
    return (jax.nn.silu(g) * u) @ w_ffn_out

def second_inputs(seed: int = 0) -> dict:
    key = jax.random.key(seed)
    ks = jax.random.split(key, 26)
    f32 = jnp.float32
    L = DEPTH

    def nrm(k, shape, scale):
        return jax.random.normal(k, shape, f32) * scale

    def gain(k, shape):
        return 1.0 + 0.02 * jax.random.normal(k, shape, f32)

    dt = jnp.exp(jax.random.uniform(ks[6], (L, SSD_HEADS), f32, math.log(DT_MIN), math.log(DT_MAX)))
    dt_bias = dt + jnp.log(-jnp.expm1(-dt))
    A_log = jnp.log(jax.random.uniform(ks[7], (L, SSD_HEADS), f32, 1.0, 16.0))
    return {
        "x": jax.random.normal(ks[0], (BATCH, SEQ, D_MODEL), f32),
        "mem": jax.random.normal(ks[1], (BATCH, MEM_LEN, D_MODEL), f32),
        "norm_mix": gain(ks[2], (L, D_MODEL)),
        "w_in": nrm(ks[3], (L, D_MODEL, IN_WIDTH_2), D_MODEL ** -0.5),
        "ssd_conv_w": nrm(ks[4], (L, SSD_CONV, 1, SSD_CONV_CH), SSD_CONV ** -0.5),
        "ssd_conv_b": nrm(ks[5], (L, SSD_CONV_CH), 0.02),
        "ssd_dt_bias": dt_bias,
        "ssd_A_log": A_log,
        "ssd_D": 1.0 + 0.1 * jax.random.normal(ks[8], (L, SSD_HEADS), f32),
        "ssd_norm": gain(ks[9], (L, SSD_D_INNER)),
        "gla_w_a2": nrm(ks[10], (L, GLA_GATE_RANK, GLA_DK), GLA_GATE_RANK ** -0.5),
        "gla_b_a": nrm(ks[11], (L, GLA_DK), 0.02),
        "gla_norm": gain(ks[12], (L, GLA_HEAD_V)),
        "w_up_ssd": nrm(ks[13], (L, SSD_D_INNER, D_MODEL), SSD_D_INNER ** -0.5),
        "w_up_gla": nrm(ks[14], (L, GLA_DV, D_MODEL), GLA_DV ** -0.5),
        "w_o": nrm(ks[15], (L, D_MODEL, D_MODEL), D_MODEL ** -0.5),
        "norm_xattn": gain(ks[16], (L, D_MODEL)),
        "norm_mem": gain(ks[17], (L, D_MODEL)),
        "w_xq": nrm(ks[18], (L, D_MODEL, D_MODEL), D_MODEL ** -0.5),
        "w_xkv": nrm(ks[19], (L, D_MODEL, 2 * D_MODEL), D_MODEL ** -0.5),
        "w_xo": nrm(ks[20], (L, D_MODEL, D_MODEL), D_MODEL ** -0.5),
        "norm_ffn": gain(ks[21], (L, D_MODEL)),
        "w_ffn_in": nrm(ks[22], (L, D_MODEL, 2 * D_FF), D_MODEL ** -0.5),
        "w_ffn_out": nrm(ks[23], (L, D_FF, D_MODEL), D_FF ** -0.5),
        "norm_final": gain(ks[24], (D_MODEL,)),
    }

def second_block(x, mem, norm_mix, w_in, ssd_conv_w, ssd_conv_b, ssd_dt_bias, ssd_A_log, ssd_D, ssd_norm,
              gla_w_a2, gla_b_a, gla_norm, w_up_ssd, w_up_gla, w_o, norm_xattn, norm_mem, w_xq, w_xkv,
              w_xo, norm_ffn, w_ffn_in, w_ffn_out, norm_final):
    h = x
    for i in range(DEPTH):
        h = h + hybrid_mixer(rmsnorm_2(h, norm_mix[i]), w_in[i], ssd_conv_w[i], ssd_conv_b[i], ssd_dt_bias[i],
                             ssd_A_log[i], ssd_D[i], ssd_norm[i], gla_w_a2[i], gla_b_a[i], gla_norm[i],
                             w_up_ssd[i], w_up_gla[i], w_o[i])
        h = h + mem_cross_attention(rmsnorm_2(h, norm_xattn[i]), rmsnorm_2(mem, norm_mem[i]),
                                    w_xq[i], w_xkv[i], w_xo[i])
        h = h + swiglu(rmsnorm_2(h, norm_ffn[i]), w_ffn_in[i], w_ffn_out[i])
    return rmsnorm_2(h, norm_final)


def setup_inputs(seed=0):
    out = dict(first_inputs(seed))
    for name, value in second_inputs(seed + 1).items():
        if name != "x":
            out[name + "_2"] = value
    return out


def reference(
    x, positions, norm_mix, w_in, cmp_pos_k, cmp_pos_v, cmp_k_w1, cmp_k_w2, cmp_v_w1, cmp_v_w2,
    w_proj_a, w_proj_b, w_out, norm_mlp, w_up, w_down, norm_final, mem_2, norm_mix_2, w_in_2,
    ssd_conv_w_2, ssd_conv_b_2, ssd_dt_bias_2, ssd_A_log_2, ssd_D_2, ssd_norm_2, gla_w_a2_2,
    gla_b_a_2, gla_norm_2, w_up_ssd_2, w_up_gla_2, w_o_2, norm_xattn_2, norm_mem_2, w_xq_2,
    w_xkv_2, w_xo_2, norm_ffn_2, w_ffn_in_2, w_ffn_out_2, norm_final_2,
):
    x = first_block(
        x, positions, norm_mix, w_in, cmp_pos_k, cmp_pos_v, cmp_k_w1, cmp_k_w2, cmp_v_w1,
        cmp_v_w2, w_proj_a, w_proj_b, w_out, norm_mlp, w_up, w_down, norm_final,
    )
    return second_block(
        x, mem_2, norm_mix_2, w_in_2, ssd_conv_w_2, ssd_conv_b_2, ssd_dt_bias_2, ssd_A_log_2,
        ssd_D_2, ssd_norm_2, gla_w_a2_2, gla_b_a_2, gla_norm_2, w_up_ssd_2, w_up_gla_2, w_o_2,
        norm_xattn_2, norm_mem_2, w_xq_2, w_xkv_2, w_xo_2, norm_ffn_2, w_ffn_in_2, w_ffn_out_2,
        norm_final_2,
    )


_drawn_inputs = setup_inputs


def setup_inputs(seed=0):
    import zlib

    import numpy as np

    out = dict(_drawn_inputs(seed))
    spreads = {}
    factors = {'norm_mix': 2.808,
     'cmp_pos_k': 8.0,
     'cmp_pos_v': 2.811,
     'norm_mix_2': 2.838,
     'ssd_conv_b_2': 4.543,
     'ssd_norm_2': 5.445,
     'gla_b_a_2': 8.0,
     'gla_norm_2': 8.0,
     'norm_xattn_2': 8.0,
     'norm_mem_2': 8.0,
     'norm_ffn_2': 12.1,
     'norm_final_2': 8.011,
     'ssd_D_2': 8.0}
    for name, (base, spread) in spreads.items():
        noise = np.random.default_rng([zlib.crc32(name.encode()), seed]).standard_normal(out[name].shape)
        drawn = base * np.exp(spread * noise) if base else spread * noise
        out[name] = __import__('jax').numpy.asarray(drawn.astype(out[name].dtype))
    for name, factor in factors.items():
        out[name] = (out[name] * factor).astype(out[name].dtype)
    return out
```

```python
import math
from contextlib import ExitStack

import numpy as np

import concourse.bass as bass
import concourse.mybir as mybir

F32 = mybir.dt.float32
I32 = mybir.dt.int32
ALU = mybir.AluOpType
ACT = mybir.ActivationFunctionType
AX = mybir.AxisListType
P = 128
D = 1024
EPS = 1e-6
NEG = -1e30
SLOTS = 8
SLOT = 2048

CONSTS = dict(ident=128, upper=128, after=128, causal=128, cmask=30, crow=2, decay=1024, inv=72, keep=256)
COLS = dict(norm_mix=8, norm_mlp=8, norm_mix_2=8, ssd_norm_2=8, gla_norm_2=2, norm_xattn_2=8, norm_mem_2=8,
            norm_ffn_2=8, conv_w=48, conv_b=12, gla_b=4, pe_k=16, pe_v=16)
ROWS = dict(norm_final=1024, norm_final_2=1024, ssd_dt_bias_2=16, ssd_A_log_2=16, ssd_D_2=16)


def offsets(sizes):
    at, out = 0, {}
    for name, n in sizes.items():
        out[name] = (at, n)
        at += n
    return out, at


class Queue:

    def __init__(self, sem, serial=False):
        self.sem, self.n, self.todo, self.seen, self.serial = sem, 0, [], {}, serial

    def wait(self, *tokens):
        for t in tokens:
            if t is None:
                continue
            if isinstance(t, list):
                self.wait(*t)
                continue
            sem, n = t
            if self.seen.get(id(sem), 0) < n:
                self.seen[id(sem)] = n
                self.todo.append(lambda e, sem=sem, n=n: e.wait_ge(sem, n))

    def do(self, fn, *waits):
        self.wait(*waits)
        if self.serial and self.n:
            self.wait((self.sem, self.n))
        self.n += 1
        self.todo.append(lambda e: fn(e).then_inc(self.sem, 1))
        return (self.sem, self.n)

    def part(self, fn, *waits):
        self.wait(*waits)
        self.todo.append(fn)

    def dma(self, sem, at, out, in_, *waits):
        self.wait(*waits)
        self.todo.append(lambda e: e.dma_start(out, in_).then_inc(sem, 16))
        return (sem, at)


def build(nc, a, out):
    ctx = ExitStack()
    with ctx:
        def sb(name, shape, dt=F32):
            return ctx.enter_context(nc.sbuf_tensor(name, shape, dt))

        def sem(name):
            return ctx.enter_context(nc.semaphore(name))

        pe, sp = Queue(sem("s_pe")), Queue(sem("s_sp"))
        act, dve, pool = (Queue(sem(f"s_{n}"), serial=True) for n in ("act", "dve", "pool"))

        ring = sb("ring", [P, SLOTS, SLOT])
        psum = ctx.enter_context(nc.psum_tensor("ps", [P, 8, 512], F32))
        co, ncol = offsets(CONSTS)
        consts = sb("consts", [P, ncol])
        cc, ncc = offsets(COLS)
        cols = sb("cols", [P, ncc])
        rr, nrr = offsets(ROWS)
        rows = sb("rows", [P, nrr])
        posi = sb("posi", [P, 2], I32)

        def const(name):
            at, n = co[name]
            return consts[:, at:at + n]

        def col(name):
            at, n = cc[name]
            return cols[:, at:at + n]

        def row(name):
            at, n = rr[name]
            return rows[:, at:at + n]

        s_in = {n: sem(f"s_in_{n}") for n in ("x", "consts", "cols", "rows", "pos", "w2k", "w2v", "wa2", "mem")}
        x = sb("x", [P, 2, D])
        big = sb("big", [P, 2, D])
        xT = sb("xT", [P, 8, 256])
        w2k = sb("w2k", [P, 2, 2, 64])
        w2v = sb("w2v", [P, 2, 64])
        wa2 = sb("wa2", [16, 512])
        AW = 23400
        arena = sb("arena", [P, AW])

        in_x = act.dma(s_in["x"], 16, x[:, :, :], a["x"].rearrange("b (t p) d -> p (b t) d", p=P))
        in_consts = act.dma(s_in["consts"], 16, consts[:, :], a["consts"])
        in_cols = act.dma(s_in["cols"], 16, cols[:, :], a["cols"])
        in_pos = act.dma(s_in["pos"], 16, posi[:, :], a["pos"])
        for h in range(2):
            in_w2k = pool.dma(s_in["w2k"], 16 * (h + 1), w2k[:, :, h, :],
                              a["cmp_k_w2"][0].rearrange("(c p) n -> p c n", p=P))
        in_w2v = pool.dma(s_in["w2v"], 16, w2v[:, :, :], a["cmp_v_w2"][0].rearrange("(c p) n -> p c n", p=P))
        in_wa2 = pool.dma(s_in["wa2"], 16, wa2[:, :], a["gla_w_a2_2"][0])
        n = 0
        for name in ROWS:
            n += 16
            src = a[name] if name == "norm_final" or name == "norm_final_2" else a[name][0]
            in_rows = pool.dma(s_in["rows"], n, row(name), src.partition_broadcast(P))

        class Space:

            def __init__(self):
                self.at = self.top = 0

            def take(self, n):
                self.at += n
                assert self.at <= AW, self.at
                return arena[:, self.at - n:self.at]

        space = Space()

        bank_free = [(b, None) for b in range(8)]

        def bank():
            return bank_free.pop(0)

        def give(b, token):
            bank_free.append((b, token))

        s_w = [sem(f"s_w{i}") for i in range(SLOTS)]
        loads = [0]
        slot_free = [None] * SLOTS

        def weight(src, k, n):
            i = loads[0] % SLOTS
            loads[0] += 1
            view = ring[:, i, 0:k * n].rearrange("p (k n) -> p k n", k=k)
            token = sp.dma(s_w[i], 16 * ((loads[0] - 1) // SLOTS + 1), view,
                           src.rearrange("(k p) n -> p k n", p=P), slot_free[i])
            return view, i, token

        def used(slot, token):
            slot_free[slot] = token

        def mm(ps, lhsT, rhs, start, stop):
            return lambda e: e.matmul(ps, lhsT, rhs, start=start, stop=stop)

        def group(ps, pairs, *waits, more=None):
            pe.wait(*waits)
            for i, (l, r) in enumerate(pairs):
                if more and more[i]:
                    pe.wait(more[i])
                f = mm(ps, l, r, i == 0, i == len(pairs) - 1)
                if i == len(pairs) - 1:
                    return pe.do(f)
                pe.part(f)

        def fm(w, c0, cn, hT, ready, evac):
            K = w.shape[0] // P
            for b0 in range(0, cn, 512):
                nb = min(512, cn - b0)
                tiles = [weight(w[k0 * P:(k0 + 4) * P, c0 + b0:c0 + b0 + nb], 4, nb) for k0 in range(0, K, 4)]
                for q0 in range(0, nb, 256):
                    b, free = bank()
                    width = min(256, nb - q0)
                    for s in range(0, width, P):
                        m = min(P, width - s)
                        ps = psum[0:m, b, 2 * s:2 * s + 256]
                        pairs = [(tiles[k // 4][0][:, k % 4, q0 + s:q0 + s + m], hT[:, k, :]) for k in range(K)]
                        t = group(ps, pairs, ready, free, more=[tiles[k // 4][2] for k in range(K)])
                    if q0 + 256 >= nb:
                        for _, i, _ in tiles:
                            used(i, t)
                    m = min(P, width)
                    v = psum[0:m, b, 0:512].rearrange("p (s n) -> p s n", s=2)
                    give(b, evac((b0 + q0) // 256, v[:, 0:(width + P - 1) // P, :], t))
                    yield

        def tm(w, c0, cn, hT, ready, evac):
            K = w.shape[0] // P
            for b0 in range(0, cn, 512):
                nb = min(512, cn - b0)
                tiles = [weight(w[k0 * P:(k0 + 4) * P, c0 + b0:c0 + b0 + nb], 4, nb) for k0 in range(0, K, 4)]
                for t in range(2):
                    b, free = bank()
                    ps = psum[:, b, 0:nb]
                    pairs = [(hT[:, k, t * P:t * P + P], tiles[k // 4][0][:, k % 4, :]) for k in range(K)]
                    tok = group(ps, pairs, ready, free, more=[tiles[k // 4][2] for k in range(K)])
                    if t == 1:
                        for _, i, _ in tiles:
                            used(i, tok)
                    give(b, evac(b0 // 512, t, ps, tok))
                    yield

        def run(*gens):
            for g in gens:
                for _ in g:
                    pass

        def down(w, hT, ready, evac):
            K = w.shape[0] // P
            banks = [bank() for _ in range(4)]
            for _, free in banks:
                pe.wait(free)
            for k0 in range(0, K, 2):
                view, i, tok = weight(w[k0 * P:(k0 + 2) * P, :], 2, D)
                pe.wait(tok, ready(k0 + 1))
                for k in range(k0, k0 + 2):
                    for t in range(2):
                        for h in range(2):
                            f = mm(psum[:, banks[2 * t + h][0], :], hT[:, k, t * P:t * P + P],
                                   view[:, k - k0, h * 512:h * 512 + 512], k == 0, k == K - 1)
                            if k == k0 + 1 and (t, h) == (1, 1):
                                last = pe.do(f)
                            else:
                                pe.part(f)
                used(i, last)
            for t in range(2):
                for h in range(2):
                    b = banks[2 * t + h][0]
                    give(b, evac(h, t, psum[:, b, :], last))

        ident = const("ident")

        def transposes(ps, ins, *waits):
            pe.wait(*waits)
            for i, v in enumerate(ins):
                n = v.shape[0]
                m = 1
                for s in v.shape[1:]:
                    m *= s
                f = (lambda e, i=i, v=v, n=n, m=m: e.transpose(ps[0:m, i * n:(i + 1) * n], v, ident[0:n, 0:n]))
                if i == len(ins) - 1:
                    return pe.do(f)
                pe.part(f)

        def copy_act(o, i, *waits):
            return act.do(lambda e: e.activation(o, i, ACT.Copy), *waits)

        def copy_dve(o, i, *waits):
            return dve.do(lambda e: e.tensor_copy(o, i), *waits)

        def tt(q, o, a0, a1, op, *waits):
            return q.do(lambda e: e.tensor_tensor(o, a0, a1, op), *waits)

        def ts(q, o, i, s1, s2, op0, op1, *waits):
            if op1 is None:
                return q.do(lambda e: e.tensor_scalar(o, i, s1, None, op0), *waits)
            return q.do(lambda e: e.tensor_scalar(o, i, s1, s2, op0, op1), *waits)

        def stt(o, i, s, i1, op0, op1, *waits):
            return dve.do(lambda e: e.scalar_tensor_tensor(out=o, in0=i, scalar=s, in1=i1, op0=op0, op1=op1), *waits)

        def fn(o, i, f, *waits, **kw):
            return act.do(lambda e: e.activation(o, i, f, **kw), *waits)

        def bc(v, axis, shape):
            return v.unsqueeze(axis).to_broadcast(shape)

        half = sb("half", [P, 16])
        k_half = pool.do(lambda e: e.memset(half[:, :], -0.5))
        ssq = sb("ssq", [P, 256])
        nstat = [0]

        def stat(n):
            nstat[0] += n
            assert nstat[0] <= 256
            return ssq[:, nstat[0] - n:nstat[0]]

        def rsqrt_mean(o, ss, count, *waits):
            n = ss.shape[-1]
            t = pool.do(lambda e: e.tensor_scalar(o, ss, 1.0 / count, EPS, ALU.mult, ALU.add), *waits)
            return pool.do(lambda e: e.tensor_tensor(o, o, half[:, 0:n], ALU.pow), t, k_half)

        junk = sb("junk", [P, D])
        junk_free = [None]

        def sum_sq(o, i, *waits):
            n = i.shape[-1]
            junk_free[0] = fn(junk[:, 0:n], i, ACT.Square, *waits, junk_free[0], accum_out=o)
            return junk_free[0]

        def norm_T(src, ready, gain, dst, xs, xs_free=None, rs=None):
            toks = []
            for t in range(2):
                ss, r = stat(1), stat(1)
                k = sum_sq(ss, src(t), ready[t])
                k = rsqrt_mean(r, ss, D, k)
                k = ts(dve, xs[:, t, :], src(t), r, None, ALU.mult, None, k, ready[t], xs_free)
                for q in range(2):
                    b, free = bank()
                    kt = transposes(psum[:, b, :], [xs[:, t, (4 * q + j) * P:(4 * q + j + 1) * P] for j in range(4)],
                                    k, free, in_consts)
                    kt = tt(dve, dst[:, 4 * q:4 * q + 4, t * P:t * P + P],
                            psum[:, b, :].rearrange("p (j n) -> p j n", j=4),
                            bc(gain[:, 4 * q:4 * q + 4], 2, [P, 4, P]), ALU.mult, kt, in_cols)
                    give(b, kt)
                toks.append(kt)
            return toks[-1]

        h_ready = norm_T(lambda t: x[:, t, :], [in_x, in_x], col("norm_mix"), xT, big)

        ang = space.take(144).rearrange("p (t f) -> p t f", t=2)
        posf = space.take(2)
        C1 = 6.28125
        C2 = float(np.float32(np.round((2 * math.pi - C1) * 2.0 ** 18) / 2.0 ** 18))
        C3 = float(np.float32(2 * math.pi - C1 - C2))
        MAGIC = 1.5 * 2.0 ** 23
        TOP = 3.1415925
        k = copy_dve(posf, posi[:, :], in_pos)
        for t in range(2):
            kang = ts(dve, ang[:, t, :], const("inv"), posf[:, t:t + 1], None, ALU.mult, None, k, in_consts)
        trig = []
        for name, quarter in (("sin", 0.0), ("cos", 0.25)):
            turns, red, tab = (space.take(144).rearrange("p (t f) -> p t f", t=2) for _ in range(3))
            k = ts(dve, turns, ang, 1 / (2 * math.pi), quarter, ALU.mult, ALU.add, kang)
            k = ts(dve, turns, turns, MAGIC, None, ALU.add, None, k)
            k = ts(dve, turns, turns, MAGIC, None, ALU.subtract, None, k)
            k = stt(red, turns, -C1, ang, ALU.mult, ALU.add, k)
            k = stt(red, turns, -C2, red, ALU.mult, ALU.add, k)
            k = stt(red, turns, -C3, red, ALU.mult, ALU.add, k)
            if quarter:
                k = ts(dve, red, red, math.pi / 2, None, ALU.add, None, k)
            k = ts(dve, red, red, TOP, -TOP, ALU.min, ALU.max, k)
            ktrig = fn(tab, red, ACT.Sin, k)
            trig.append(tab)
        sin, cos = trig

        w_in = a["w_in"][0]
        qkv = space.take(2 * 1304).rearrange("p (t n) -> p t n", t=2)

        def to_qkv(c):
            def evac(blk, t, ps, tok):
                n = ps.shape[-1]
                kq[(c, t)] = copy_act(qkv[:, t, c + 512 * blk:c + 512 * blk + n], ps, tok)
                return kq[(c, t)]
            return evac
        kq = {}
        run(tm(w_in, 0, 1304, xT, h_ready, to_qkv(0)))
        k_qkv = kq[(0, 1)]
        tmp_all = space.take(2048)
        tmp = [tmp_all[:, 512 * i:512 * i + 512] for i in range(4)]

        def rotate(o1, o2, i1, i2, c, s, shape, *waits):
            n = int(np.prod(shape[1:]))
            names = " ".join("abc"[:len(shape) - 1])
            v = [z[:, 0:n].rearrange(f"p ({names}) -> p {names}", **dict(zip("abc", shape[1:]))) for z in tmp]
            dve.wait(*waits, ktrig)
            tt(dve, v[0], i1, c, ALU.mult)
            tt(dve, v[1], i2, s, ALU.mult)
            tt(dve, v[2], i1, s, ALU.mult)
            k = tt(dve, v[3], i2, c, ALU.mult)
            tt(dve, o1, v[0], v[1], ALU.subtract, k)
            return tt(dve, o2, v[2], v[3], ALU.add, k)

        heads = qkv[:, :, 0:1280].rearrange("p t (h d) -> p t h d", d=64)
        for t in range(2):
            c, s = cos[:, t, 0:8], sin[:, t, 0:8]
            q1, q2 = heads[:, t, 0:8, 0:8], heads[:, t, 0:8, 8:16]
            k_rot = rotate(q1, q2, q1, q2, bc(c, 1, [P, 8, 8]), bc(s, 1, [P, 8, 8]), [P, 8, 8], k_qkv)
            for h in (8, 12, 16):
                q1, q2 = heads[:, t, h:h + 2, 0:8], heads[:, t, h:h + 2, 8:16]
                k_rot = rotate(q1, q2, q1, q2, bc(c, 1, [P, 2, 8]), bc(s, 1, [P, 2, 8]), [P, 2, 8], k_qkv, k_rot)

        rq, rk, rv, rg = (space.take(1024).rearrange("p (t n) -> p t n", t=2) for _ in range(4))
        kr = {}

        def to_rot(dst, name):
            def evac(blk, t, ps, tok):
                v = ps.rearrange("p (h s d) -> p h s d", h=4, s=2)
                o = dst[:, t, :].rearrange("p (h s d) -> p h s d", h=4, s=2)
                kr[name] = rotate(o[:, :, 0, :], o[:, :, 1, :], v[:, :, 0, :], v[:, :, 1, :],
                                  bc(cos[:, t, 8:72], 1, [P, 4, 64]), bc(sin[:, t, 8:72], 1, [P, 4, 64]),
                                  [P, 4, 64], tok, kr.get(name))
                return kr[name]
            return evac

        def to_copy(dst, name):
            def evac(blk, t, ps, tok):
                kr[name] = copy_act(dst[:, t, :], ps, tok)
                return kr[name]
            return evac

        def to_silu(dst, name):
            def evac(blk, t, ps, tok):
                kr[name] = fn(dst[:, t, :], ps, ACT.Silu, tok)
                return kr[name]
            return evac

        run(tm(w_in, 1304, 512, xT, h_ready, to_rot(rq, "rq")), tm(w_in, 1816, 512, xT, h_ready, to_rot(rk, "rk")),
            tm(w_in, 2328, 512, xT, h_ready, to_copy(rv, "rv")), tm(w_in, 2840, 512, xT, h_ready, to_silu(rg, "rg")))

        sig = space.take(4096).rearrange("p (c n) -> p c n", c=16)
        k_sig = {}

        def to_sigmoid(dst, c0, keep):
            def evac(q, ps, tok):
                n = ps.shape[1]
                keep[c0 + 2 * q] = fn(dst[:, c0 + 2 * q:c0 + 2 * q + n, :], ps, ACT.Sigmoid, tok)
                return keep[c0 + 2 * q]
            return evac
        gsig = space.take(48).rearrange("p (t h b) -> p t h b", t=2, h=8)
        for t in range(2):
            k_gsig = fn(gsig[:, t, :, :], qkv[:, t, 1280:1304].rearrange("p (h b) -> p h b", b=3), ACT.Sigmoid, k_qkv)
        fill = fm(w_in, 3352, 2048, xT, h_ready, to_sigmoid(sig, 0, k_sig))

        def step(n=1):
            for _ in range(n):
                next(fill, None)

        qT = space.take(1024).rearrange("p (c n) -> p c n", c=4)
        kT = space.take(1024).rearrange("p (b g n) -> p b g n", b=2, g=2)
        for t in range(2):
            b, free = bank()
            k = transposes(psum[:, b, :], [heads[:, t, 2 * c:2 * c + 2, :].rearrange("p h d -> p (h d)")
                                           for c in range(4)], k_rot, free)
            k_qT = copy_act(qT[:, :, t * P:t * P + P], psum[:, b, :].rearrange("p (c n) -> p c n", c=4), k)
            give(b, k_qT)

        dup = space.take(256).rearrange("p (g t n) -> p g t n", g=2, t=1)
        dup_free = [None]

        def twice(h, t, *waits):
            o = dup[:, :, 0, :]
            for r in range(2):
                k = copy_dve(o.rearrange("p g (r d) -> p g r d", r=2)[:, :, r, :], heads[:, t, h:h + 2, :],
                             *waits, dup_free[0])
            return o, k

        for br, h in ((0, 12), (1, 16)):
            b, free = bank()
            for t in range(2):
                o, k = twice(h, t, k_rot)
                for g in range(2):
                    f = (lambda e, g=g, t=t, b=b, o=o: e.transpose(
                        psum[:, b, (2 * g + t) * P:(2 * g + t + 1) * P], o[:, g, :], ident))
                    k = pe.do(f, k, free)
                dup_free[0] = k
            k_kT = copy_act(kT[:, br, :, :], psum[:, b, :].rearrange("p (g n) -> p g n", g=2), k)
            give(b, k_kT)

        win = space.take(1472)

        def windows(h, pe_col, ready):
            A = win[:, 0:256] if h == 8 else win[:, 736:992]
            B = (win[:, 256:736] if h == 8 else win[:, 992:1472]).rearrange("p (j c) -> p j c", j=16)
            b, free = bank()
            for t in range(2):
                o, k = twice(h, t, ready)
                for g in range(2):
                    f = (lambda e, g=g, t=t, b=b, o=o: e.transpose(
                        psum[:, b, (2 * g + t) * P:(2 * g + t + 1) * P], o[:, g, :], ident))
                    k = pe.do(f, k, free)
                dup_free[0] = k
            for r in range(2):
                rows_ = slice(64 * r, 64 * r + 64)
                k2 = copy_act(A[rows_, :], psum[rows_, b, r::2], k)
            give(b, k2)
            src = bass.AP(A.tensor, A.offset, [list(A.ap[0]), [1, 16], [128, 2], [8, 15]])
            return B, tt(dve, B.rearrange("p j (g c) -> p j g c", g=2), src,
                         pe_col.unsqueeze(2).unsqueeze(3).to_broadcast([P, 16, 2, 15]), ALU.add, k2, in_cols)

        def hidden(w1, B, ready):
            tiles = []
            for j0 in (0, 8):
                tiles.append(weight(w1[j0 * P:(j0 + 8) * P, :], 8, 256))
            h1 = space.take(60).rearrange("p (s c) -> p s c", s=2)
            b, free = bank()
            for s in range(2):
                pairs = [(tiles[j // 8][0][:, j % 8, s * P:s * P + P], B[:, j, :]) for j in range(16)]
                t = group(psum[:, b, 32 * s:32 * s + 30], pairs, ready, free, more=[tiles[j // 8][2] for j in range(16)])
            for _, i, _ in tiles:
                used(i, t)
            k = fn(h1, psum[:, b, 0:64].rearrange("p (s c) -> p s c", s=2)[:, :, 0:30], ACT.Silu, t)
            give(b, k)
            return h1, k

        Bk, k_Bk = windows(8, col("pe_k"), k_rot)
        Bv, k_Bv = windows(10, col("pe_v"), k_qkv)
        step()
        hk, k_hk = hidden(a["cmp_k_w1"][0], Bk, k_Bk)
        hv, k_hv = hidden(a["cmp_v_w1"][0], Bv, k_Bv)
        step()
        kTc = space.take(30)
        vc = space.take(128).rearrange("p (g d) -> p g d", g=2)
        b, free = bank()
        k = group(psum[:, b, 0:30], [(w2k[:, s, :, :].rearrange("p r d -> p (r d)"), hk[:, s, :]) for s in range(2)],
                  k_hk, free, in_w2k)
        k_kTc = copy_act(kTc, psum[:, b, 0:30], k)
        give(b, k_kTc)
        b, free = bank()
        for g in range(2):
            k = group(psum[0:15, b, 64 * g:64 * g + 64],
                      [(hv[:, s, 15 * g:15 * g + 15], w2v[:, s, :]) for s in range(2)], k_hv, free, in_w2v)
        k_vc = copy_act(vc[0:15, :, :], psum[0:15, b, 0:128].rearrange("p (g d) -> p g d", g=2), k)
        give(b, k_vc)

        den = space.take(48).rearrange("p (t h b) -> p t h b", t=2, h=8)
        coef = space.take(48).rearrange("p (t h b) -> p t h b", t=2, h=8)
        pc = space.take(240).rearrange("p (t h c) -> p t h c", t=2, h=8)
        pc2 = pc.rearrange("p t h c -> p (t h) c")
        mxc = space.take(16)
        for odd in range(2):
            b, free = bank()
            C = psum[:, b, 0:120].rearrange("p (t h c) -> p t h c", t=2, h=4)
            r = slice(64 * odd, 64 * odd + 64)
            for t in range(2):
                for i in range(4):
                    g = i // 2
                    k = group(C[:, t, i, :], [(qT[r, i, t * P:t * P + P], kTc[r, 15 * g:15 * g + 15])],
                              k_qT, k_kTc, free)
            for t in range(2):
                kc_ = stt(pc[:, t, odd::2, :], C[:, t, :, :], 0.125,
                          bc(const("cmask")[:, 15 * t:15 * t + 15], 1, [P, 4, 15]), ALU.mult, ALU.add, k)
            give(b, kc_)
        k = dve.do(lambda e: e.tensor_reduce(mxc, pc2, AX.X, ALU.max), kc_)
        k = tt(dve, pc2, pc2, bc(mxc, 2, [P, 16, 15]), ALU.subtract, k)
        k_pc = fn(pc2, pc2, ACT.Exp, k)
        k_dc = dve.do(lambda e: e.tensor_reduce(den.rearrange("p t h b -> p (t h) b")[:, :, 0:1], pc2, AX.X, ALU.add), k_pc)

        probs1 = space.take(4096)
        probs = [big[:, :, :].rearrange("p t n -> p (t n)").rearrange("p (h b n) -> p h b n", h=8, b=2),
                 probs1.rearrange("p (h b n) -> p h b n", h=8, b=2)]
        mx = space.take(32).rearrange("p (t h b) -> p t h b", t=2, h=8)
        k_exp = {}

        def scores(t, h):
            nk = P * (t + 1)
            g, r = h // 4, slice(64 * (h % 2), 64 * (h % 2) + 64)
            b, free = bank()
            S = psum[:, b, 0:2 * nk].rearrange("p (b n) -> p b n", b=2)
            for br in range(2):
                k = group(S[:, br, :], [(qT[r, h // 2, t * P:t * P + P], kT[r, br, g, 0:nk])], k_qT, k_kT, free)
            diag = S[:, :, t * P:t * P + P]
            k = tt(dve, diag, diag, bc(const("causal"), 1, [P, 2, P]), ALU.add, k)
            m = mx[:, t, h, :]
            k = dve.do(lambda e: e.tensor_reduce(m, S, AX.X, ALU.max), k)
            k = ts(dve, m, m, -0.125, None, ALU.mult, None, k)
            for br in range(2):
                k2 = fn(probs[t][:, h, br, :], S[:, br, :], ACT.Exp, k, bias=m[:, br:br + 1], scale=0.125,
                        accum_out=den[:, t, h, 1 + br:2 + br])
            k_exp[t, h] = k2
            give(b, k2)

        def weights(t):
            k = dve.do(lambda e: e.reciprocal(coef[:, t, :, :], den[:, t, :, :]), k_exp[t, 7], k_dc)
            k = tt(dve, coef[:, t, :, :], coef[:, t, :, :], gsig[:, t, :, :], ALU.mult, k, k_gsig)
            k = ts(dve, coef[:, t, :, 0:1], coef[:, t, :, 0:1], const("crow")[:, t:t + 1], None, ALU.mult, None, k)
            k = tt(dve, pc[:, t, :, :], pc[:, t, :, :], coef[:, t, :, 0:1].to_broadcast([P, 8, 15]), ALU.mult, k)
            return k

        nsaT = win[:, 0:1024].rearrange("p (c n) -> p c n", c=4)
        pT = [tmp_all[:, 1024:1536], tmp_all[:, 1536:2048]]
        pcT = tmp_all[:, 0:1024].rearrange("p (h n) -> p h n", h=8)
        pT_free = [None] * 2
        npt = [0]

        def cmp_T(t, k, pv_done):
            for h0 in (0, 4):
                b, free = bank()
                k2 = transposes(psum[:, b, :], [pc[:, t, h, :] for h in range(h0, h0 + 4)], k, free)
                k2 = copy_dve(pcT[0:15, h0:h0 + 4, :], psum[0:15, b, :].rearrange("p (h n) -> p h n", h=4), k2, pv_done)
                give(b, k2)
            return k2

        def pv(t, h, O, kw_, kcT, ofree):
            nk = P * (t + 1)
            Ph = probs[t][:, h, :, :]
            k = tt(dve, Ph, Ph, coef[:, t, h, 1:3].unsqueeze(2).to_broadcast([P, 2, nk]), ALU.mult, kw_)
            b, free = bank()
            parts = [(br, kt) for br in range(2) for kt in range(t + 1)]
            k = transposes(psum[:, b, :], [Ph[:, br, kt * P:kt * P + P] for br, kt in parts], k, free)
            i = npt[0] % 2
            npt[0] += 1
            n = len(parts) * P
            k = copy_act(pT[i][:, 0:n], psum[:, b, 0:n], k, pT_free[i])
            give(b, k)
            g, r = h // 4, 64 * (h % 2)
            pairs = [(vc[0:15, g, :], pcT[0:15, h, :])]
            for n, (br, kt) in enumerate(parts):
                v = heads[:, kt, (14, 18)[br] + g, :]
                pairs.append((v, pT[i][:, n * P:n * P + P]))
            k = group(O[r:r + 64, h // 2, :], pairs, k, k_vc, kcT, ofree)
            pT_free[i] = k
            return k

        done = None
        kws = []
        for t in range(2):
            for h in range(8):
                scores(t, h)
                if h % 3 == 2:
                    step()
            kws.append(weights(t))
        for t in range(2):
            kcT = cmp_T(t, kws[t], done)
            b, free = bank()
            O = psum[:, b, :].rearrange("p (c n) -> p c n", c=4)
            for h in range(8):
                done = pv(t, h, O, kws[t], kcT, free)
            k_nsaT = copy_dve(nsaT[:, :, t * P:t * P + P], O, done)
            give(b, k_nsaT)

        rqT, rkT = (probs1[:, i:i + 1024].rearrange("p (h n) -> p h n", h=4) for i in (0, 1024))
        for dst, src, name in ((rqT, rq, "rq"), (rkT, rk, "rk")):
            for t in range(2):
                b, free = bank()
                k = transposes(psum[:, b, :], [src[:, t, h * P:h * P + P] for h in range(4)], kr[name], free)
                k_rT = copy_act(dst[:, :, t * P:t * P + P], psum[:, b, :].rearrange("p (h n) -> p h n", h=4), k)
                give(b, k_rT)
        RS = probs1[:, 2048:3584].rearrange("p (h n) -> p h n", h=4)
        decay = const("decay").rearrange("p (h n) -> p h n", h=4)
        for h in range(4):
            b, free = bank()
            group(psum[:, b, 0:256], [(rkT[:, h, 0:P], rqT[:, h, :])], k_rT, free)
            k = group(psum[:, b, 256:384], [(rkT[:, h, P:256], rqT[:, h, P:256])])
            tt(dve, RS[:, h, 0:256], psum[:, b, 0:256], decay[:, h, :], ALU.mult, k)
            k_RS = tt(dve, RS[:, h, 256:384], psum[:, b, 256:384], decay[:, h, 0:P], ALU.mult)
            give(b, k_RS)
        rss, rrs = stat(8), stat(8)
        retT = rqT
        for t in range(2):
            b, free = bank()
            O = psum[:, b, :].rearrange("p (h n) -> p h n", h=4)
            for h in range(4):
                pairs = [(RS[:, h, t * P:t * P + P], rv[:, 0, h * P:h * P + P])]
                if t:
                    pairs.append((RS[:, h, 256:384], rv[:, 1, h * P:h * P + P]))
                k = group(O[:, h, :], pairs, k_RS, kr["rv"], free)
            for h in range(4):
                k2 = sum_sq(rss[:, 4 * t + h:4 * t + h + 1], O[:, h, :], k)
            k2 = rsqrt_mean(rrs[:, 4 * t:4 * t + 4], rss[:, 4 * t:4 * t + 4], P, k2)
            ro = rg[:, t, :].rearrange("p (h n) -> p h n", h=4)
            k = tt(dve, ro, O, ro, ALU.mult, k, kr["rg"], k2)
            give(b, k)
            k = tt(dve, ro, ro, bc(rrs[:, 4 * t:4 * t + 4], 2, [P, 4, P]), ALU.mult, k)
            b, free = bank()
            k = transposes(psum[:, b, :], [ro[:, h, :] for h in range(4)], k, free)
            k_retT = copy_act(retT[:, :, t * P:t * P + P], psum[:, b, :].rearrange("p (h n) -> p h n", h=4), k)
            give(b, k_retT)
        step(8)

        def merge(wa, aT, ka, wb, bT, kb, sig, ksig, dst):
            got = {}

            def evac(which):
                def f(q, ps, tok):
                    g = sig[:, 8 * which + 2 * q:8 * which + 2 * q + 2, :]
                    k = tt(dve, g, ps, g, ALU.mult, tok, ksig[8 * which + 2 * q])
                    if which:
                        o = dst[:, 2 * q:2 * q + 2, :]
                        got["k"] = tt(dve, o, sig[:, 2 * q:2 * q + 2, :], g, ALU.add, k, got.get(q))
                    else:
                        got[q] = k
                    return k
                return f
            ga, gb = fm(wa, 0, D, aT, ka, evac(0)), fm(wb, 0, D, bT, kb, evac(1))
            run(ga, gb)
            return got["k"]

        mixT = xT
        k_mix = merge(a["w_proj_a"][0], nsaT, k_nsaT, a["w_proj_b"][0], retT, k_retT, sig, k_sig, mixT)

        k_x = {}

        def to_residual(blk, t, ps, tok):
            k_x[t] = tt(dve, x[:, t, blk * 512:blk * 512 + 512], ps, x[:, t, blk * 512:blk * 512 + 512], ALU.add, tok)
            return k_x[t]

        run(tm(a["w_out"][0], 0, D, mixT, k_mix, to_residual))
        h_ready = norm_T(lambda t: x[:, t, :], [k_x[0], k_x[1]], col("norm_mlp"), xT, big)

        space.at = 0
        uT = space.take(8192).rearrange("p (c n) -> p c n", c=32)
        k_u = {}

        def to_relu2(q, ps, tok):
            o = uT[:, 2 * q:2 * q + 2, :]
            k = fn(o, ps, ACT.Relu, tok)
            k_u[q] = stt(o, ps, 0.0, o, ALU.max, ALU.mult, k)
            return k_u[q]

        run(fm(a["w_up"][0], 0, 4096, xT, h_ready, to_relu2))

        def to_down(h, t, ps, tok):
            return to_residual(h, t, ps, tok)
        down(a["w_down"][0], uT, lambda k: k_u[k // 2], to_down)

        k_y = []
        for t in range(2):
            ss, r = stat(1), stat(1)
            k = sum_sq(ss, x[:, t, :], k_x[t])
            k = rsqrt_mean(r, ss, D, k)
            k_y.append(stt(x[:, t, :], x[:, t, :], r, row("norm_final"), ALU.mult, ALU.mult, k, k_x[t], in_rows))

        space.at = 0
        w2 = a["w_in_2"][0]
        h_ready = norm_T(lambda t: x[:, t, :], k_y, col("norm_mix_2"), xT, big)
        raw = space.take(3108).rearrange("p (c n) -> p c n", c=12)
        cv = space.take(3072).rearrange("p (c n) -> p c n", c=12)
        k_pad = pool.do(lambda e: e.memset(raw[:, :, 0:3], 0.0), h_ready)
        cw = col("conv_w").rearrange("p (c k) -> p c k", k=4)
        k_cv = {}

        def to_conv(q, ps, tok):
            c = 2 * q
            k = copy_act(raw[:, c:c + 2, 3:259], ps, tok)
            dve.wait(k, k_pad)
            for i in (c, c + 1):
                ts(dve, cv[:, i, :], raw[:, i, 0:256], cw[:, i, 0:1], col("conv_b")[:, i:i + 1], ALU.mult, ALU.add)
                for j in range(1, 4):
                    k2 = stt(cv[:, i, :], raw[:, i, j:j + 256], cw[:, i, j:j + 1], cv[:, i, :], ALU.mult, ALU.add)
            k_cv[q] = fn(cv[:, c:c + 2, :], cv[:, c:c + 2, :], ACT.Silu, k2)
            return k

        run(fm(w2, 1024, 1536, xT, h_ready, to_conv))

        small = space.take(400)
        dt_, e_, s_, s2_, p_, aa = (small[:, 32 * i:32 * i + 32] for i in range(6))
        Aexp, e1, d0 = (small[:, 192 + 16 * i:208 + 16 * i] for i in range(3))
        k_Ae = fn(Aexp, row("ssd_A_log_2"), ACT.Exp, in_rows, h_ready)
        kdt = {}

        def to_dt(blk, t, ps, tok):
            kdt[t] = tt(dve, dt_[:, 16 * t:16 * t + 16], ps, row("ssd_dt_bias_2"), ALU.add, tok)
            return kdt[t]

        run(tm(w2, 2560, 16, xT, h_ready, to_dt))
        k = stt(e_, dt_, -1.0, dt_, ALU.mult, ALU.min, kdt[1])
        k = fn(e_, e_, ACT.Exp, k)
        k = ts(dve, s_, e_, 2.0, None, ALU.add, None, k)
        k = dve.do(lambda e: e.reciprocal(s_, s_), k)
        k = tt(dve, s_, s_, e_, ALU.mult, k)
        k = tt(dve, s2_, s_, s_, ALU.mult, k)
        k = ts(dve, p_, s2_, 1 / 17, None, ALU.mult, None, k)
        for c in (15, 13, 11, 9, 7, 5, 3):
            k = stt(p_, p_, 1 / c, s2_, ALU.add, ALU.mult, k)
        k = stt(p_, p_, 1.0, s_, ALU.add, ALU.mult, k)
        k = ts(dve, p_, p_, 2.0, None, ALU.mult, None, k)
        k_dt = stt(dt_, dt_, 0.0, p_, ALU.max, ALU.add, k)
        dt3 = dt_.rearrange("p (t h) -> p t h", t=2)
        a3 = aa.rearrange("p (t h) -> p t h", t=2)
        k_a = stt(a3, dt3, -1.0, bc(Aexp, 1, [P, 2, 16]), ALU.mult, ALU.mult, k_dt, k_Ae)
        upper, after = const("upper"), const("after")
        b, free = bank()
        group(psum[:, b, 0:16], [(upper, a3[:, 1, :])], k_a, free)
        k = group(psum[:, b, 16:32], [(after, a3[:, 0, :])])
        fn(e1, psum[:, b, 0:16], ACT.Exp, k)
        k_dec = fn(d0, psum[:, b, 16:32], ACT.Exp, k)
        give(b, k_dec)

        zs = space.take(2048).rearrange("p (t n) -> p t n", t=2)
        gq, gk = (space.take(1024).rearrange("p (h n) -> p h n", h=4) for _ in range(2))
        gv = space.take(2048).rearrange("p (t n) -> p t n", t=2)
        a1T = space.take(256)
        kg = {}

        def keep_fm(dst, name):
            def evac(q, ps, tok):
                kg[name] = copy_act(dst[:, 2 * q:2 * q + 2, :], ps, tok)
                return kg[name]
            return evac

        def keep_a1(q, ps, tok):
            kg["a1"] = copy_act(a1T[0:16, :], ps[:, 0, :], tok)
            return kg["a1"]

        def keep_tm(dst, name, f):
            def evac(blk, t, ps, tok):
                kg[name] = fn(dst[:, t, 512 * blk:512 * blk + 512], ps, f, tok)
                return kg[name]
            return evac

        def chain(*gens):
            for g in gens:
                yield from g

        fill = chain(tm(w2, 0, 1024, xT, h_ready, keep_tm(zs, "z", ACT.Silu)),
                     fm(w2, 2576, 512, xT, h_ready, keep_fm(gq, "q")),
                     fm(w2, 3088, 512, xT, h_ready, keep_fm(gk, "k")),
                     fm(w2, 5648, 16, xT, h_ready, keep_a1),
                     tm(w2, 3600, 1024, xT, h_ready, keep_tm(gv, "v", ACT.Copy)))

        xs = space.take(2048).rearrange("p (t n) -> p t n", t=2)
        X = space.take(2048).rearrange("p (t n) -> p t n", t=2)
        Xd = space.take(1024)
        CB = space.take(768).rearrange("p (g n) -> p g n", g=2)
        step()
        for t in range(2):
            for q in range(2):
                b, free = bank()
                k = transposes(psum[:, b, :], [cv[:, 4 * q + j, t * P:t * P + P] for j in range(4)],
                               k_cv[2 * q], k_cv[2 * q + 1], free)
                k_xs = copy_act(xs[:, t, 512 * q:512 * q + 512], psum[:, b, :], k)
                give(b, k_xs)
            k_X = tt(dve, X[:, t, :].rearrange("p (h d) -> p h d", h=16), xs[:, t, :].rearrange("p (h d) -> p h d", h=16),
                     bc(dt3[:, t, :], 2, [P, 16, 64]), ALU.mult, k_xs, k_dt)
        k_Xd = tt(dve, Xd.rearrange("p (h d) -> p h d", h=16), X[:, 0, :].rearrange("p (h d) -> p h d", h=16),
                  bc(d0, 2, [P, 16, 64]), ALU.mult, k_X, k_dec)
        for g in range(2):
            b, free = bank()
            group(psum[:, b, 0:256], [(cv[:, 8 + g, 0:P], cv[:, 10 + g, :])], k_cv[4], k_cv[5], free)
            k = group(psum[:, b, 256:384], [(cv[:, 8 + g, P:256], cv[:, 10 + g, P:256])])
            v = psum[:, b, 0:384]
            dve.wait(k)
            tt(dve, CB[:, g, 0:P], v[:, 0:P], upper, ALU.mult)
            tt(dve, CB[:, g, 256:384], v[:, 256:384], upper, ALU.mult)
            k_CB = copy_dve(CB[:, g, P:256], v[:, P:256])
            give(b, k_CB)

        rot = [raw.rearrange("p c n -> p (c n)")[:, 512 * i:512 * i + 512].rearrange("p (h n) -> p h n", h=4)
               for i in range(6)]
        La, E = rot[0:3], rot[3:6]
        k_La, k_E, E_free, La_free = {}, {}, [None] * 3, [None] * 3
        quads = [(t, q) for t in range(2) for q in range(4)]

        def seg(i):
            t, q = quads[i]
            v = La[i % 3]
            k = tt(dve, v, bc(after, 1, [P, 4, P]), bc(a3[:, t, 4 * q:4 * q + 4], 2, [P, 4, P]), ALU.mult,
                   k_a, La_free[i % 3])
            b, free = bank()
            for h in range(4):
                k = group(psum[:, b, h * P:h * P + P], [(v[:, h, :], upper)], k, free)
            La_free[i % 3] = k
            o = E[i % 3]
            k = fn(o, psum[:, b, :].rearrange("p (h n) -> p h n", h=4), ACT.Exp, k, E_free[i % 3])
            give(b, k)
            k_E[i] = tt(dve, o, o, bc(CB[:, q // 2, 256 * t:256 * t + P], 1, [P, 4, P]), ALU.mult, k, k_CB)

        yss, yrs = stat(4), stat(4)
        yT = space.take(2048).rearrange("p (c n) -> p c n", c=8)
        k_yT = None
        ybank = {}

        def diag(i):
            t, q = quads[i]
            g = q // 2
            if q % 2 == 0:
                ybank[t, g] = bank()
            b, free = ybank[t, g]
            for h in range(4):
                o = 256 * (q % 2) + 64 * h
                k = group(psum[:, b, o:o + 64], [(E[i % 3][:, h, :], X[:, t, 256 * q + 64 * h:256 * q + 64 * h + 64])],
                          k_E[i], k_X, free)
            E_free[i % 3] = k
            if q % 2 == 0:
                return
            c = slice(512 * g, 512 * g + 512)
            by_head = lambda v: v.rearrange("p (h d) -> p h d", h=8)
            Dr = bc(row("ssd_D_2")[:, 8 * g:8 * g + 8], 2, [P, 8, 64])
            y = xs[:, t, c]
            k2 = tt(dve, by_head(y), by_head(y), Dr, ALU.mult, in_rows)
            k2 = tt(dve, y, psum[:, b, :], y, ALU.add, k2, k)
            give(b, k2)
            if t:
                b, free = bank()
                k = group(psum[:, b, :], [(CB[:, g, P:256], Xd[:, c])], k_CB, k_Xd, free)
                x1 = X[:, 1, c]
                k = tt(dve, by_head(x1), by_head(psum[:, b, :]), bc(e1[:, 8 * g:8 * g + 8], 2, [P, 8, 64]), ALU.mult,
                       k, k_dec)
                give(b, k)
                k2 = tt(dve, y, y, x1, ALU.add, k, k2)
            k2 = tt(dve, y, y, zs[:, t, c], ALU.mult, k2, kg["z"])
            j = 2 * t + g
            k = sum_sq(yss[:, j:j + 1], y, k2)
            k = rsqrt_mean(yrs[:, j:j + 1], yss[:, j:j + 1], 512, k)
            k = ts(dve, y, y, yrs[:, j:j + 1], None, ALU.mult, None, k)
            k_y2[t, g] = k

        def y_out(t, g):
            y = xs[:, t, 512 * g:512 * g + 512]
            b, free = bank()
            k = transposes(psum[:, b, :], [y[:, 128 * j:128 * j + 128] for j in range(4)], k_y2[t, g], free)
            k = tt(dve, yT[:, 4 * g:4 * g + 4, t * P:t * P + P], psum[:, b, :].rearrange("p (j n) -> p j n", j=4),
                   bc(col("ssd_norm_2")[:, 4 * g:4 * g + 4], 2, [P, 4, P]), ALU.mult, k, in_cols)
            give(b, k)
            return k
        k_y2 = {}
        seg(0)
        step()
        seg(1)
        step(2)
        for i in range(8):
            if i + 2 < 8:
                seg(i + 2)
            diag(i)
            step()
            if i in (2, 4, 6):
                k_yT = y_out(*((0, 0), (0, 1), (1, 0))[i // 2 - 1])
        step(20)
        k_yT = y_out(1, 1)

        def region(at, n):
            return arena[:, at:at + n]

        gr = region(0, 2048).rearrange("p (t n) -> p t n", t=2)
        la, bcum, kt_, kh = (region(2048 + 1024 * i, 1024).rearrange("p (h n) -> p h n", h=4) for i in range(4))
        sig = region(12980, 4096).rearrange("p (c n) -> p c n", c=16)
        ST = region(17076, 1536).rearrange("p (c h n) -> p c h n", c=3, h=4)
        oT = region(6580, 2048).rearrange("p (c n) -> p c n", c=8)
        ke, qe = (space.take(512).rearrange("p (h n) -> p h n", h=4) for _ in range(2))
        dec = space.take(16)
        tmpg = big[:, 0, :].rearrange("p (h n) -> p h n", h=4)
        k_sig = {}

        for i in range(2):
            b, free = bank()
            for s in range(2):
                h = 2 * i + s
                k = group(psum[:, b, 256 * s:256 * s + 256], [(wa2[:, h * P:h * P + P], a1T[0:16, :])],
                          kg["a1"], in_wa2, free)
            for s in range(2):
                h = 2 * i + s
                k_la = ts(dve, la[:, h, :], psum[:, b, 256 * s:256 * s + 256], col("gla_b")[:, h:h + 1], None,
                          ALU.add, None, k, k_yT)
            give(b, k_la)
        k = stt(tmpg, la, -1.0, la, ALU.mult, ALU.min, k_la)
        k = fn(tmpg, tmpg, ACT.Exp, k)
        k = fn(tmpg, tmpg, ACT.Ln, k, bias=1.0)
        k = stt(la, la, 0.0, tmpg, ALU.min, ALU.subtract, k)
        for h in range(4):
            k_b = dve.do(lambda e, h=h: e.tensor_tensor_scan(bcum[:, h, :], const("keep"), la[:, h, :], 0.0,
                                                             ALU.mult, ALU.add), k)
        k = fn(tmpg, bcum, ACT.Exp, k_b, scale=1 / 16)
        k_qt = stt(gq, gq, P ** -0.5, tmpg, ALU.mult, ALU.mult, k, kg["q"])
        k = fn(kt_, bcum, ACT.Exp, k_b, scale=-1 / 16)
        k_kt = tt(dve, kt_, kt_, gk, ALU.mult, k, kg["k"])
        by_chunk = lambda v: v.rearrange("p h (c n) -> p (h c) n", c=4)
        last = by_chunk(bcum)[:, :, 63:64]
        k = tt(dve, by_chunk(kh), last.to_broadcast([P, 16, 64]), by_chunk(bcum), ALU.subtract, k_b)
        k = fn(kh, kh, ACT.Exp, k, scale=1 / 16)
        k_kh = tt(dve, kh, kh, gk, ALU.mult, k)
        k_dec = fn(dec.unsqueeze(2), last, ACT.Exp, k_b, scale=1 / 16)
        dec3 = dec.rearrange("p (h c) -> p h c", c=4)
        dve.wait(k_dec)
        tt(dve, ke[:, :, 0:64], kh[:, :, 0:64], dec3[:, :, 1:2].to_broadcast([P, 4, 64]), ALU.mult)
        copy_dve(ke[:, :, 64:P], kh[:, :, 64:P])
        tt(dve, qe[:, :, 64:P], gq[:, :, 192:256], dec3[:, :, 2:3].to_broadcast([P, 4, 64]), ALU.mult)
        k_e2 = copy_dve(qe[:, :, 0:64], gq[:, :, P:192])

        fill = chain(tm(w2, 4624, 1024, xT, h_ready, keep_tm(gr, "r", ACT.Silu)),
                     fm(w2, 5664, 2048, xT, h_ready, to_sigmoid(sig, 0, k_sig)))
        act.wait(k_yT)
        step(4)
        for t in range(2):
            b, free = bank()
            c0, c1 = 2 * t * 64, 2 * t * 64 + 64
            for h in range(4):
                o = psum[:, b, h * P:h * P + P]
                group(o[0:64, 0:64], [(kt_[:, h, c0:c1], gq[:, h, c0:c1])], k_qt, k_kt, k_kh, free)
                group(o[0:64, 64:P], [(kh[:, h, c0:c1], gq[:, h, c1:c1 + 64])])
                k = group(o[64:P, :], [(kt_[:, h, c1:c1 + 64], gq[:, h, c0:c1 + 64])])
            k_ST = tt(dve, ST[:, t, :, :], psum[:, b, :].rearrange("p (h n) -> p h n", h=4), bc(upper, 1, [P, 4, P]),
                      ALU.mult, k)
            give(b, k_ST)
            step()
        b, free = bank()
        for h in range(4):
            k = group(psum[:, b, h * P:h * P + P], [(ke[:, h, :], qe[:, h, :])], k_e2, free)
        k_ST = copy_dve(ST[:, 2, :, :], psum[:, b, :].rearrange("p (h n) -> p h n", h=4), k)
        give(b, k_ST)
        step()
        gss, grs = stat(8), stat(8)
        for t in range(2):
            for i in range(2):
                b, free = bank()
                for s in range(2):
                    h = 2 * i + s
                    pairs = [(ST[:, t, h, :], gv[:, t, 256 * h:256 * h + 256])]
                    if t:
                        pairs.append((ST[:, 2, h, :], gv[:, 0, 256 * h:256 * h + 256]))
                    k = group(psum[:, b, 256 * s:256 * s + 256], pairs, k_ST, kg["v"], free)
                j = 4 * t + 2 * i
                for s in range(2):
                    k2 = sum_sq(gss[:, j + s:j + s + 1], psum[:, b, 256 * s:256 * s + 256], k)
                k2 = rsqrt_mean(grs[:, j:j + 2], gss[:, j:j + 2], 256, k2)
                o = gr[:, t, 512 * i:512 * i + 512]
                k = tt(dve, o, psum[:, b, :], o, ALU.mult, k, kg["r"], k2)
                give(b, k)
                o2 = o.rearrange("p (h n) -> p h n", h=2)
                k = tt(dve, o2, o2, bc(grs[:, j:j + 2], 2, [P, 2, 256]), ALU.mult, k)
                step()
                b, free = bank()
                k = transposes(psum[:, b, :], [o[:, 128 * m:128 * m + 128] for m in range(4)], k, free)
                k_oT = tt(dve, oT[:, 4 * i:4 * i + 4, t * P:t * P + P].rearrange("p (h c) n -> p h c n", c=2),
                          psum[:, b, :].rearrange("p (h c n) -> p h c n", h=2, c=2),
                          col("gla_norm_2").unsqueeze(1).unsqueeze(3).to_broadcast([P, 2, 2, P]), ALU.mult, k, in_cols)
                give(b, k_oT)
        step(20)
        k_mix = merge(a["w_up_ssd_2"][0], yT, k_yT, a["w_up_gla_2"][0], oT, k_oT, sig, k_sig, mixT)
        run(tm(a["w_o_2"][0], 0, D, mixT, k_mix, to_residual))

        kx = [k_x[0], k_x[1]]
        space.at = 0
        mem = space.take(2048).rearrange("p (t n) -> p t n", t=2)
        memT, mkT, oxT = (space.take(2048).rearrange("p (c n) -> p c n", c=8) for _ in range(3))
        mv = space.take(2048).rearrange("p (t n) -> p t n", t=2)
        qx = space.take(2048).rearrange("p (c n) -> p c n", c=8)
        px = space.take(2048).rearrange("p (t h n) -> p t h n", t=2, h=4)
        pxT = space.take(2048).rearrange("p (h m n) -> p h m n", h=4, m=2)
        in_mem = sp.dma(s_in["mem"], 16, mem, a["mem_2"].rearrange("b (t p) d -> p (b t) d", p=P), kx)
        k_mem = norm_T(lambda t: mem[:, t, :], [in_mem, in_mem], col("norm_mem_2"), memT, big)
        wkv = a["w_xkv_2"][0]
        run(fm(wkv, 0, D, memT, k_mem, keep_fm(mkT, "mk")), tm(wkv, D, D, memT, k_mem, keep_tm(mv, "mv", ACT.Copy)))
        h_ready = norm_T(lambda t: x[:, t, :], kx, col("norm_xattn_2"), xT, big)
        run(fm(a["w_xq_2"][0], 0, D, xT, h_ready, keep_fm(qx, "qx")))
        xm, xden = stat(8), stat(8)
        for h in range(4):
            b, free = bank()
            S = psum[:, b, :].rearrange("p (t n) -> p t n", t=2)
            for t in range(2):
                k = group(S[:, t, :], [(qx[:, 2 * h + c, t * P:t * P + P], mkT[:, 2 * h + c, :]) for c in range(2)],
                          kg["qx"], kg["mk"], free)
            m, d = xm[:, 2 * h:2 * h + 2], xden[:, 2 * h:2 * h + 2]
            k = dve.do(lambda e, m=m, S=S: e.tensor_reduce(m, S, AX.X, ALU.max), k)
            k = ts(dve, m, m, -1 / 16, None, ALU.mult, None, k)
            for t in range(2):
                k2 = fn(px[:, t, h, :], S[:, t, :], ACT.Exp, k, bias=m[:, t:t + 1], scale=1 / 16, accum_out=d[:, t:t + 1])
            give(b, k2)
            k = dve.do(lambda e, d=d: e.reciprocal(d, d), k2)
            k = tt(dve, px[:, :, h, :], px[:, :, h, :], bc(d, 2, [P, 2, 256]), ALU.mult, k)
            b, free = bank()
            k = transposes(psum[:, b, :], [px[:, t, h, m * P:m * P + P] for m in range(2) for t in range(2)], k, free)
            k = copy_act(pxT[:, h, :, :], psum[:, b, :].rearrange("p (m n) -> p m n", m=2), k)
            give(b, k)
            b, free = bank()
            for c in range(2):
                f = 256 * h + 128 * c
                k = group(psum[:, b, 256 * c:256 * c + 256], [(mv[:, m, f:f + P], pxT[:, h, m, :]) for m in range(2)],
                          k, kg["mv"], free)
            k_ox = copy_act(oxT[:, 2 * h:2 * h + 2, :], psum[:, b, :].rearrange("p (c n) -> p c n", c=2), k)
            give(b, k_ox)
        run(tm(a["w_xo_2"][0], 0, D, oxT, k_ox, to_residual))

        kx = [k_x[0], k_x[1]]
        h_ready = norm_T(lambda t: x[:, t, :], kx, col("norm_ffn_2"), xT, big)
        space.at = 0
        gT = space.take(5632).rearrange("p (c n) -> p c n", c=22)
        k_u, k_g = {}, {}

        def to_gate(q, ps, tok):
            k_g[q] = fn(gT[:, 2 * q:2 * q + 2, :], ps, ACT.Silu, tok)
            return k_g[q]

        def to_up(q, ps, tok):
            o = gT[:, 2 * q:2 * q + 2, :]
            k_u[q] = tt(dve, o, ps, o, ALU.mult, tok, k_g[q])
            return k_u[q]

        wf = a["w_ffn_in_2"][0]
        for _ in zip(fm(wf, 0, 2816, xT, h_ready, to_gate), fm(wf, 2816, 2816, xT, h_ready, to_up)):
            pass
        down(a["w_ffn_out_2"][0], gT, lambda k: k_u[k // 2], to_down)
        k_y = []
        for t in range(2):
            ss, r = stat(1), stat(1)
            k = sum_sq(ss, x[:, t, :], k_x[t])
            k = rsqrt_mean(r, ss, D, k)
            k_y.append(stt(x[:, t, :], x[:, t, :], r, row("norm_final_2"), ALU.mult, ALU.mult, k, k_x[t], in_rows))
        k_out = k_y
        s_out = sem("s_out")
        sp.dma(s_out, 16, out.rearrange("b (t p) d -> p (b t) d", p=P), x[:, :, :], *k_out)
        sp.wait((s_out, 16))

        block = ctx.enter_context(nc.Block())
        for name, q in (("tensor", pe), ("scalar", act), ("vector", dve), ("gpsimd", pool), ("sync", sp)):
            def emit(e, q=q):
                for f in q.todo:
                    f(e)
            (block.tensor if name == "tensor" else block.scalar if name == "scalar" else
             block.vector if name == "vector" else block.gpsimd if name == "gpsimd" else block.sync)(emit)


def shape_constants():
    i = np.arange(P)
    v = {}
    v["ident"] = np.eye(P)
    v["upper"] = i[:, None] <= i[None, :]
    v["after"] = i[:, None] > i[None, :]
    v["causal"] = np.where(i[None, :] <= i[:, None], 0.0, NEG)
    end = 16 * np.arange(15) + 31
    tok = i[:, None] + P * np.arange(2)[None, :]
    v["cmask"] = np.where(end[None, None, :] <= tok[:, :, None], 0.0, NEG).reshape(P, 30)
    v["crow"] = tok >= 31
    lg = np.log(1.0 - np.exp2(-5.0 - np.arange(4)))
    rel = np.arange(256)[None, :] - i[:, None]
    v["decay"] = np.concatenate([np.where(rel >= 0, np.exp(g * np.maximum(rel, 0)), 0.0) * P ** -0.5 for g in lg], 1)
    v["inv"] = np.tile(np.array(INV_BITS, np.uint32).view(np.float32)[None, :], (P, 1))
    v["keep"] = np.tile((np.arange(256) % 64 != 0)[None, :], (P, 1))
    return np.ascontiguousarray(np.concatenate([np.asarray(v[n], np.float32) for n in CONSTS], 1))


INV_BITS = [
    0x3f800000, 0x3e4693b0, 0x3d1a08c9, 0x3beef752, 0x3ab95d24, 0x398fc8f8, 0x385f10cb, 0x372d07a6, 0x3f800000,
    0x3f5dafd6, 0x3f3ff911, 0x3f263de0, 0x3f0ff59a, 0x3ef953ce, 0x3ed7e89a, 0x3ebaf81a, 0x3ea1e89b, 0x3e8c3503,
    0x3e72d422, 0x3e5247ed, 0x3e361887, 0x3e1db040, 0x3e088d77, 0x3dec7fd5, 0x3dcccccc, 0x3db15978, 0x3d99940d,
    0x3d84fe4c, 0x3d6655c1, 0x3d477640, 0x3d2cba16, 0x3d159348, 0x3d0186e2, 0x3ce054d1, 0x3cc2434e, 0x3ca83989,
    0x3c91ad3a, 0x3c7c4d30, 0x3c5a7bf1, 0x3c3d330e, 0x3c23d70a, 0x3c0de12e, 0x3bf5b9ad, 0x3bd4ca16, 0x3bb8449a,
    0x3b9f91cc, 0x3b8a2e75, 0x3b6f520d, 0x3b4f3e33, 0x3b33770d, 0x3b1b690e, 0x3b06946d, 0x3ae91528, 0x3ac9d759,
    0x3aaec98d, 0x3a975c0b, 0x3a83126e, 0x3a6301e3, 0x3a44948a, 0x3a2a3b44, 0x3a136a14, 0x39ff4fac, 0x39dd1722,
    0x39bf74d6, 0x39a5cb60, 0x398f9275, 0x3978a80d, 0x395753e2, 0x393a7753, 0x39217918, 0x390bd46d, 0x38f22cdd]


WEIGHTS = ["x", "w_in", "cmp_k_w1", "cmp_k_w2", "cmp_v_w1", "cmp_v_w2", "w_proj_a", "w_proj_b", "w_out", "w_up",
           "w_down", "norm_final", "mem_2", "w_in_2", "ssd_dt_bias_2", "ssd_A_log_2", "ssd_D_2", "gla_w_a2_2",
           "w_up_ssd_2", "w_up_gla_2", "w_o_2", "w_xq_2", "w_xkv_2", "w_xo_2", "w_ffn_in_2", "w_ffn_out_2",
           "norm_final_2"]


def kernel(**inputs):
    import concourse.bacc as bacc
    from concourse.bass_utils import run_bass_kernel_spmd

    get = {n: np.asarray(v) for n, v in inputs.items()}

    def by_column(v):
        return v.reshape(-1, P).T

    cols = {n: by_column(get[n]) for n in ("norm_mix", "norm_mlp", "norm_mix_2", "ssd_norm_2", "gla_norm_2",
                                            "norm_xattn_2", "norm_mem_2", "norm_ffn_2")}
    cols["conv_w"] = get["ssd_conv_w_2"].reshape(4, 12, P).transpose(2, 1, 0).reshape(P, 48)
    cols["conv_b"] = by_column(get["ssd_conv_b_2"])
    cols["gla_b"] = by_column(get["gla_b_a_2"])
    cols["pe_k"] = by_column(get["cmp_pos_k"])
    cols["pe_v"] = by_column(get["cmp_pos_v"])
    arrays = {n: np.ascontiguousarray(get[n]) for n in WEIGHTS}
    arrays["cols"] = np.ascontiguousarray(np.concatenate([cols[n] for n in COLS], 1))
    arrays["pos"] = np.ascontiguousarray(get["positions"].reshape(2, P).T)
    arrays["consts"] = shape_constants()

    nc = bacc.Bacc("TRN2", target_bir_lowering=False, num_devices=1)
    aps = {n: nc.dram_tensor(f"in_{n}", v.shape, mybir.dt.from_np(v.dtype), kind="ExternalInput").ap()
           for n, v in arrays.items()}
    out = nc.dram_tensor("out_0", (1, 256, D), F32, kind="ExternalOutput").ap()
    build(nc, aps, out)
    r = run_bass_kernel_spmd(nc, [{f"in_{n}": v for n, v in arrays.items()}], core_ids=[0])
    return r.results[0]["out_0"]
```

```python
import math
from contextlib import ExitStack

import numpy as np

import concourse.bass as bass
import concourse.mybir as mybir

F32 = mybir.dt.float32
F32R = mybir.dt.float32r
I32 = mybir.dt.int32
ALU = mybir.AluOpType
ACT = mybir.ActivationFunctionType
AX = mybir.AxisListType
P = 128
D = 1024
EPS = 1e-6
NEG = -1e30
RAW = 4
PARTS = 5
TILE = 1024
ROOM = 28400

CONSTS = dict(upper=128, after=128, causal=128, cmask=30, crow=2, decay=1024, inv=72, keep=256)
COLS = dict(norm_mix=8, norm_mlp=8, norm_mix_2=8, ssd_norm_2=8, gla_norm_2=2, norm_xattn_2=8, norm_mem_2=8,
            norm_ffn_2=8, conv_w=48, conv_b=12, gla_b=4, pe_k=16, pe_v=16)
ROWS = dict(norm_final=1024, norm_final_2=1024, ssd_dt_bias_2=16, ssd_A_log_2=16, ssd_D_2=16)
LOADS = ("x0", "x1", "ident", "consts", "cols", "rows", "pos", "w2k", "w2v", "wa2", "mem", "out")


def offsets(sizes):
    at, out = 0, {}
    for name, n in sizes.items():
        out[name] = (at, n)
        at += n
    return out, at


class Queue:

    def __init__(self, sem, serial=False):
        self.sem, self.n, self.todo, self.seen, self.serial = sem, 0, [], {}, serial

    def wait(self, *tokens):
        for t in tokens:
            if isinstance(t, list):
                self.wait(*t)
            elif t is not None:
                sem, n = t
                if self.seen.get(id(sem), 0) < n:
                    self.seen[id(sem)] = n
                    self.todo.append(lambda e, sem=sem, n=n: e.wait_ge(sem, n))

    def do(self, fn, *waits):
        self.wait(*waits)
        if self.serial and self.n:
            self.wait((self.sem, self.n))
        self.n += 1
        self.todo.append(lambda e: fn(e).then_inc(self.sem, 1))
        return (self.sem, self.n)

    def part(self, fn, *waits):
        self.wait(*waits)
        self.todo.append(fn)

    def dma(self, sem, at, out, in_, *waits):
        self.wait(*waits)
        self.todo.append(lambda e: e.dma_start(out, in_).then_inc(sem, 16))
        return (sem, at)


def build(nc, a, out):
    with ExitStack() as ctx:
        m = {}
        for name, shape, dt in (
                ("raws", [P, RAW, TILE], F32), ("parts", [P, PARTS, 2, TILE], F32R),
                ("consts", [P, offsets(CONSTS)[1]], F32), ("cols", [P, offsets(COLS)[1]], F32),
                ("rows", [P, offsets(ROWS)[1]], F32), ("posi", [P, 2], I32), ("x", [P, 2, D], F32),
                ("big", [P, 2, D], F32), ("w2k", [P, 2, 2, 64], F32), ("w2v", [P, 2, 64], F32), ("wa2", [16, 512], F32),
                ("ident", [P, P], F32), ("junk", [P, D], F32), ("half", [P, 16], F32), ("ssq", [P, 256], F32)):
            m[name] = ctx.enter_context(nc.sbuf_tensor(name, shape, dt))
        with nc.sbuf_tensor("room", [P, ROOM], F32) as m["room"]:
            pass
        m["room_r"] = ctx.enter_context(nc.sbuf_tensor("room_r", [P, ROOM], F32R))
        m["ps"] = ctx.enter_context(nc.psum_tensor("ps", [P, 8, 512], F32))
        for name in ("pe", "act", "dve", "pool", "sp", *LOADS, *(f"w{i}" for i in range(RAW))):
            m["s_" + name] = ctx.enter_context(nc.semaphore("s_" + name))
        plan = record(a, out, m, None)[1]
        queues = record(a, out, m, plan)[0]
        block = ctx.enter_context(nc.Block())
        for engine, q in zip((block.tensor, block.scalar, block.vector, block.gpsimd, block.sync), queues):
            def emit(e, q=q):
                for f in q.todo:
                    f(e)
            engine(emit)


def record(a, out, m, plan):
    pe, sp = Queue(m["s_pe"]), Queue(m["s_sp"])
    act, dve, pool = (Queue(m[f"s_{n}"], serial=True) for n in ("act", "dve", "pool"))
    raws, parts, psum, x, big, ident = (m[n] for n in ("raws", "parts", "ps", "x", "big", "ident"))
    w2k, w2v, wa2, half, ssq, junk = (m[n] for n in ("w2k", "w2v", "wa2", "half", "ssq", "junk"))

    def table(name, sizes):
        at, _ = offsets(sizes)
        return lambda n: m[name][:, at[n][0]:at[n][0] + at[n][1]]

    const, col, row = table("consts", CONSTS), table("cols", COLS), table("rows", ROWS)
    ident = ident[:, :]

    def f32(at, n):
        return m["room"][:, at:at + n]

    def pair(at, chunks):
        return [m["room_r"][:, at + i * 256 * chunks:at + (i + 1) * 256 * chunks]
                .rearrange("p (c n) -> p c n", c=chunks) for i in range(2)]

    xin = a["x"].rearrange("b (t p) d -> p (b t) d", p=P)
    in_x = [act.dma(m["s_x0"], 16, x[:, 0, :], xin[:, 0, :]), None]
    in_ident = act.dma(m["s_ident"], 16, m["ident"][:, :], a["ident"])
    in_x[1] = act.dma(m["s_x1"], 16, x[:, 1, :], xin[:, 1, :])
    in_cols = act.dma(m["s_cols"], 16, m["cols"][:, :], a["cols"])
    in_pos = act.dma(m["s_pos"], 16, m["posi"][:, :], a["pos"])
    in_consts = act.dma(m["s_consts"], 16, m["consts"][:, :], a["consts"])
    for h in range(2):
        in_w2k = pool.dma(m["s_w2k"], 16 * (h + 1), w2k[:, :, h, :], a["cmp_k_w2"][0].rearrange("(c p) n -> p c n", p=P))
    in_w2v = pool.dma(m["s_w2v"], 16, w2v[:, :, :], a["cmp_v_w2"][0].rearrange("(c p) n -> p c n", p=P))
    in_wa2 = pool.dma(m["s_wa2"], 16, wa2[:, :], a["gla_w_a2_2"][0])
    n = 0
    for name in ROWS:
        n += 16
        src = a[name] if name.startswith("norm_final") else a[name][0]
        in_rows = pool.dma(m["s_rows"], n, row(name), src.partition_broadcast(P))

    bank_free = [(b, None) for b in range(8)]

    def bank():
        return bank_free.pop(0)

    def give(b, token):
        bank_free.append((b, token))

    wanted = []
    raw_free = [None] * RAW
    part_free = [None] * PARTS
    raw_busy, part_busy = [False] * RAW, [False] * PARTS
    n_parts = [0]
    loaded, divided = [], []

    def load_ahead():
        while len(loaded) < len(plan) and not raw_busy[len(loaded) % RAW]:
            i = len(loaded)
            src, k, n, _ = plan[i]
            s = i % RAW
            raw_busy[s] = True
            view = raws[:, s, 0:k * n].rearrange("p (k n) -> p k n", k=k)
            token = sp.dma(m[f"s_w{s}"], 16 * (i // RAW + 1), view, src.rearrange("(k p) n -> p k n", p=P), raw_free[s])
            loaded.append((view, token))

    def divide_ahead():
        while len(divided) < len(plan):
            load_ahead()
            i = len(divided)
            if i == len(loaded):
                return
            _, k, n, whole = plan[i]
            view, token = loaded[i]
            if whole:
                divided.append((view, None, token, i % RAW))
                continue
            p = n_parts[0] % PARTS
            if part_busy[p]:
                return
            part_busy[p] = True
            n_parts[0] += 1
            h, l = (parts[:, p, j, 0:k * n].rearrange("p (k n) -> p k n", k=k) for j in range(2))
            kl = divide(view, h, l, token, part_free[p])
            raw_free[i % RAW] = kl
            raw_busy[i % RAW] = False
            divided.append((h, l, kl, p))

    def weight(src, k, n, whole=False):
        if plan:
            divide_ahead()
            got = divided[len(wanted)]
        else:
            got = (raws[:, 0, 0:k * n].rearrange("p (k n) -> p k n", k=k),
                   parts[:, 0, 1, 0:k * n].rearrange("p (k n) -> p k n", k=k), None, 0)
        wanted.append((src, k, n, whole))
        return got

    def used(tile, token):
        if tile[1] is None:
            raw_free[tile[3]] = token
            raw_busy[tile[3]] = False
        else:
            part_free[tile[3]] = token
            part_busy[tile[3]] = False

    def mm(ps, lhsT, rhs, start, stop):
        return lambda e: e.matmul(ps, lhsT, rhs, start=start, stop=stop)

    def group(ps, pairs, *waits):
        pe.wait(*waits)
        for i, (l, r) in enumerate(pairs):
            f = mm(ps, l, r, i == 0, i == len(pairs) - 1)
            if i == len(pairs) - 1:
                return pe.do(f)
            pe.part(f)

    def fm(w, c0, cn, hT, ready, evac):
        K = w.shape[0] // P
        for q0 in range(0, cn, 256):
            nb = min(256, cn - q0)
            tiles = [weight(w[k0 * P:(k0 + 4) * P, c0 + q0:c0 + q0 + nb], 4, nb) for k0 in range(0, K, 4)]
            b, free = bank()
            pe.wait(ready, free)
            for s in range(0, nb, P):
                ps = psum[:, b, 2 * s:2 * s + 256]
                for k in range(K):
                    wh, wl, tok, _ = tiles[k // 4]
                    pe.wait(tok)
                    wh, wl = (v[:, k % 4, s:s + P] for v in (wh, wl))
                    pe.part(mm(ps, wh, hT[0][:, k, :], k == 0, False))
                    pe.part(mm(ps, wh, hT[1][:, k, :], False, False))
                    f = mm(ps, wl, hT[0][:, k, :], False, k == K - 1)
                    if k % 4 == 3:
                        t = pe.do(f)
                        if s + P >= nb:
                            used(tiles[k // 4], t)
                    else:
                        pe.part(f)
            v = psum[:, b, 0:512].rearrange("p (s n) -> p s n", s=2)
            give(b, evac(q0 // 256, v[:, 0:nb // P, :], t))
            yield

    def tm(w, c0, cn, hT, ready, evac):
        K = w.shape[0] // P
        for b0 in range(0, cn, 512):
            nb = min(512, cn - b0)
            banks = [bank(), bank()]
            pe.wait(ready, banks[0][1], banks[1][1])
            for k0 in range(0, K, 2):
                tile = weight(w[k0 * P:(k0 + 2) * P, c0 + b0:c0 + b0 + nb], 2, nb)
                wh, wl, tok, _ = tile
                pe.wait(tok)
                done = [None, None]
                for t in range(2):
                    ps = psum[:, banks[t][0], 0:nb]
                    c = slice(t * P, t * P + P)
                    for k in range(k0, k0 + 2):
                        pe.part(mm(ps, hT[0][:, k, c], wh[:, k - k0, :], k == 0, False))
                        pe.part(mm(ps, hT[0][:, k, c], wl[:, k - k0, :], False, False))
                        f = mm(ps, hT[1][:, k, c], wh[:, k - k0, :], False, k == K - 1)
                        if k == k0 + 1:
                            done[t] = pe.do(f)
                        else:
                            pe.part(f)
                used(tile, done[1])
                if k0 + 2 == K:
                    for t in range(2):
                        give(banks[t][0], evac(b0 // 512, t, psum[:, banks[t][0], 0:nb], done[t]))
                if k0 % 4 == 2:
                    yield

    def run(*gens):
        for g in gens:
            for _ in g:
                pass

    def chain(*gens):
        for g in gens:
            yield from g

    fill = [iter(())]

    def step(n=1):
        for _ in range(n):
            next(fill[0], None)

    def transposes(ps, ins, *waits):
        pe.wait(*waits)
        for i, v in enumerate(ins):
            f = (lambda e, i=i, v=v: e.transpose(ps[0:v.shape[1], i * P:(i + 1) * P], v, ident))
            if i == len(ins) - 1:
                return pe.do(f)
            pe.part(f)

    def copy_act(o, i, *waits):
        return act.do(lambda e: e.activation(o, i, ACT.Copy), *waits)

    def copy_dve(o, i, *waits):
        return dve.do(lambda e: e.tensor_copy(o, i), *waits)

    def tt(q, o, a0, a1, op, *waits):
        return q.do(lambda e: e.tensor_tensor(o, a0, a1, op), *waits)

    def ts(q, o, i, s1, s2, op0, op1, *waits):
        if op1 is None:
            return q.do(lambda e: e.tensor_scalar(o, i, s1, None, op0), *waits)
        return q.do(lambda e: e.tensor_scalar(o, i, s1, s2, op0, op1), *waits)

    def stt(o, i, s, i1, op0, op1, *waits):
        return dve.do(lambda e: e.scalar_tensor_tensor(out=o, in0=i, scalar=s, in1=i1, op0=op0, op1=op1), *waits)

    def fn(o, i, f, *waits, **kw):
        return act.do(lambda e: e.activation(o, i, f, **kw), *waits)

    def bc(v, axis, shape):
        return v.unsqueeze(axis).to_broadcast(shape)

    def divide(v, h, l, *waits):
        k = copy_act(h, v, *waits)
        return tt(dve, l, v, h.bitcast(F32), ALU.subtract, k)

    k_half = pool.do(lambda e: e.memset(half[:, :], -0.5))
    nstat = [0]

    def stat(n):
        nstat[0] += n
        assert nstat[0] <= 256
        return ssq[:, nstat[0] - n:nstat[0]]

    def rsqrt_mean(o, ss, count, *waits):
        n = ss.shape[-1]
        k = pool.do(lambda e: e.tensor_scalar(o, ss, 1.0 / count, EPS, ALU.mult, ALU.add), *waits)
        return pool.do(lambda e: e.tensor_tensor(o, o, half[:, 0:n], ALU.pow), k, k_half)

    def sum_sq(o, i, *waits):
        return fn(junk[:, 0:i.shape[-1]], i, ACT.Square, *waits, accum_out=o)

    def gain_T(src, dst, c0, t, gain, *waits):
        b, free = bank()
        k = transposes(psum[:, b, :], [src[:, j * P:(j + 1) * P] for j in range(4)], *waits, free, in_ident)
        v = src.rearrange("p (j n) -> p j n", j=4)
        g = gain
        if len(g.shape) == 4:
            k = tt(dve, src.rearrange("p (i j n) -> p i j n", i=2, j=2),
                   psum[:, b, :].rearrange("p (i j n) -> p i j n", i=2, j=2), g, ALU.mult, k, in_cols)
        else:
            k = tt(dve, v, psum[:, b, :].rearrange("p (j n) -> p j n", j=4), g, ALU.mult, k, in_cols)
        give(b, k)
        return divide(v, dst[0][:, c0:c0 + 4, t * P:t * P + P], dst[1][:, c0:c0 + 4, t * P:t * P + P], k)

    def norm_T(src, ready, gain, dst, after=None):
        rs = []
        for t in range(2):
            ss, r = stat(1), stat(1)
            k = sum_sq(ss, src(t), ready[t])
            rs.append((r, rsqrt_mean(r, ss, D, k)))
        for t in range(2):
            r, k = rs[t]
            for q in range(2):
                c = slice(512 * q, 512 * q + 512)
                k2 = ts(dve, big[:, t, c], src(t)[:, c], r, None, ALU.mult, None, k, ready[t], after)
                k3 = gain_T(big[:, t, c], dst, 4 * q, t, bc(gain[:, 4 * q:4 * q + 4], 2, [P, 4, P]), k2)
        return k3

    xT = pair(0, 8)
    at = [8192]

    def take(n):
        at[0] += n
        assert at[0] <= ROOM, at[0]
        return f32(at[0] - n, n)

    h_ready = norm_T(lambda t: x[:, t, :], in_x, col("norm_mix"), xT)

    tmp_all = take(2048)
    tmp = [tmp_all[:, 512 * i:512 * i + 512] for i in range(4)]
    ang = take(144).rearrange("p (t f) -> p t f", t=2)
    posf = take(2)
    C1 = 6.28125
    C2 = float(np.float32(np.round((2 * math.pi - C1) * 2.0 ** 18) / 2.0 ** 18))
    C3 = float(np.float32(2 * math.pi - C1 - C2))
    MAGIC = 1.5 * 2.0 ** 23
    TOP = 3.1415925
    k = copy_dve(posf, m["posi"][:, :], in_pos)
    for t in range(2):
        kang = ts(dve, ang[:, t, :], const("inv"), posf[:, t:t + 1], None, ALU.mult, None, k, in_consts)
    trig = []
    for name, quarter in (("sin", 0.0), ("cos", 0.25)):
        turns, red = (tmp[i][:, 0:144].rearrange("p (t f) -> p t f", t=2) for i in range(2))
        tab = take(144).rearrange("p (t f) -> p t f", t=2)
        k = ts(dve, turns, ang, 1 / (2 * math.pi), quarter, ALU.mult, ALU.add, kang)
        k = ts(dve, turns, turns, MAGIC, None, ALU.add, None, k)
        k = ts(dve, turns, turns, MAGIC, None, ALU.subtract, None, k)
        k = stt(red, turns, -C1, ang, ALU.mult, ALU.add, k)
        k = stt(red, turns, -C2, red, ALU.mult, ALU.add, k)
        k = stt(red, turns, -C3, red, ALU.mult, ALU.add, k)
        if quarter:
            k = ts(dve, red, red, math.pi / 2, None, ALU.add, None, k)
        k = ts(dve, red, red, TOP, -TOP, ALU.min, ALU.max, k)
        ktrig = fn(tab, red, ACT.Sin, k)
        dve.wait(ktrig)
        trig.append(tab)
    sin, cos = trig

    w_in = a["w_in"][0]
    qkv = take(2 * 1304).rearrange("p (t n) -> p t n", t=2)
    kq = {}

    def to_qkv(blk, t, ps, tok):
        kq[t] = copy_act(qkv[:, t, 512 * blk:512 * blk + ps.shape[-1]], ps, tok)
        return kq[t]

    run(tm(w_in, 0, 1304, xT, h_ready, to_qkv))
    k_qkv = kq[1]

    def rotate(o1, o2, i1, i2, c, s, shape, *waits):
        n = int(np.prod(shape[1:]))
        names = " ".join("abc"[:len(shape) - 1])
        v = [z[:, 0:n].rearrange(f"p ({names}) -> p {names}", **dict(zip("abc", shape[1:]))) for z in tmp]
        dve.wait(*waits, ktrig)
        tt(dve, v[0], i1, c, ALU.mult)
        tt(dve, v[1], i2, s, ALU.mult)
        tt(dve, v[2], i1, s, ALU.mult)
        k = tt(dve, v[3], i2, c, ALU.mult)
        tt(dve, o1, v[0], v[1], ALU.subtract, k)
        return tt(dve, o2, v[2], v[3], ALU.add, k)

    heads = qkv[:, :, 0:1280].rearrange("p t (h d) -> p t h d", d=64)
    for t in range(2):
        c, s = cos[:, t, 0:8], sin[:, t, 0:8]
        q1, q2 = heads[:, t, 0:8, 0:8], heads[:, t, 0:8, 8:16]
        k_rot = rotate(q1, q2, q1, q2, bc(c, 1, [P, 8, 8]), bc(s, 1, [P, 8, 8]), [P, 8, 8], k_qkv)
        for h in (8, 12, 16):
            q1, q2 = heads[:, t, h:h + 2, 0:8], heads[:, t, h:h + 2, 8:16]
            k_rot = rotate(q1, q2, q1, q2, bc(c, 1, [P, 2, 8]), bc(s, 1, [P, 2, 8]), [P, 2, 8], k_qkv, k_rot)

    rqk_all = take(2048)
    rq, rk = (rqk_all[:, i:i + 1024].rearrange("p (t n) -> p t n", t=2) for i in (0, 1024))
    rv, rg = (take(1024).rearrange("p (t n) -> p t n", t=2) for _ in range(2))
    kr = {}

    def to_rot(dst, name):
        def evac(blk, t, ps, tok):
            v = ps.rearrange("p (h s d) -> p h s d", h=4, s=2)
            o = dst[:, t, :].rearrange("p (h s d) -> p h s d", h=4, s=2)
            kr[name] = rotate(o[:, :, 0, :], o[:, :, 1, :], v[:, :, 0, :], v[:, :, 1, :],
                              bc(cos[:, t, 8:72], 1, [P, 4, 64]), bc(sin[:, t, 8:72], 1, [P, 4, 64]),
                              [P, 4, 64], tok, kr.get(name))
            return kr[name]
        return evac

    def keep_tm(dst, keep, name, f):
        def evac(blk, t, ps, tok):
            keep[name] = fn(dst[:, t, 512 * blk:512 * blk + 512], ps, f, tok)
            return keep[name]
        return evac

    def keep_fm(dst, keep, name, f=ACT.Copy):
        def evac(q, ps, tok):
            keep[name] = keep[name, q] = fn(dst[:, 2 * q:2 * q + 2, :], ps, f, tok)
            return keep[name]
        return evac

    sig = take(4096).rearrange("p (c n) -> p c n", c=16)
    k_sig = {}
    gsig = take(48).rearrange("p (t h b) -> p t h b", t=2, h=8)
    for t in range(2):
        k_gsig = fn(gsig[:, t, :, :], qkv[:, t, 1280:1304].rearrange("p (h b) -> p h b", b=3), ACT.Sigmoid, k_qkv)
    fill[0] = chain(tm(w_in, 1304, 512, xT, h_ready, to_rot(rq, "rq")), tm(w_in, 1816, 512, xT, h_ready, to_rot(rk, "rk")),
                    tm(w_in, 2328, 512, xT, h_ready, keep_tm(rv, kr, "rv", ACT.Copy)),
                    tm(w_in, 2840, 512, xT, h_ready, keep_tm(rg, kr, "rg", ACT.Silu)),
                    fm(w_in, 3352, 2048, xT, h_ready, keep_fm(sig, k_sig, "g", ACT.Sigmoid)))
    step(4)

    qT = take(1024).rearrange("p (c n) -> p c n", c=4)
    kT = take(1024).rearrange("p (b g n) -> p b g n", b=2, g=2)
    for t in range(2):
        b, free = bank()
        k = transposes(psum[:, b, :], [qkv[:, t, P * c:P * c + P] for c in range(4)], k_rot, free, in_ident)
        k_qT = copy_act(qT[:, :, t * P:t * P + P], psum[:, b, :].rearrange("p (c n) -> p c n", c=4), k)
        give(b, k_qT)

    dups = [take(256).rearrange("p (g r d) -> p g r d", g=2, r=2) for _ in range(2)]
    dup_free = [None, None]

    def twice_T(h, ready):
        b, free = bank()
        for t in range(2):
            o = dups[t]
            for r in range(2):
                k = copy_dve(o[:, :, r, :], heads[:, t, h:h + 2, :], ready, dup_free[t])
            pe.wait(k, free)
            for g in range(2):
                f = (lambda e, g=g, t=t, o=o: e.transpose(psum[:, b, (2 * g + t) * P:(2 * g + t + 1) * P],
                                                          o[:, g, :, :].rearrange("p r d -> p (r d)"), ident))
                k = pe.do(f)
            dup_free[t] = k
        return b, k

    for br, h in ((0, 12), (1, 16)):
        b, k = twice_T(h, k_rot)
        k_kT = copy_act(kT[:, br, :, :], psum[:, b, :].rearrange("p (g n) -> p g n", g=2), k)
        give(b, k_kT)

    def windows(h, pe_col, ready):
        A, B = take(256), take(480).rearrange("p (j c) -> p j c", j=16)
        b, k = twice_T(h, ready)
        for r in range(2):
            half_ = slice(64 * r, 64 * r + 64)
            k2 = copy_act(A[half_, :], psum[half_, b, r::2], k)
        give(b, k2)
        src = bass.AP(A.tensor, A.offset, [list(A.ap[0]), [1, 16], [128, 2], [8, 15]])
        return B, tt(dve, B.rearrange("p j (g c) -> p j g c", g=2), src,
                     pe_col.unsqueeze(2).unsqueeze(3).to_broadcast([P, 16, 2, 15]), ALU.add, k2, in_cols)

    def hidden(w1, B, ready):
        h1 = take(60).rearrange("p (s c) -> p s c", s=2)
        b, free = bank()
        b2, free2 = bank()
        pe.wait(ready, free, free2)
        for j0 in range(0, 16, 4):
            tile = weight(w1[j0 * P:(j0 + 4) * P, :], 4, 256, whole=True)
            pe.wait(tile[2])
            for s, bb in ((0, b), (1, b2)):
                for j in range(j0, j0 + 4):
                    f = mm(psum[:, bb, 0:30], tile[0][:, j - j0, s * P:s * P + P], B[:, j, :], j == 0, j == 15)
                    if (s, j) == (1, j0 + 3):
                        t = pe.do(f)
                    else:
                        pe.part(f)
            used(tile, t)
        fn(h1[:, 0, :], psum[:, b, 0:30], ACT.Silu, t)
        k = fn(h1[:, 1, :], psum[:, b2, 0:30], ACT.Silu, t)
        give(b, k)
        give(b2, k)
        return h1, k

    Bk, k_Bk = windows(8, col("pe_k"), k_rot)
    step()
    Bv, k_Bv = windows(10, col("pe_v"), k_qkv)
    step()
    hk, k_hk = hidden(a["cmp_k_w1"][0], Bk, k_Bk)
    step()
    hv, k_hv = hidden(a["cmp_v_w1"][0], Bv, k_Bv)
    step()
    kTc = take(30)
    vc = take(128).rearrange("p (g d) -> p g d", g=2)
    b, free = bank()
    k = group(psum[:, b, 0:30], [(w2k[:, s, :, :].rearrange("p r d -> p (r d)"), hk[:, s, :]) for s in range(2)],
              k_hk, free, in_w2k)
    k_kTc = copy_act(kTc, psum[:, b, 0:30], k)
    give(b, k_kTc)
    b, free = bank()
    for g in range(2):
        k = group(psum[0:15, b, 64 * g:64 * g + 64], [(hv[:, s, 15 * g:15 * g + 15], w2v[:, s, :]) for s in range(2)],
                  k_hv, free, in_w2v)
    k_vc = copy_act(vc[0:15, :, :], psum[0:15, b, 0:128].rearrange("p (g d) -> p g d", g=2), k)
    give(b, k_vc)
    step()

    coef = take(48).rearrange("p (t h b) -> p t h b", t=2, h=8)
    pc = take(240).rearrange("p (t h c) -> p t h c", t=2, h=8)
    pc2 = pc.rearrange("p t h c -> p (t h) c")
    mxc = take(16)
    for odd in range(2):
        b, free = bank()
        C = psum[:, b, 0:120].rearrange("p (t h c) -> p t h c", t=2, h=4)
        r = slice(64 * odd, 64 * odd + 64)
        for t in range(2):
            for i in range(4):
                g = i // 2
                k = group(C[:, t, i, :], [(qT[r, i, t * P:t * P + P], kTc[r, 15 * g:15 * g + 15])], k_qT, k_kTc, free)
        for t in range(2):
            kc_ = stt(pc[:, t, odd::2, :], C[:, t, :, :], 0.125,
                      bc(const("cmask")[:, 15 * t:15 * t + 15], 1, [P, 4, 15]), ALU.mult, ALU.add, k)
        give(b, kc_)
    step()
    k = dve.do(lambda e: e.tensor_reduce(mxc, pc2, AX.X, ALU.max), kc_)
    k = tt(dve, pc2, pc2, bc(mxc, 2, [P, 16, 15]), ALU.subtract, k)
    k_pc = fn(pc2, pc2, ACT.Exp, k)
    cf = coef.rearrange("p t h b -> p (t h) b")[:, :, 0:1]
    k = dve.do(lambda e: e.tensor_reduce(cf, pc2, AX.X, ALU.add), k_pc)
    k = dve.do(lambda e: e.reciprocal(cf, cf), k)
    k = tt(dve, cf, cf, gsig.rearrange("p t h b -> p (t h) b")[:, :, 0:1], ALU.mult, k, k_gsig)
    for t in range(2):
        k = ts(dve, coef[:, t, :, 0:1], coef[:, t, :, 0:1], const("crow")[:, t:t + 1], None, ALU.mult, None, k)
    k_pc = tt(dve, pc2, pc2, cf.to_broadcast([P, 16, 15]), ALU.mult, k)
    pcT = tmp_all[:, 0:1024].rearrange("p (h n) -> p h n", h=8)
    pT = [tmp_all[:, 1024:1536], tmp_all[:, 1536:2048]]
    pT_free = [None] * 2
    probs = [big[:, i // 2, 512 * (i % 2):512 * (i % 2) + 512] for i in range(4)]
    probs_free = [None] * 4
    nmax = take(64).rearrange("p (i b) -> p i b", b=4)
    nsaT, retT = pair(4096, 4), pair(6144, 4)

    def cmp_T(t, pv_done):
        for h0 in (0, 4):
            b, free = bank()
            k2 = transposes(psum[:, b, :], [pc[:, t, h, :] for h in range(h0, h0 + 4)], k_pc, free)
            k2 = copy_dve(pcT[0:15, h0:h0 + 4, :], psum[0:15, b, :].rearrange("p (h n) -> p h n", h=4), k2, pv_done)
            give(b, k2)
        return k2

    def scores(i):
        t, h = divmod(i, 8)
        nk = P * (t + 1)
        g, r = h // 4, slice(64 * (h % 2), 64 * (h % 2) + 64)
        b, free = bank()
        S = psum[:, b, 0:2 * nk].rearrange("p (b n) -> p b n", b=2)
        for br in range(2):
            k = group(S[:, br, :], [(qT[r, h // 2, t * P:t * P + P], kT[r, br, g, 0:nk])], k_qT, k_kT, free)
        diag_ = S[:, :, t * P:t * P + P]
        k = tt(dve, diag_, diag_, bc(const("causal"), 1, [P, 2, P]), ALU.add, k)
        mx, sm = nmax[:, i, 0:2], nmax[:, i, 2:4]
        k = dve.do(lambda e: e.tensor_reduce(mx, S, AX.X, ALU.max), k)
        k = ts(dve, mx, mx, -0.125, None, ALU.mult, None, k)
        Ph = probs[i % 4][:, 0:2 * nk].rearrange("p (b n) -> p b n", b=2)
        for br in range(2):
            k2 = fn(Ph[:, br, :], S[:, br, :], ACT.Exp, k, probs_free[i % 4], bias=mx[:, br:br + 1], scale=0.125,
                    accum_out=sm[:, br:br + 1])
        give(b, k2)
        return Ph, sm, k2

    def pv(i, Ph, sm, k, O, kcT, ofree):
        t, h = divmod(i, 8)
        nk = P * (t + 1)
        k = dve.do(lambda e: e.reciprocal(sm, sm), k)
        k = tt(dve, sm, sm, gsig[:, t, h, 1:3], ALU.mult, k, k_gsig)
        k = tt(dve, Ph, Ph, bc(sm, 2, [P, 2, nk]), ALU.mult, k)
        b, free = bank()
        parts_ = [(br, kt) for br in range(2) for kt in range(t + 1)]
        k = transposes(psum[:, b, :], [Ph[:, br, kt * P:kt * P + P] for br, kt in parts_], k, free)
        probs_free[i % 4] = k
        n = len(parts_) * P
        j = i % 2
        k = copy_act(pT[j][:, 0:n], psum[:, b, 0:n], k, pT_free[j])
        give(b, k)
        g, r = h // 4, 64 * (h % 2)
        pairs = [(vc[0:15, g, :], pcT[0:15, h, :])]
        for n, (br, kt) in enumerate(parts_):
            pairs.append((heads[:, kt, (14, 18)[br] + g, :], pT[j][:, n * P:n * P + P]))
        pT_free[j] = group(O[r:r + 64, h // 2, :], pairs, k, k_vc, kcT, ofree)
        return pT_free[j]

    def evac_pair(dst, c0, t, b, k):
        v = psum[:, b, :].rearrange("p (c n) -> p c n", c=4)
        k = divide(v, dst[0][:, c0:c0 + 4, t * P:t * P + P], dst[1][:, c0:c0 + 4, t * P:t * P + P], k)
        give(b, k)
        return k

    rqT, rkT = (take(1024).rearrange("p (h n) -> p h n", h=4) for _ in range(2))

    def turn(dst, src, name, t):
        b, free = bank()
        k = transposes(psum[:, b, :], [src[:, t, h * P:h * P + P] for h in range(4)], kr[name], free)
        k = copy_act(dst[:, :, t * P:t * P + P], psum[:, b, :].rearrange("p (h n) -> p h n", h=4), k)
        give(b, k)
        return k

    RS = rqk_all[:, 0:1536].rearrange("p (h n) -> p h n", h=4)
    decay = const("decay").rearrange("p (h n) -> p h n", h=4)
    rss, rrs = stat(8), stat(8)

    def ret_scores(h):
        b, free = bank()
        group(psum[:, b, 0:256], [(rkT[:, h, 0:P], rqT[:, h, :])], k_rT, free)
        k = group(psum[:, b, 256:384], [(rkT[:, h, P:256], rqT[:, h, P:256])])
        tt(dve, RS[:, h, 0:256], psum[:, b, 0:256], decay[:, h, :], ALU.mult, k, in_consts)
        k = tt(dve, RS[:, h, 256:384], psum[:, b, 256:384], decay[:, h, 0:P], ALU.mult)
        give(b, k)
        return k

    def ret_out(t):
        b, free = bank()
        O = psum[:, b, :].rearrange("p (h n) -> p h n", h=4)
        for h in range(4):
            pairs = [(RS[:, h, t * P:t * P + P], rv[:, 0, h * P:h * P + P])]
            if t:
                pairs.append((RS[:, h, 256:384], rv[:, 1, h * P:h * P + P]))
            k = group(O[:, h, :], pairs, k_RS, kr["rv"], free)
        for h in range(4):
            k2 = sum_sq(rss[:, 4 * t + h:4 * t + h + 1], O[:, h, :], k)
        k2 = rsqrt_mean(rrs[:, 4 * t:4 * t + 4], rss[:, 4 * t:4 * t + 4], P, k2)
        ro = rg[:, t, :].rearrange("p (h n) -> p h n", h=4)
        k = tt(dve, ro, O, ro, ALU.mult, k, kr["rg"], k2)
        give(b, k)
        return tt(dve, ro, ro, bc(rrs[:, 4 * t:4 * t + 4], 2, [P, 4, P]), ALU.mult, k)

    def ret_T(t, k):
        b, free = bank()
        k = transposes(psum[:, b, :], [rg[:, t, h * P:h * P + P] for h in range(4)], k, free)
        return evac_pair(retT, 0, t, b, k)

    done = None
    kcT = cmp_T(0, None)
    got = {}
    got[0] = scores(0)
    got[1] = scores(1)
    k_rT = [turn(rqT, rq, "rq", 0), turn(rkT, rk, "rk", 0)]
    for i in range(16):
        if i % 8 == 0:
            ob, ofree = bank()
            O = psum[:, ob, :].rearrange("p (c n) -> p c n", c=4)
            if i:
                kcT = cmp_T(1, done)
        if i + 2 < 16:
            got[i + 2] = scores(i + 2)
        if i in (1, 3, 5, 6, 8, 10, 12, 14):
            step()
        if i == 2:
            k_rT += [turn(rqT, rq, "rq", 1), turn(rkT, rk, "rk", 1)]
        if 4 <= i < 8:
            k_RS = ret_scores(i - 4)
        if i in (9, 12):
            k_ro = ret_out((i - 9) // 3)
        if i in (10, 13):
            k_retT = ret_T((i - 10) // 3, k_ro)
        done = pv(i, *got.pop(i), O, kcT, ofree)
        if i % 8 == 7:
            k_nsaT = evac_pair(nsaT, 0, i // 8, ob, done)
    step(20)

    def merge(wa, aT, ka, wb, bT, kb, sig, ksig, dst):
        got = {}

        def first(q, ps, tok):
            g = sig[:, 2 * q:2 * q + 2, :]
            got[q] = tt(dve, g, ps, g, ALU.mult, tok, ksig["g", q])
            return got[q]

        def second(q, ps, tok):
            g, f = sig[:, 8 + 2 * q:10 + 2 * q, :], sig[:, 2 * q:2 * q + 2, :]
            free = tt(dve, g, ps, g, ALU.mult, tok, ksig["g", 4 + q])
            k = tt(dve, g, g, f, ALU.add, free, got[q])
            got["k"] = divide(g, dst[0][:, 2 * q:2 * q + 2, :], dst[1][:, 2 * q:2 * q + 2, :], k)
            return free
        run(fm(wa, 0, D, aT, ka, first), fm(wb, 0, D, bT, kb, second))
        return got["k"]

    k_mix = merge(a["w_proj_a"][0], nsaT, k_nsaT, a["w_proj_b"][0], retT, k_retT, sig, k_sig, xT)
    k_x = {}

    def to_residual(blk, t, ps, tok):
        k_x[t] = tt(dve, x[:, t, blk * 512:blk * 512 + 512], ps, x[:, t, blk * 512:blk * 512 + 512], ALU.add, tok)
        return k_x[t]

    run(tm(a["w_out"][0], 0, D, xT, k_mix, to_residual))

    def mlp(pairs, up, w_down):
        bufs = [pair(4096 + 1024 * i, 2) for i in range(4)]
        banks = [bank() for _ in range(4)]
        for _, free in banks:
            pe.wait(free)
        done = [None] * 4
        ready = {}
        for q in range(pairs + 2):
            if q < pairs:
                ready[q] = up(q, bufs[q % 4], done[q % 4])
            if q < 2:
                continue
            q -= 2
            u = bufs[q % 4]
            pe.wait(ready[q])
            for h in range(2):
                tile = weight(w_down[256 * q:256 * q + 256, 512 * h:512 * h + 512], 2, 512)
                wh, wl, tok, _ = tile
                pe.wait(tok)
                for t in range(2):
                    ps = psum[:, banks[2 * h + t][0], :]
                    c = slice(t * P, t * P + P)
                    for k in range(2):
                        pe.part(mm(ps, u[0][:, k, c], wh[:, k, :], q == 0 and k == 0, False))
                        pe.part(mm(ps, u[0][:, k, c], wl[:, k, :], False, False))
                        f = mm(ps, u[1][:, k, c], wh[:, k, :], False, q == pairs - 1 and k == 1)
                        if k:
                            tok = pe.do(f)
                        else:
                            pe.part(f)
                    if q == pairs - 1:
                        b = banks[2 * h + t][0]
                        give(b, to_residual(h, t, psum[:, b, :], tok))
                used(tile, tok)
            done[q % 4] = tok

    h_ready = norm_T(lambda t: x[:, t, :], [k_x[0], k_x[1]], col("norm_mlp"), xT)
    tmps = [f32(8192 + 512 * i, 512).rearrange("p (c n) -> p c n", c=2) for i in range(4)]
    gens = fm(a["w_up"][0], 0, 4096, xT, h_ready, lambda q, ps, tok: up_evac(q, ps, tok))
    state = {}

    def up_evac(q, ps, tok):
        r = tmps[q % 4]
        k = fn(r, ps, ACT.Relu, tok)
        k = stt(r, ps, 0.0, r, ALU.max, ALU.mult, k)
        dst, free = state["dst"]
        state["k"] = divide(r, dst[0], dst[1], k, free)
        return k

    def up_relu2(q, dst, free):
        state["dst"] = dst, free
        next(gens)
        return state["k"]

    mlp(16, up_relu2, a["w_down"][0])

    def last_norm(name):
        out_ = []
        for t in range(2):
            ss, r = stat(1), stat(1)
            k = sum_sq(ss, x[:, t, :], k_x[t])
            k = rsqrt_mean(r, ss, D, k)
            out_.append(stt(x[:, t, :], x[:, t, :], r, row(name), ALU.mult, ALU.mult, k, k_x[t], in_rows))
        return out_
    k_y = last_norm("norm_final")
    at[0] = 8192
    w2 = a["w_in_2"][0]
    h_ready = norm_T(lambda t: x[:, t, :], k_y, col("norm_mix_2"), xT)
    raw = take(3108).rearrange("p (c n) -> p c n", c=12)
    cv = take(3072).rearrange("p (c n) -> p c n", c=12)
    k_pad = pool.do(lambda e: e.memset(raw[:, :, 0:3], 0.0), h_ready)
    cw = col("conv_w").rearrange("p (c k) -> p c k", k=4)
    k_cv = {}

    def to_conv(q, ps, tok):
        c = 2 * q
        k = copy_act(raw[:, c:c + 2, 3:259], ps, tok)
        dve.wait(k, k_pad)
        for i in (c, c + 1):
            ts(dve, cv[:, i, :], raw[:, i, 0:256], cw[:, i, 0:1], col("conv_b")[:, i:i + 1], ALU.mult, ALU.add)
            for j in range(1, 4):
                k2 = stt(cv[:, i, :], raw[:, i, j:j + 256], cw[:, i, j:j + 1], cv[:, i, :], ALU.mult, ALU.add)
        k_cv[q] = fn(cv[:, c:c + 2, :], cv[:, c:c + 2, :], ACT.Silu, k2)
        return k

    run(fm(w2, 1024, 1536, xT, h_ready, to_conv))

    small = take(256)
    dt_, e_, s_, s2_, p_, aa = (small[:, 32 * i:32 * i + 32] for i in range(6))
    Aexp, e1, d0 = (small[:, 192 + 16 * i:208 + 16 * i] for i in range(3))
    k_Ae = fn(Aexp, row("ssd_A_log_2"), ACT.Exp, in_rows, h_ready)
    kdt = {}

    def to_dt(blk, t, ps, tok):
        kdt[t] = tt(dve, dt_[:, 16 * t:16 * t + 16], ps, row("ssd_dt_bias_2"), ALU.add, tok)
        return kdt[t]

    run(tm(w2, 2560, 16, xT, h_ready, to_dt))
    k = stt(e_, dt_, -1.0, dt_, ALU.mult, ALU.min, kdt[1])
    k = fn(e_, e_, ACT.Exp, k)
    k = ts(dve, s_, e_, 2.0, None, ALU.add, None, k)
    k = dve.do(lambda e: e.reciprocal(s_, s_), k)
    k = tt(dve, s_, s_, e_, ALU.mult, k)
    k = tt(dve, s2_, s_, s_, ALU.mult, k)
    k = ts(dve, p_, s2_, 1 / 17, None, ALU.mult, None, k)
    for c in (15, 13, 11, 9, 7, 5, 3):
        k = stt(p_, p_, 1 / c, s2_, ALU.add, ALU.mult, k)
    k = stt(p_, p_, 1.0, s_, ALU.add, ALU.mult, k)
    k = ts(dve, p_, p_, 2.0, None, ALU.mult, None, k)
    k_dt = stt(dt_, dt_, 0.0, p_, ALU.max, ALU.add, k)
    dt3 = dt_.rearrange("p (t h) -> p t h", t=2)
    a3 = aa.rearrange("p (t h) -> p t h", t=2)
    k_a = stt(a3, dt3, -1.0, bc(Aexp, 1, [P, 2, 16]), ALU.mult, ALU.mult, k_dt, k_Ae)
    upper, after = const("upper"), const("after")
    b, free = bank()
    group(psum[:, b, 0:16], [(upper, a3[:, 1, :])], k_a, free)
    k = group(psum[:, b, 16:32], [(after, a3[:, 0, :])])
    fn(e1, psum[:, b, 0:16], ACT.Exp, k)
    k_dec = fn(d0, psum[:, b, 16:32], ACT.Exp, k)
    give(b, k_dec)

    flat = {}
    flat["zs"] = take(2048)
    zs = flat["zs"].rearrange("p (t n) -> p t n", t=2)
    gq = take(1024).rearrange("p (h n) -> p h n", h=4)
    flat["gk"] = take(1024)
    gk = flat["gk"].rearrange("p (h n) -> p h n", h=4)
    flat["gv"] = at[0]
    gv = take(2048).rearrange("p (t n) -> p t n", t=2)
    a1T = take(256)
    kg = {}

    def keep_a1(q, ps, tok):
        kg["a1"] = copy_act(a1T[0:16, :], ps[0:16, 0, :], tok)
        return kg["a1"]

    fill[0] = chain(tm(w2, 0, 1024, xT, h_ready, keep_tm(zs, kg, "z", ACT.Silu)),
                    fm(w2, 2576, 512, xT, h_ready, keep_fm(gq, kg, "q")),
                    fm(w2, 3088, 512, xT, h_ready, keep_fm(gk, kg, "k")),
                    fm(w2, 5648, 128, xT, h_ready, keep_a1),
                    tm(w2, 3600, 1024, xT, h_ready, keep_tm(gv, kg, "v", ACT.Copy)))

    flat["xs"] = take(2048)
    flat["sig"] = at[0] - 1024
    xs = flat["xs"].rearrange("p (t n) -> p t n", t=2)
    X = take(2048).rearrange("p (t n) -> p t n", t=2)
    Xd = take(1024)
    flat["CB"] = take(768)
    CB = flat["CB"].rearrange("p (g n) -> p g n", g=2)
    step()
    for t in range(2):
        for q in range(2):
            b, free = bank()
            k = transposes(psum[:, b, :], [cv[:, 4 * q + j, t * P:t * P + P] for j in range(4)],
                           k_cv[2 * q], k_cv[2 * q + 1], free)
            k_xs = copy_act(xs[:, t, 512 * q:512 * q + 512], psum[:, b, :], k)
            give(b, k_xs)
        k_X = tt(dve, X[:, t, :].rearrange("p (h d) -> p h d", h=16), xs[:, t, :].rearrange("p (h d) -> p h d", h=16),
                 bc(dt3[:, t, :], 2, [P, 16, 64]), ALU.mult, k_xs, k_dt)
    k_Xd = tt(dve, Xd.rearrange("p (h d) -> p h d", h=16), X[:, 0, :].rearrange("p (h d) -> p h d", h=16),
              bc(d0, 2, [P, 16, 64]), ALU.mult, k_X, k_dec)
    for g in range(2):
        b, free = bank()
        group(psum[:, b, 0:256], [(cv[:, 8 + g, 0:P], cv[:, 10 + g, :])], k_cv[4], k_cv[5], free)
        k = group(psum[:, b, 256:384], [(cv[:, 8 + g, P:256], cv[:, 10 + g, P:256])])
        v = psum[:, b, 0:384]
        dve.wait(k)
        tt(dve, CB[:, g, 0:P], v[:, 0:P], upper, ALU.mult)
        tt(dve, CB[:, g, 256:384], v[:, 256:384], upper, ALU.mult)
        k_CB = copy_dve(CB[:, g, P:256], v[:, P:256])
        give(b, k_CB)

    rot = [raw.rearrange("p c n -> p (c n)")[:, 512 * i:512 * i + 512].rearrange("p (h n) -> p h n", h=4)
           for i in range(6)]
    La, E = rot[0:3], rot[3:6]
    k_La, k_E, E_free, La_free = {}, {}, [None] * 3, [None] * 3
    quads = [(t, q) for t in range(2) for q in range(4)]

    def seg(i):
        t, q = quads[i]
        v = La[i % 3]
        k = tt(dve, v, bc(after, 1, [P, 4, P]), bc(a3[:, t, 4 * q:4 * q + 4], 2, [P, 4, P]), ALU.mult,
               k_a, La_free[i % 3])
        b, free = bank()
        for h in range(4):
            k = group(psum[:, b, h * P:h * P + P], [(v[:, h, :], upper)], k, free)
        La_free[i % 3] = k
        o = E[i % 3]
        k = fn(o, psum[:, b, :].rearrange("p (h n) -> p h n", h=4), ACT.Exp, k, E_free[i % 3])
        give(b, k)
        k_E[i] = tt(dve, o, o, bc(CB[:, q // 2, 256 * t:256 * t + P], 1, [P, 4, P]), ALU.mult, k, k_CB)

    yss, yrs = stat(4), stat(4)
    yT = pair(4096, 8)
    k_yT = None
    ybank = {}

    def diag(i):
        t, q = quads[i]
        g = q // 2
        if q % 2 == 0:
            ybank[t, g] = bank()
        b, free = ybank[t, g]
        for h in range(4):
            o = 256 * (q % 2) + 64 * h
            k = group(psum[:, b, o:o + 64], [(E[i % 3][:, h, :], X[:, t, 256 * q + 64 * h:256 * q + 64 * h + 64])],
                      k_E[i], k_X, free)
        E_free[i % 3] = k
        if q % 2 == 0:
            return
        c = slice(512 * g, 512 * g + 512)
        by_head = lambda v: v.rearrange("p (h d) -> p h d", h=8)
        Dr = bc(row("ssd_D_2")[:, 8 * g:8 * g + 8], 2, [P, 8, 64])
        y = xs[:, t, c]
        k2 = tt(dve, by_head(y), by_head(y), Dr, ALU.mult, in_rows)
        k2 = tt(dve, y, psum[:, b, :], y, ALU.add, k2, k)
        give(b, k2)
        if t:
            b, free = bank()
            k = group(psum[:, b, :], [(CB[:, g, P:256], Xd[:, c])], k_CB, k_Xd, free)
            x1 = X[:, 1, c]
            k = tt(dve, by_head(x1), by_head(psum[:, b, :]), bc(e1[:, 8 * g:8 * g + 8], 2, [P, 8, 64]), ALU.mult,
                   k, k_dec)
            give(b, k)
            k2 = tt(dve, y, y, x1, ALU.add, k, k2)
        k2 = tt(dve, y, y, zs[:, t, c], ALU.mult, k2, kg["z"])
        j = 2 * t + g
        k = sum_sq(yss[:, j:j + 1], y, k2)
        k = rsqrt_mean(yrs[:, j:j + 1], yss[:, j:j + 1], 512, k)
        k = ts(dve, y, y, yrs[:, j:j + 1], None, ALU.mult, None, k)
        k_y2[t, g] = k

    def y_out(t, g):
        y = xs[:, t, 512 * g:512 * g + 512]
        return gain_T(y, yT, 4 * g, t, bc(col("ssd_norm_2")[:, 4 * g:4 * g + 4], 2, [P, 4, P]), k_y2[t, g])

    k_y2 = {}
    seg(0)
    step()
    seg(1)
    step(2)
    for i in range(8):
        if i + 2 < 8:
            seg(i + 2)
        diag(i)
        step()
        if i in (2, 4, 6):
            k_yT = y_out(*((0, 0), (0, 1), (1, 0))[i // 2 - 1])
    step(20)
    k_yT = y_out(1, 1)

    oT = pair(8192, 8)
    gr = f32(12288, 2048).rearrange("p (t n) -> p t n", t=2)

    la, bcum = (flat["zs"][:, i:i + 1024].rearrange("p (h n) -> p h n", h=4) for i in (0, 1024))
    kt_ = la
    kh = flat["xs"][:, 0:1024].rearrange("p (h n) -> p h n", h=4)
    sig = f32(flat["sig"], 4096).rearrange("p (c n) -> p c n", c=16)
    ST = [flat["gk"][:, 0:512], flat["gk"][:, 512:1024], flat["CB"][:, 0:512]]
    ST = [v.rearrange("p (h n) -> p h n", h=4) for v in ST]
    ke, qe = (take(512).rearrange("p (h n) -> p h n", h=4) for _ in range(2))
    dec = take(16)
    tmpg = big[:, 0, :].rearrange("p (h n) -> p h n", h=4)
    k_sig = {}

    for i in range(2):
        b, free = bank()
        for s in range(2):
            h = 2 * i + s
            k = group(psum[:, b, 256 * s:256 * s + 256], [(wa2[:, h * P:h * P + P], a1T[0:16, :])],
                      kg["a1"], in_wa2, free)
        for s in range(2):
            h = 2 * i + s
            k_la = ts(dve, la[:, h, :], psum[:, b, 256 * s:256 * s + 256], col("gla_b")[:, h:h + 1], None,
                      ALU.add, None, k, k_yT)
        give(b, k_la)
    k = stt(tmpg, la, -1.0, la, ALU.mult, ALU.min, k_la)
    k = fn(tmpg, tmpg, ACT.Exp, k)
    k = fn(tmpg, tmpg, ACT.Ln, k, bias=1.0)
    k = stt(la, la, 0.0, tmpg, ALU.min, ALU.subtract, k)
    for h in range(4):
        k_b = dve.do(lambda e, h=h: e.tensor_tensor_scan(bcum[:, h, :], const("keep"), la[:, h, :], 0.0,
                                                         ALU.mult, ALU.add), k)
    k = fn(tmpg, bcum, ACT.Exp, k_b, scale=1 / 16)
    k_qt = stt(gq, gq, P ** -0.5, tmpg, ALU.mult, ALU.mult, k, kg["q"])
    k = fn(kt_, bcum, ACT.Exp, k_b, scale=-1 / 16)
    k_kt = tt(dve, kt_, kt_, gk, ALU.mult, k, kg["k"])
    by_chunk = lambda v: v.rearrange("p h (c n) -> p (h c) n", c=4)
    last = by_chunk(bcum)[:, :, 63:64]
    k = tt(dve, by_chunk(kh), last.to_broadcast([P, 16, 64]), by_chunk(bcum), ALU.subtract, k_b)
    k = fn(kh, kh, ACT.Exp, k, scale=1 / 16)
    k_kh = tt(dve, kh, kh, gk, ALU.mult, k)
    k_dec = fn(dec.unsqueeze(2), last, ACT.Exp, k_b, scale=1 / 16)
    dec3 = dec.rearrange("p (h c) -> p h c", c=4)
    dve.wait(k_dec)
    tt(dve, ke[:, :, 0:64], kh[:, :, 0:64], dec3[:, :, 1:2].to_broadcast([P, 4, 64]), ALU.mult)
    copy_dve(ke[:, :, 64:P], kh[:, :, 64:P])
    tt(dve, qe[:, :, 64:P], gq[:, :, 192:256], dec3[:, :, 2:3].to_broadcast([P, 4, 64]), ALU.mult)
    k_e2 = copy_dve(qe[:, :, 0:64], gq[:, :, P:192])

    fill[0] = chain(tm(w2, 4624, 1024, xT, h_ready, keep_tm(gr, kg, "r", ACT.Silu)),
                    fm(w2, 5664, 2048, xT, h_ready, keep_fm(sig, k_sig, "g", ACT.Sigmoid)))
    act.wait(k_yT)
    step(4)
    for t in range(2):
        b, free = bank()
        c0, c1 = 2 * t * 64, 2 * t * 64 + 64
        for h in range(4):
            o = psum[:, b, h * P:h * P + P]
            group(o[0:64, 0:64], [(kt_[:, h, c0:c1], gq[:, h, c0:c1])], k_qt, k_kt, k_kh, free)
            group(o[0:64, 64:P], [(kh[:, h, c0:c1], gq[:, h, c1:c1 + 64])])
            k = group(o[64:P, :], [(kt_[:, h, c1:c1 + 64], gq[:, h, c0:c1 + 64])])
        k_ST = tt(dve, ST[t], psum[:, b, :].rearrange("p (h n) -> p h n", h=4), bc(upper, 1, [P, 4, P]),
                  ALU.mult, k)
        give(b, k_ST)
        step()
    b, free = bank()
    for h in range(4):
        k = group(psum[:, b, h * P:h * P + P], [(ke[:, h, :], qe[:, h, :])], k_e2, free)
    k_ST = copy_dve(ST[2], psum[:, b, :].rearrange("p (h n) -> p h n", h=4), k)
    give(b, k_ST)
    step()
    gss, grs = stat(8), stat(8)
    for t in range(2):
        for i in range(2):
            b, free = bank()
            for s in range(2):
                h = 2 * i + s
                pairs = [(ST[t][:, h, :], gv[:, t, 256 * h:256 * h + 256])]
                if t:
                    pairs.append((ST[2][:, h, :], gv[:, 0, 256 * h:256 * h + 256]))
                k = group(psum[:, b, 256 * s:256 * s + 256], pairs, k_ST, kg["v"], free)
            j = 4 * t + 2 * i
            for s in range(2):
                k2 = sum_sq(gss[:, j + s:j + s + 1], psum[:, b, 256 * s:256 * s + 256], k)
            k2 = rsqrt_mean(grs[:, j:j + 2], gss[:, j:j + 2], 256, k2)
            o = gr[:, t, 512 * i:512 * i + 512]
            k = tt(dve, o, psum[:, b, :], o, ALU.mult, k, kg["r"], k2)
            give(b, k)
            o2 = o.rearrange("p (h n) -> p h n", h=2)
            k = tt(dve, o2, o2, bc(grs[:, j:j + 2], 2, [P, 2, 256]), ALU.mult, k)
            step()
            k_oT = gain_T(o, oT, 4 * i, t, col("gla_norm_2").unsqueeze(1).unsqueeze(3).to_broadcast([P, 2, 2, P]), k)
    step(20)
    memT = pair(14336, 8)
    mem = f32(12288, 2048).rearrange("p (t n) -> p t n", t=2)
    in_mem = sp.dma(m["s_mem"], 16, mem, a["mem_2"].rearrange("b (t p) d -> p (b t) d", p=P), k_oT)
    k_mem = norm_T(lambda t: mem[:, t, :], [in_mem, in_mem], col("norm_mem_2"), memT)
    k_mix = merge(a["w_up_ssd_2"][0], yT, k_yT, a["w_up_gla_2"][0], oT, k_oT, sig, k_sig, xT)
    run(tm(a["w_o_2"][0], 0, D, xT, k_mix, to_residual))

    kx = [k_x[0], k_x[1]]
    mkT = f32(flat["gv"], 2048).rearrange("p (c n) -> p c n", c=8)
    mv = f32(flat["sig"], 2048).rearrange("p (t n) -> p t n", t=2)
    qx = f32(flat["sig"] + 2048, 2048).rearrange("p (c n) -> p c n", c=8)
    px = f32(flat["sig"] + 4096, 2048).rearrange("p (t h n) -> p t h n", t=2, h=4)
    pxT = f32(8192, 2048).rearrange("p (h m n) -> p h m n", h=4, m=2)
    oxT = pair(4096, 8)
    wkv = a["w_xkv_2"][0]
    fill[0] = chain(fm(wkv, 0, D, memT, k_mem, keep_fm(mkT, kg, "mk")),
                    tm(wkv, D, D, memT, k_mem, keep_tm(mv, kg, "mv", ACT.Copy)))
    step(3)
    h_ready = norm_T(lambda t: x[:, t, :], kx, col("norm_xattn_2"), xT)
    step(1)
    run(fm(a["w_xq_2"][0], 0, D, xT, h_ready, keep_fm(qx, kg, "qx")))
    xm, xden = stat(8), stat(8)

    def x_scores(h):
        b, free = bank()
        S = psum[:, b, :].rearrange("p (t n) -> p t n", t=2)
        for t in range(2):
            k = group(S[:, t, :], [(qx[:, 2 * h + c, t * P:t * P + P], mkT[:, 2 * h + c, :]) for c in range(2)],
                      kg["qx", h], kg["mk", h], free)
        mx, d = xm[:, 2 * h:2 * h + 2], xden[:, 2 * h:2 * h + 2]
        k = dve.do(lambda e: e.tensor_reduce(mx, S, AX.X, ALU.max), k)
        k = ts(dve, mx, mx, -1 / 16, None, ALU.mult, None, k)
        for t in range(2):
            k2 = fn(px[:, t, h, :], S[:, t, :], ACT.Exp, k, bias=mx[:, t:t + 1], scale=1 / 16, accum_out=d[:, t:t + 1])
        give(b, k2)
        k = dve.do(lambda e: e.reciprocal(d, d), k2)
        return tt(dve, px[:, :, h, :], px[:, :, h, :], bc(d, 2, [P, 2, 256]), ALU.mult, k)

    def x_out(h, k):
        b, free = bank()
        k = transposes(psum[:, b, :], [px[:, t, h, c * P:c * P + P] for c in range(2) for t in range(2)], k, free)
        k = copy_act(pxT[:, h, :, :], psum[:, b, :].rearrange("p (m n) -> p m n", m=2), k)
        give(b, k)
        b, free = bank()
        pe.wait(k)
        for c in range(2):
            f = 256 * h + 128 * c
            k = group(psum[:, b, 256 * c:256 * c + 256], [(mv[:, i, f:f + P], pxT[:, h, i, :]) for i in range(2)],
                      kg["mv"], free)
        v = psum[:, b, :].rearrange("p (c n) -> p c n", c=2)
        k = divide(v, oxT[0][:, 2 * h:2 * h + 2, :], oxT[1][:, 2 * h:2 * h + 2, :], k)
        give(b, k)
        return k

    k_px = []
    for h in range(4):
        k_px.append(x_scores(h))
        step()
    for h in range(4):
        k_ox = x_out(h, k_px[h])
    run(tm(a["w_xo_2"][0], 0, D, oxT, k_ox, to_residual))

    kx = [k_x[0], k_x[1]]
    h_ready = norm_T(lambda t: x[:, t, :], kx, col("norm_ffn_2"), xT)
    wf = a["w_ffn_in_2"][0]

    def gate_evac(q, ps, tok):
        state["gate"] = fn(tmps[q % 4], ps, ACT.Silu, tok)
        return state["gate"]

    def prod_evac(q, ps, tok):
        r = tmps[q % 4]
        k = tt(dve, r, ps, r, ALU.mult, tok, state["gate"])
        dst, free = state["dst"]
        state["k"] = divide(r, dst[0], dst[1], k, free)
        return k

    gates = fm(wf, 0, 2816, xT, h_ready, gate_evac)
    prods = fm(wf, 2816, 2816, xT, h_ready, prod_evac)

    def up_swiglu(q, dst, free):
        state["dst"] = dst, free
        next(gates)
        next(prods)
        return state["k"]

    mlp(11, up_swiglu, a["w_ffn_out_2"][0])
    k_y = last_norm("norm_final_2")
    sp.dma(m["s_out"], 16, out.rearrange("b (t p) d -> p (b t) d", p=P), x[:, :, :], *k_y)
    sp.wait((m["s_out"], 16))
    return (pe, act, dve, pool, sp), wanted


def shape_constants():
    i = np.arange(P)
    v = {}
    v["upper"] = i[:, None] <= i[None, :]
    v["after"] = i[:, None] > i[None, :]
    v["causal"] = np.where(i[None, :] <= i[:, None], 0.0, NEG)
    end = 16 * np.arange(15) + 31
    tok = i[:, None] + P * np.arange(2)[None, :]
    v["cmask"] = np.where(end[None, None, :] <= tok[:, :, None], 0.0, NEG).reshape(P, 30)
    v["crow"] = tok >= 31
    lg = np.log(1.0 - np.exp2(-5.0 - np.arange(4)))
    rel = np.arange(256)[None, :] - i[:, None]
    v["decay"] = np.concatenate([np.where(rel >= 0, np.exp(g * np.maximum(rel, 0)), 0.0) * P ** -0.5 for g in lg], 1)
    v["inv"] = np.tile(np.array(INV_BITS, np.uint32).view(np.float32)[None, :], (P, 1))
    v["keep"] = np.tile((np.arange(256) % 64 != 0)[None, :], (P, 1))
    return np.ascontiguousarray(np.concatenate([np.asarray(v[n], np.float32) for n in CONSTS], 1))


INV_BITS = [
    0x3f800000, 0x3e4693b0, 0x3d1a08c9, 0x3beef752, 0x3ab95d24, 0x398fc8f8, 0x385f10cb, 0x372d07a6, 0x3f800000,
    0x3f5dafd6, 0x3f3ff911, 0x3f263de0, 0x3f0ff59a, 0x3ef953ce, 0x3ed7e89a, 0x3ebaf81a, 0x3ea1e89b, 0x3e8c3503,
    0x3e72d422, 0x3e5247ed, 0x3e361887, 0x3e1db040, 0x3e088d77, 0x3dec7fd5, 0x3dcccccc, 0x3db15978, 0x3d99940d,
    0x3d84fe4c, 0x3d6655c1, 0x3d477640, 0x3d2cba16, 0x3d159348, 0x3d0186e2, 0x3ce054d1, 0x3cc2434e, 0x3ca83989,
    0x3c91ad3a, 0x3c7c4d30, 0x3c5a7bf1, 0x3c3d330e, 0x3c23d70a, 0x3c0de12e, 0x3bf5b9ad, 0x3bd4ca16, 0x3bb8449a,
    0x3b9f91cc, 0x3b8a2e75, 0x3b6f520d, 0x3b4f3e33, 0x3b33770d, 0x3b1b690e, 0x3b06946d, 0x3ae91528, 0x3ac9d759,
    0x3aaec98d, 0x3a975c0b, 0x3a83126e, 0x3a6301e3, 0x3a44948a, 0x3a2a3b44, 0x3a136a14, 0x39ff4fac, 0x39dd1722,
    0x39bf74d6, 0x39a5cb60, 0x398f9275, 0x3978a80d, 0x395753e2, 0x393a7753, 0x39217918, 0x390bd46d, 0x38f22cdd]


WEIGHTS = ["x", "w_in", "cmp_k_w1", "cmp_k_w2", "cmp_v_w1", "cmp_v_w2", "w_proj_a", "w_proj_b", "w_out", "w_up",
           "w_down", "norm_final", "mem_2", "w_in_2", "ssd_dt_bias_2", "ssd_A_log_2", "ssd_D_2", "gla_w_a2_2",
           "w_up_ssd_2", "w_up_gla_2", "w_o_2", "w_xq_2", "w_xkv_2", "w_xo_2", "w_ffn_in_2", "w_ffn_out_2",
           "norm_final_2"]


def kernel(**inputs):
    import concourse.bacc as bacc
    from concourse.bass_utils import run_bass_kernel_spmd

    get = {n: np.asarray(v) for n, v in inputs.items()}

    def by_column(v):
        return v.reshape(-1, P).T

    cols = {n: by_column(get[n]) for n in ("norm_mix", "norm_mlp", "norm_mix_2", "ssd_norm_2", "gla_norm_2",
                                            "norm_xattn_2", "norm_mem_2", "norm_ffn_2")}
    cols["conv_w"] = get["ssd_conv_w_2"].reshape(4, 12, P).transpose(2, 1, 0).reshape(P, 48)
    cols["conv_b"] = by_column(get["ssd_conv_b_2"])
    cols["gla_b"] = by_column(get["gla_b_a_2"])
    cols["pe_k"] = by_column(get["cmp_pos_k"])
    cols["pe_v"] = by_column(get["cmp_pos_v"])
    arrays = {n: np.ascontiguousarray(get[n]) for n in WEIGHTS}
    arrays["cols"] = np.ascontiguousarray(np.concatenate([cols[n] for n in COLS], 1))
    arrays["pos"] = np.ascontiguousarray(get["positions"].reshape(2, P).T)
    arrays["consts"] = shape_constants()
    arrays["ident"] = np.eye(P, dtype=np.float32)

    nc = bacc.Bacc("TRN2", target_bir_lowering=False, num_devices=1)
    aps = {n: nc.dram_tensor(f"in_{n}", v.shape, mybir.dt.from_np(v.dtype), kind="ExternalInput").ap()
           for n, v in arrays.items()}
    out = nc.dram_tensor("out_0", (1, 256, D), F32, kind="ExternalOutput").ap()
    build(nc, aps, out)
    r = run_bass_kernel_spmd(nc, [{f"in_{n}": v for n, v in arrays.items()}], core_ids=[0])
    return r.results[0]["out_0"]
```

```python
import math
from contextlib import ExitStack

import numpy as np

import concourse.bass as bass
import concourse.mybir as mybir

F32 = mybir.dt.float32
F32R = mybir.dt.float32r
I32 = mybir.dt.int32
ALU = mybir.AluOpType
ACT = mybir.ActivationFunctionType
AX = mybir.AxisListType
P = 128
D = 1024
EPS = 1e-6
NEG = -1e30
RAW = 4
PARTS = 5
TILE = 1024
ROOM = 28400

CONSTS = dict(upper=128, after=128, causal=128, cmask=30, crow=2, decay=1024, inv=72, keep=256)
COLS = dict(norm_mix=8, norm_mlp=8, norm_mix_2=8, ssd_norm_2=8, gla_norm_2=2, norm_xattn_2=8, norm_mem_2=8,
            norm_ffn_2=8, conv_w=48, conv_b=12, gla_b=4, pe_k=16, pe_v=16)
ROWS = dict(norm_final=1024, norm_final_2=1024, ssd_dt_bias_2=16, ssd_A_log_2=16, ssd_D_2=16)
LOADS = ("x0", "x1", "ident", "consts", "cols", "rows", "pos", "w2k", "w2v", "wa2", "mem", "out")


def offsets(sizes):
    at, out = 0, {}
    for name, n in sizes.items():
        out[name] = (at, n)
        at += n
    return out, at


class Queue:

    def __init__(self, sem, serial=False):
        self.sem, self.n, self.todo, self.seen, self.serial = sem, 0, [], {}, serial

    def wait(self, *tokens):
        for t in tokens:
            if callable(t):
                t = t()
            if isinstance(t, list):
                self.wait(*t)
            elif t is not None:
                sem, n = t
                if self.seen.get(id(sem), 0) < n:
                    self.seen[id(sem)] = n
                    self.todo.append(lambda e, sem=sem, n=n: e.wait_ge(sem, n))

    def do(self, fn, *waits, free=False):
        self.wait(*waits)
        if self.serial and self.n and not free:
            self.wait((self.sem, self.n))
        self.n += 1
        self.todo.append(lambda e: fn(e).then_inc(self.sem, 1))
        return (self.sem, self.n)

    def part(self, fn, *waits):
        self.wait(*waits)
        self.todo.append(fn)

    def dma(self, sem, at, out, in_, *waits):
        self.wait(*waits)
        self.todo.append(lambda e: e.dma_start(out, in_).then_inc(sem, 16))
        return (sem, at)


def build(nc, a, out):
    with ExitStack() as ctx:
        m = {}
        for name, shape, dt in (
                ("raws", [P, RAW, TILE], F32), ("parts", [P, PARTS, 2, TILE], F32R),
                ("consts", [P, offsets(CONSTS)[1]], F32), ("cols", [P, offsets(COLS)[1]], F32),
                ("rows", [P, offsets(ROWS)[1]], F32), ("posi", [P, 2], I32), ("x", [P, 2, D], F32),
                ("big", [P, 2, D], F32), ("w2k", [P, 2, 2, 64], F32), ("w2v", [P, 2, 64], F32), ("wa2", [16, 512], F32),
                ("ident", [P, P], F32), ("junk", [P, D], F32), ("half", [P, 16], F32), ("ssq", [P, 256], F32)):
            m[name] = ctx.enter_context(nc.sbuf_tensor(name, shape, dt))
        with nc.sbuf_tensor("room", [P, ROOM], F32) as m["room"]:
            pass
        m["room_r"] = ctx.enter_context(nc.sbuf_tensor("room_r", [P, ROOM], F32R))
        m["ps"] = ctx.enter_context(nc.psum_tensor("ps", [P, 8, 512], F32))
        for name in ("pe", "act", "dve", "pool", "sp", *LOADS, *(f"w{i}" for i in range(RAW))):
            m["s_" + name] = ctx.enter_context(nc.semaphore("s_" + name))
        plan = record(a, out, m, None)[1]
        queues = record(a, out, m, plan)[0]
        block = ctx.enter_context(nc.Block())
        for engine, q in zip((block.tensor, block.scalar, block.vector, block.gpsimd, block.sync), queues):
            def emit(e, q=q):
                for f in q.todo:
                    f(e)
            engine(emit)


def record(a, out, m, plan):
    pe, sp = Queue(m["s_pe"]), Queue(m["s_sp"])
    act, dve, pool = (Queue(m[f"s_{n}"], serial=True) for n in ("act", "dve", "pool"))
    raws, parts, psum, x, big, ident = (m[n] for n in ("raws", "parts", "ps", "x", "big", "ident"))
    w2k, w2v, wa2, half, ssq, junk = (m[n] for n in ("w2k", "w2v", "wa2", "half", "ssq", "junk"))

    def table(name, sizes):
        at, _ = offsets(sizes)
        return lambda n: m[name][:, at[n][0]:at[n][0] + at[n][1]]

    const, col, row = table("consts", CONSTS), table("cols", COLS), table("rows", ROWS)
    ident = ident[:, :]

    def f32(at, n):
        return m["room"][:, at:at + n]

    def pair(at, chunks):
        return [m["room_r"][:, at + i * 256 * chunks:at + (i + 1) * 256 * chunks]
                .rearrange("p (c n) -> p c n", c=chunks) for i in range(2)]

    xin = a["x"].rearrange("b (t p) d -> p (b t) d", p=P)
    in_x = [q.dma(m[f"s_x{t}"], 16, x[:, t, :], xin[:, t, :]) for t, q in enumerate((act, sp))]
    in_ident = act.dma(m["s_ident"], 16, m["ident"][:, :], a["ident"])
    sp.wait(in_x[0])
    in_cols = act.dma(m["s_cols"], 16, m["cols"][:, :], a["cols"])
    in_pos = act.dma(m["s_pos"], 16, m["posi"][:, :], a["pos"])
    in_consts = act.dma(m["s_consts"], 16, m["consts"][:, :], a["consts"])

    bank_free = [(b, None) for b in range(8)]

    def bank():
        return bank_free.pop(0)

    def give(b, token):
        bank_free.append((b, token))

    wanted = []
    halfway = [False]
    raw_free = [None] * RAW
    part_free = [None] * PARTS
    raw_busy, part_busy = [False] * RAW, [False] * PARTS
    n_parts = [0]
    late = []
    loaded, divided = [], []

    def load_ahead():
        while len(loaded) < len(plan) and not raw_busy[len(loaded) % RAW]:
            i = len(loaded)
            src, k, n, _ = plan[i]
            s = i % RAW
            if raw_free[s] in late:
                return
            raw_busy[s] = True
            view = raws[:, s, 0:k * n].rearrange("p (k n) -> p k n", k=k)
            token = sp.dma(m[f"s_w{s}"], 16 * (i // RAW + 1), view, src.rearrange("(k p) n -> p k n", p=P), raw_free[s])
            loaded.append((view, token))

    def divide_ahead(most=PARTS):
        most += len(divided)
        while len(divided) < min(len(plan), most):
            load_ahead()
            i = len(divided)
            if i == len(loaded):
                return
            _, k, n, whole = plan[i]
            view, token = loaded[i]
            if whole:
                divided.append((view, None, token, i % RAW))
                continue
            p = n_parts[0] % PARTS
            if part_busy[p]:
                return
            part_busy[p] = True
            n_parts[0] += 1
            h, l = (parts[:, p, j, 0:k * n].rearrange("p (k n) -> p k n", k=k) for j in range(2))
            kl = divide(view, h, l, token, part_free[p])
            raw_free[i % RAW] = kl
            raw_busy[i % RAW] = False
            divided.append((h, l, kl, p))

    def weight(src, k, n, whole=False):
        if plan:
            divide_ahead()
            while len(divided) <= len(wanted):
                settle()
                divide_ahead()
            got = divided[len(wanted)]
        else:
            got = (raws[:, 0, 0:k * n].rearrange("p (k n) -> p k n", k=k),
                   parts[:, 0, 1, 0:k * n].rearrange("p (k n) -> p k n", k=k), None, 0)
        wanted.append((src, k, n, whole))
        return got

    def used(tile, token):
        if tile[1] is None:
            raw_free[tile[3]] = token
            raw_busy[tile[3]] = False
        else:
            part_free[tile[3]] = token
            part_busy[tile[3]] = False

    def mm(ps, lhsT, rhs, start, stop):
        return lambda e: e.matmul(ps, lhsT, rhs, start=start, stop=stop)

    def group(ps, pairs, *waits):
        pe.wait(*waits)
        for i, (l, r) in enumerate(pairs):
            f = mm(ps, l, r, i == 0, i == len(pairs) - 1)
            if i == len(pairs) - 1:
                return pe.do(f)
            pe.part(f)

    def chunk(ready, k):
        return ready[k] if isinstance(ready, list) else ready

    def fm(w, c0, cn, hT, ready, evac):
        K = w.shape[0] // P
        for q0 in range(0, cn, 256):
            nb = min(256, cn - q0)
            tiles = [weight(w[k0 * P:(k0 + 4) * P, c0 + q0:c0 + q0 + nb], 4, nb) for k0 in range(0, K, 4)]
            b, free = bank()
            pe.wait(free)
            for s in range(0, nb, P):
                ps = psum[:, b, 2 * s:2 * s + 256]
                for k in range(K):
                    wh, wl, tok, _ = tiles[k // 4]
                    pe.wait(tok, chunk(ready, k))
                    wh, wl = (v[:, k % 4, s:s + P] for v in (wh, wl))
                    pe.part(mm(ps, wh, hT[0][:, k, :], k == 0, False))
                    pe.part(mm(ps, wh, hT[1][:, k, :], False, False))
                    f = mm(ps, wl, hT[0][:, k, :], False, k == K - 1)
                    if k % 4 == 3:
                        t = pe.do(f)
                        if s + P >= nb:
                            used(tiles[k // 4], t)
                    else:
                        pe.part(f)
                if s + P < nb:
                    halfway[0] = True
                    yield
                    halfway[0] = False
            v = psum[:, b, 0:512].rearrange("p (s n) -> p s n", s=2)
            give(b, evac(q0 // 256, v[:, 0:nb // P, :], t))
            yield

    def tm(w, c0, cn, hT, ready, evac):
        K = w.shape[0] // P
        for b0 in range(0, cn, 512):
            nb = min(512, cn - b0)
            banks = [bank(), bank()]
            pe.wait(banks[0][1], banks[1][1])
            for k0 in range(0, K, 2):
                tile = weight(w[k0 * P:(k0 + 2) * P, c0 + b0:c0 + b0 + nb], 2, nb)
                wh, wl, tok, _ = tile
                pe.wait(tok, chunk(ready, k0), chunk(ready, k0 + 1))
                done = [None, None]
                for t in range(2):
                    ps = psum[:, banks[t][0], 0:nb]
                    c = slice(t * P, t * P + P)
                    for k in range(k0, k0 + 2):
                        pe.part(mm(ps, hT[0][:, k, c], wh[:, k - k0, :], k == 0, False))
                        pe.part(mm(ps, hT[0][:, k, c], wl[:, k - k0, :], False, False))
                        f = mm(ps, hT[1][:, k, c], wh[:, k - k0, :], False, k == K - 1)
                        if k == k0 + 1:
                            done[t] = pe.do(f)
                        else:
                            pe.part(f)
                used(tile, done[1])
                if k0 + 2 == K:
                    for t in range(2):
                        give(banks[t][0], evac(b0 // 512, t, psum[:, banks[t][0], 0:nb], done[t]))
                yield

    def run(*gens):
        while halfway[0]:
            step()
        for g in gens:
            for _ in g:
                pass

    def chain(*gens):
        for g in gens:
            yield from g

    fill = [iter(())]

    def step(n=1):
        for _ in range(n):
            next(fill[0], None)

    def transposes(ps, ins, *waits):
        pe.wait(*waits)
        for i, v in enumerate(ins):
            f = (lambda e, i=i, v=v: e.transpose(ps[0:v.shape[1], i * P:(i + 1) * P], v, ident))
            if i == len(ins) - 1:
                return pe.do(f)
            pe.part(f)

    def copy_act(o, i, *waits, free=False):
        return act.do(lambda e: e.activation(o, i, ACT.Copy), *waits, free=free)

    def copy_dve(o, i, *waits, free=False):
        return dve.do(lambda e: e.tensor_copy(o, i), *waits, free=free)

    def tt(q, o, a0, a1, op, *waits, free=False):
        return q.do(lambda e: e.tensor_tensor(o, a0, a1, op), *waits, free=free)

    def ts(q, o, i, s1, s2, op0, op1, *waits, free=False):
        if op1 is None:
            return q.do(lambda e: e.tensor_scalar(o, i, s1, None, op0), *waits, free=free)
        return q.do(lambda e: e.tensor_scalar(o, i, s1, s2, op0, op1), *waits, free=free)

    def stt(o, i, s, i1, op0, op1, *waits, free=False):
        return dve.do(lambda e: e.scalar_tensor_tensor(out=o, in0=i, scalar=s, in1=i1, op0=op0, op1=op1), *waits,
                      free=free)

    def fn(o, i, f, *waits, free=False, **kw):
        return act.do(lambda e: e.activation(o, i, f, **kw), *waits, free=free)

    def bc(v, axis, shape):
        return v.unsqueeze(axis).to_broadcast(shape)

    def settle():
        while late:
            late.pop(0)()

    def divide(v, h, l, *waits):
        settle()
        k = copy_act(h, v, *waits, free=True)
        got = []

        def token():
            if not got:
                got.append(tt(dve, l, v, h.bitcast(F32), ALU.subtract, k, free=True))
            return got[0]
        late.append(token)
        return token

    k_half = pool.do(lambda e: e.memset(half[:, :], -0.5))
    nstat = [0]

    def stat(n):
        nstat[0] += n
        assert nstat[0] <= 256
        return ssq[:, nstat[0] - n:nstat[0]]

    def rsqrt_mean(o, ss, count, *waits):
        n = ss.shape[-1]
        k = pool.do(lambda e: e.tensor_scalar(o, ss, 1.0 / count, EPS, ALU.mult, ALU.add), *waits)
        return pool.do(lambda e: e.tensor_tensor(o, o, half[:, 0:n], ALU.pow), k, k_half)

    def sum_sq(o, i, *waits):
        return fn(junk[:, 0:i.shape[-1]], i, ACT.Square, *waits, accum_out=o)

    def turn_T(src, *waits):
        b, free = bank()
        return b, transposes(psum[:, b, :], [src[:, j * P:(j + 1) * P] for j in range(4)], *waits, free, in_ident)

    def gain_in(turned, src, dst, c0, t, gain):
        b, k = turned
        if len(gain.shape) == 4:
            k = tt(dve, src.rearrange("p (i j n) -> p i j n", i=2, j=2),
                   psum[:, b, :].rearrange("p (i j n) -> p i j n", i=2, j=2), gain, ALU.mult, k, in_cols)
        else:
            k = tt(dve, src.rearrange("p (j n) -> p j n", j=4), psum[:, b, :].rearrange("p (j n) -> p j n", j=4),
                   gain, ALU.mult, k, in_cols)
        give(b, k)
        return divide(src.rearrange("p (j n) -> p j n", j=4), dst[0][:, c0:c0 + 4, t * P:t * P + P],
                      dst[1][:, c0:c0 + 4, t * P:t * P + P], k)

    def gain_T(src, dst, c0, t, gain, *waits):
        return gain_in(turn_T(src, *waits), src, dst, c0, t, gain)

    def stats(src, t, blk, *waits):
        c = slice(512 * blk, 512 * blk + 512)
        o = stat(1)
        return o, fn(big[:, t, c], src(t)[:, c], ACT.Square, *waits, free=True, accum_out=o, scale=1 / 32)

    def rsqrt_of(shares):
        (s0, k0), (s1, k1) = shares
        r = stat(1)
        k = pool.do(lambda e: e.tensor_scalar(r, s0, s1, EPS, ALU.add, ALU.add), k0, k1)
        return r, pool.do(lambda e: e.tensor_tensor(r, r, half[:, 0:1], ALU.pow), k, k_half)

    def norm_T(src, ready, gain, dst, after=None, shares=None, rs=None):
        if not rs:
            rs = [rsqrt_of(shares[t] if shares else [stats(src, t, q, ready[t], after) for q in range(2)])
                  for t in range(2)]
        if plan:
            divide_ahead(2)
        step(3)
        todo = [(t, q) for q in range(2) for t in range(2)]
        turned, done = {}, {}

        def scale(t, q):
            c = slice(512 * q, 512 * q + 512)
            r, k = rs[t]
            if q:
                k = fn(big[:, t, c], src(t)[:, c], ACT.Copy, k, ready[t], after, scale=r)
            else:
                k = ts(dve, big[:, t, c], src(t)[:, c], r, None, ALU.mult, None, k, ready[t], after)
            turned[t, q] = turn_T(big[:, t, c], k)

        scale(*todo[0])
        scale(*todo[1])
        for i, (t, q) in enumerate(todo):
            done[t, q] = gain_in(turned[t, q], big[:, t, 512 * q:512 * q + 512], dst, 4 * q, t,
                                 bc(gain[:, 4 * q:4 * q + 4], 2, [P, 4, P]))
            if i + 2 < 4:
                scale(*todo[i + 2])
        if plan:
            divide_ahead()
        return [[done[0, q], done[1, q]] for q in range(2) for _ in range(4)]

    shares = {}

    def to_residual(blk, t, ps, tok):
        k_x[t] = tt(dve, x[:, t, blk * 512:blk * 512 + 512], ps, x[:, t, blk * 512:blk * 512 + 512], ALU.add, tok,
                    free=True)
        shares.setdefault(t, [None, None])[blk] = stats(lambda t: x[:, t, :], t, blk, k_x[t])
        if twice[0]:
            c = slice(512 * blk, 512 * blk + 512)
            k_z[t] = tt(dve, z[:, t, c], x[:, t, c], row("norm_final")[:, c], ALU.mult, k_x[t], in_rows, free=True)
            o = stat(1)
            k = fn(junk[:, c], z[:, t, c], ACT.Square, k_z[t], accum_out=o, scale=1 / 32)
            z_shares.setdefault(t, [None, None])[blk] = (o, k)
        return k_x[t]

    twice, z, z_shares, k_z = [False], f32(24576, 2048).rearrange("p (t n) -> p t n", t=2), {}, {}

    def twice_rsqrt(t):
        r, k = rsqrt_of(shares[t])
        (s0, k0), (s1, k1) = z_shares[t]
        sq, both, rr = stat(1), stat(1), stat(1)
        pool.do(lambda e: e.tensor_tensor(sq, r, r, ALU.mult))
        pool.do(lambda e: e.tensor_tensor(both, s0, s1, ALU.add), k0, k1)
        pool.do(lambda e: e.tensor_scalar(rr, both, sq, EPS, ALU.mult, ALU.add))
        pool.do(lambda e: e.tensor_tensor(rr, rr, half[:, 0:1], ALU.pow))
        return r, k, rr, pool.do(lambda e: e.tensor_tensor(rr, rr, r, ALU.mult))

    xT = pair(0, 8)
    at = [8192]

    def take(n):
        at[0] += n
        assert at[0] <= ROOM, at[0]
        return f32(at[0] - n, n)

    h_ready = norm_T(lambda t: x[:, t, :], in_x, col("norm_mix"), xT)
    for h in range(2):
        in_w2k = pool.dma(m["s_w2k"], 16 * (h + 1), w2k[:, :, h, :], a["cmp_k_w2"][0].rearrange("(c p) n -> p c n", p=P))
    in_w2v = pool.dma(m["s_w2v"], 16, w2v[:, :, :], a["cmp_v_w2"][0].rearrange("(c p) n -> p c n", p=P))
    in_wa2 = pool.dma(m["s_wa2"], 16, wa2[:, :], a["gla_w_a2_2"][0])
    n = 0
    for name in ROWS:
        n += 16
        src = a[name] if name.startswith("norm_final") else a[name][0]
        in_rows = pool.dma(m["s_rows"], n, row(name), src.partition_broadcast(P))

    tmp_all = take(2048)
    tmp = [tmp_all[:, 512 * i:512 * i + 512] for i in range(4)]
    w_in = a["w_in"][0]
    qkv = take(2 * 1304).rearrange("p (t n) -> p t n", t=2)
    kq = {}

    def to_qkv(blk, t, ps, tok):
        kq[t] = copy_act(qkv[:, t, 512 * blk:512 * blk + ps.shape[-1]], ps, tok)
        return kq[t]

    gens = tm(w_in, 0, 1304, xT, h_ready, to_qkv)
    for _ in range(4):
        next(gens)
    ang = take(144).rearrange("p (t f) -> p t f", t=2)
    posf = take(2)
    C1 = 6.28125
    C2 = float(np.float32(np.round((2 * math.pi - C1) * 2.0 ** 18) / 2.0 ** 18))
    C3 = float(np.float32(2 * math.pi - C1 - C2))
    MAGIC = 1.5 * 2.0 ** 23
    TOP = 3.1415925
    k = copy_dve(posf, m["posi"][:, :], in_pos)
    for t in range(2):
        kang = ts(dve, ang[:, t, :], const("inv"), posf[:, t:t + 1], None, ALU.mult, None, k, in_consts)
    trig = []
    for name, quarter in (("sin", 0.0), ("cos", 0.25)):
        turns, red = (tmp[i][:, 0:144].rearrange("p (t f) -> p t f", t=2) for i in range(2))
        tab = take(144).rearrange("p (t f) -> p t f", t=2)
        k = ts(dve, turns, ang, 1 / (2 * math.pi), quarter, ALU.mult, ALU.add, kang)
        k = ts(dve, turns, turns, MAGIC, None, ALU.add, None, k)
        k = ts(dve, turns, turns, MAGIC, None, ALU.subtract, None, k)
        k = stt(red, turns, -C1, ang, ALU.mult, ALU.add, k)
        k = stt(red, turns, -C2, red, ALU.mult, ALU.add, k)
        k = stt(red, turns, -C3, red, ALU.mult, ALU.add, k)
        if quarter:
            k = ts(dve, red, red, math.pi / 2, None, ALU.add, None, k)
        k = ts(dve, red, red, TOP, -TOP, ALU.min, ALU.max, k)
        ktrig = fn(tab, red, ACT.Sin, k)
        dve.wait(ktrig)
        trig.append(tab)
    sin, cos = trig

    run(gens)
    k_qkv = kq[1]
    if plan:
        divide_ahead()
        settle()

    def rotate(o1, o2, i1, i2, c, s, shape, *waits):
        n = int(np.prod(shape[1:]))
        names = " ".join("abc"[:len(shape) - 1])
        v = [z[:, 0:n].rearrange(f"p ({names}) -> p {names}", **dict(zip("abc", shape[1:]))) for z in tmp]
        dve.wait(*waits, ktrig)
        tt(dve, v[0], i1, c, ALU.mult)
        tt(dve, v[1], i2, s, ALU.mult, free=True)
        tt(dve, v[2], i1, s, ALU.mult, free=True)
        k = tt(dve, v[3], i2, c, ALU.mult, free=True)
        tt(dve, o1, v[0], v[1], ALU.subtract, k)
        return tt(dve, o2, v[2], v[3], ALU.add, k, free=True)

    heads = qkv[:, :, 0:1280].rearrange("p t (h d) -> p t h d", d=64)
    for t in range(2):
        c, s = cos[:, t, 0:8], sin[:, t, 0:8]
        q1, q2 = heads[:, t, 0:8, 0:8], heads[:, t, 0:8, 8:16]
        k_rot = rotate(q1, q2, q1, q2, bc(c, 1, [P, 8, 8]), bc(s, 1, [P, 8, 8]), [P, 8, 8], k_qkv)
        for h in (8, 12, 16):
            q1, q2 = heads[:, t, h:h + 2, 0:8], heads[:, t, h:h + 2, 8:16]
            k_rot = rotate(q1, q2, q1, q2, bc(c, 1, [P, 2, 8]), bc(s, 1, [P, 2, 8]), [P, 2, 8], k_qkv, k_rot)

    rqk_all = take(2048)
    rq, rk = (rqk_all[:, i:i + 1024].rearrange("p (t n) -> p t n", t=2) for i in (0, 1024))
    rv, rg = (take(1024).rearrange("p (t n) -> p t n", t=2) for _ in range(2))
    kr = {}

    def to_rot(dst, name):
        def evac(blk, t, ps, tok):
            v = ps.rearrange("p (h s d) -> p h s d", h=4, s=2)
            o = dst[:, t, :].rearrange("p (h s d) -> p h s d", h=4, s=2)
            kr[name] = rotate(o[:, :, 0, :], o[:, :, 1, :], v[:, :, 0, :], v[:, :, 1, :],
                              bc(cos[:, t, 8:72], 1, [P, 4, 64]), bc(sin[:, t, 8:72], 1, [P, 4, 64]),
                              [P, 4, 64], tok, kr.get(name))
            return kr[name]
        return evac

    def keep_tm(dst, keep, name, f):
        def evac(blk, t, ps, tok):
            keep[name] = fn(dst[:, t, 512 * blk:512 * blk + 512], ps, f, tok)
            return keep[name]
        return evac

    def keep_fm(dst, keep, name, f=ACT.Copy):
        def evac(q, ps, tok):
            keep[name] = keep[name, q] = fn(dst[:, 2 * q:2 * q + 2, :], ps, f, tok)
            return keep[name]
        return evac

    def gates(sig, k_sig):
        for i in range(4):
            v = sig[:, 4 * i:4 * i + 4, :]
            k_sig["g", 2 * i] = k_sig["g", 2 * i + 1] = fn(v, v, ACT.Sigmoid, k_sig["g"], free=i > 0)

    sig = take(4096).rearrange("p (c n) -> p c n", c=16)
    k_sig = {}
    gsig = take(48).rearrange("p (t h b) -> p t h b", t=2, h=8)
    for t in range(2):
        k_gsig = fn(gsig[:, t, :, :], qkv[:, t, 1280:1304].rearrange("p (h b) -> p h b", b=3), ACT.Sigmoid, k_qkv)
    fill[0] = chain(tm(w_in, 1304, 512, xT, h_ready, to_rot(rq, "rq")), tm(w_in, 1816, 512, xT, h_ready, to_rot(rk, "rk")),
                    tm(w_in, 2328, 512, xT, h_ready, keep_tm(rv, kr, "rv", ACT.Copy)),
                    tm(w_in, 2840, 512, xT, h_ready, keep_tm(rg, kr, "rg", ACT.Silu)),
                    fm(w_in, 3352, 2048, xT, h_ready, keep_fm(sig, k_sig, "g")))
    step(3)

    qT = take(1024).rearrange("p (c n) -> p c n", c=4)
    kT = take(1024).rearrange("p (b g n) -> p b g n", b=2, g=2)
    for t in range(2):
        b, free = bank()
        k = transposes(psum[:, b, :], [qkv[:, t, P * c:P * c + P] for c in range(4)], k_rot, free, in_ident)
        k_qT = copy_act(qT[:, :, t * P:t * P + P], psum[:, b, :].rearrange("p (c n) -> p c n", c=4), k)
        give(b, k_qT)

    dups_at = at[0]
    dups = [take(256).rearrange("p (g r d) -> p g r d", g=2, r=2) for _ in range(2)]
    dup_free = [None, None]

    def twice_T(h, ready):
        b, free = bank()
        for t in range(2):
            o = dups[t]
            for r in range(2):
                k = copy_dve(o[:, :, r, :], heads[:, t, h:h + 2, :], ready, dup_free[t], free=True)
            pe.wait(k, free)
            for g in range(2):
                f = (lambda e, g=g, t=t, o=o: e.transpose(psum[:, b, (2 * g + t) * P:(2 * g + t + 1) * P],
                                                          o[:, g, :, :].rearrange("p r d -> p (r d)"), ident))
                k = pe.do(f)
            dup_free[t] = k
        return b, k

    for br, h in ((0, 12), (1, 16)):
        b, k = twice_T(h, k_rot)
        k_kT = copy_act(kT[:, br, :, :], psum[:, b, :].rearrange("p (g n) -> p g n", g=2), k)
        give(b, k_kT)

    def windows(h, pe_col, ready):
        A, B = take(256), take(480).rearrange("p (j c) -> p j c", j=16)
        b, k = twice_T(h, ready)
        for r in range(2):
            half_ = slice(64 * r, 64 * r + 64)
            k2 = copy_act(A[half_, :], psum[half_, b, r::2], k)
        give(b, k2)
        src = bass.AP(A.tensor, A.offset, [list(A.ap[0]), [1, 16], [128, 2], [8, 15]])
        return B, tt(dve, B.rearrange("p j (g c) -> p j g c", g=2), src,
                     pe_col.unsqueeze(2).unsqueeze(3).to_broadcast([P, 16, 2, 15]), ALU.add, k2, in_cols)

    def hidden(w1, B, ready):
        h1 = take(60).rearrange("p (s c) -> p s c", s=2)
        b, free = bank()
        b2, free2 = bank()
        pe.wait(ready, free, free2)
        for j0 in range(0, 16, 4):
            tile = weight(w1[j0 * P:(j0 + 4) * P, :], 4, 256, whole=True)
            pe.wait(tile[2])
            for s, bb in ((0, b), (1, b2)):
                for j in range(j0, j0 + 4):
                    f = mm(psum[:, bb, 0:30], tile[0][:, j - j0, s * P:s * P + P], B[:, j, :], j == 0, j == 15)
                    if (s, j) == (1, j0 + 3):
                        t = pe.do(f)
                    else:
                        pe.part(f)
            used(tile, t)
        fn(h1[:, 0, :], psum[:, b, 0:30], ACT.Silu, t)
        k = fn(h1[:, 1, :], psum[:, b2, 0:30], ACT.Silu, t)
        give(b, k)
        give(b2, k)
        return h1, k

    Bk, k_Bk = windows(8, col("pe_k"), k_rot)
    step(3)
    Bv, k_Bv = windows(10, col("pe_v"), k_qkv)
    step(2)
    hk, k_hk = hidden(a["cmp_k_w1"][0], Bk, k_Bk)
    step(2)
    hv, k_hv = hidden(a["cmp_v_w1"][0], Bv, k_Bv)
    step()
    kTc = take(30)
    vc = take(128).rearrange("p (g d) -> p g d", g=2)
    b, free = bank()
    k = group(psum[:, b, 0:30], [(w2k[:, s, :, :].rearrange("p r d -> p (r d)"), hk[:, s, :]) for s in range(2)],
              k_hk, free, in_w2k)
    k_kTc = copy_act(kTc, psum[:, b, 0:30], k)
    give(b, k_kTc)
    b, free = bank()
    for g in range(2):
        k = group(psum[0:15, b, 64 * g:64 * g + 64], [(hv[:, s, 15 * g:15 * g + 15], w2v[:, s, :]) for s in range(2)],
                  k_hv, free, in_w2v)
    k_vc = copy_act(vc[0:15, :, :], psum[0:15, b, 0:128].rearrange("p (g d) -> p g d", g=2), k)
    give(b, k_vc)
    step(2)

    coef = take(48).rearrange("p (t h b) -> p t h b", t=2, h=8)
    pc = take(240).rearrange("p (t h c) -> p t h c", t=2, h=8)
    pc2 = pc.rearrange("p t h c -> p (t h) c")
    mxc = take(16)
    for odd in range(2):
        b, free = bank()
        C = psum[:, b, 0:120].rearrange("p (t h c) -> p t h c", t=2, h=4)
        r = slice(64 * odd, 64 * odd + 64)
        for t in range(2):
            for i in range(4):
                g = i // 2
                k = group(C[:, t, i, :], [(qT[r, i, t * P:t * P + P], kTc[r, 15 * g:15 * g + 15])], k_qT, k_kTc, free)
        for t in range(2):
            kc_ = stt(pc[:, t, odd::2, :], C[:, t, :, :], 0.125,
                      bc(const("cmask")[:, 15 * t:15 * t + 15], 1, [P, 4, 15]), ALU.mult, ALU.add, k)
        give(b, kc_)
    step()
    k = dve.do(lambda e: e.tensor_reduce(mxc, pc2, AX.X, ALU.max), kc_)
    k = tt(dve, pc2, pc2, bc(mxc, 2, [P, 16, 15]), ALU.subtract, k)
    k_pc = fn(pc2, pc2, ACT.Exp, k)
    cf = coef.rearrange("p t h b -> p (t h) b")[:, :, 0:1]
    k = dve.do(lambda e: e.tensor_reduce(cf, pc2, AX.X, ALU.add), k_pc)
    k = dve.do(lambda e: e.reciprocal(cf, cf), k)
    k = tt(dve, cf, cf, gsig.rearrange("p t h b -> p (t h) b")[:, :, 0:1], ALU.mult, k, k_gsig)
    for t in range(2):
        k = ts(dve, coef[:, t, :, 0:1], coef[:, t, :, 0:1], const("crow")[:, t:t + 1], None, ALU.mult, None, k)
    k_pc = tt(dve, pc2, pc2, cf.to_broadcast([P, 16, 15]), ALU.mult, k)
    pcT = [v.rearrange("p (h n) -> p h n", h=8) for v in (tmp_all[:, 0:1024], f32(dups_at, 1024))]
    pT = [tmp_all[:, 1024:1536], tmp_all[:, 1536:2048]]
    pT_free = [None] * 2
    probs = [big[:, i // 2, 512 * (i % 2):512 * (i % 2) + 512] for i in range(4)]
    probs_free = [None] * 4
    nmax = take(64).rearrange("p (i b) -> p i b", b=4)
    nsaT, retT = pair(4096, 4), pair(6144, 4)

    def cmp_T(t):
        for h0 in (0, 4):
            b, free = bank()
            k2 = transposes(psum[:, b, :], [pc[:, t, h, :] for h in range(h0, h0 + 4)], k_pc, free)
            k2 = copy_dve(pcT[t][0:15, h0:h0 + 4, :], psum[0:15, b, :].rearrange("p (h n) -> p h n", h=4), k2)
            give(b, k2)
        return k2

    def scores(i):
        t, h = divmod(i, 8)
        nk = P * (t + 1)
        g, r = h // 4, slice(64 * (h % 2), 64 * (h % 2) + 64)
        b, free = bank()
        S = psum[:, b, 0:2 * nk].rearrange("p (b n) -> p b n", b=2)
        for br in range(2):
            k = group(S[:, br, :], [(qT[r, h // 2, t * P:t * P + P], kT[r, br, g, 0:nk])], k_qT, k_kT, free)
        diag_ = S[:, :, t * P:t * P + P]
        k = tt(dve, diag_, diag_, bc(const("causal"), 1, [P, 2, P]), ALU.add, k)
        mx, sm = nmax[:, i, 0:2], nmax[:, i, 2:4]
        k = dve.do(lambda e: e.tensor_reduce(mx, S, AX.X, ALU.max), k)
        k = ts(dve, mx, mx, -0.125, None, ALU.mult, None, k)
        Ph = probs[i % 4][:, 0:2 * nk].rearrange("p (b n) -> p b n", b=2)
        for br in range(2):
            k2 = fn(Ph[:, br, :], S[:, br, :], ACT.Exp, k, probs_free[i % 4], bias=mx[:, br:br + 1], scale=0.125,
                    accum_out=sm[:, br:br + 1])
        give(b, k2)
        return Ph, sm, k2

    def weigh(i, Ph, sm, k):
        t, h = divmod(i, 8)
        k = dve.do(lambda e: e.reciprocal(sm, sm), k)
        k = tt(dve, sm, sm, gsig[:, t, h, 1:3], ALU.mult, k, k_gsig)
        return Ph, tt(dve, Ph, Ph, bc(sm, 2, [P, 2, P * (t + 1)]), ALU.mult, k)

    def probs_T(i, Ph, k):
        t = i // 8
        b, free = bank()
        parts_ = [(br, kt) for br in range(2) for kt in range(t + 1)]
        k = transposes(psum[:, b, :], [Ph[:, br, kt * P:kt * P + P] for br, kt in parts_], k, free)
        probs_free[i % 4] = k
        n = len(parts_) * P
        j = i % 2
        k = copy_act(pT[j][:, 0:n], psum[:, b, 0:n], k, pT_free[j], free=True)
        give(b, k)
        return parts_, k

    def pv(i, parts_, k, O, kcT, ofree):
        h, j = i % 8, i % 2
        g, r = h // 4, 64 * (h % 2)
        pairs = [(vc[0:15, g, :], pcT[i // 8][0:15, h, :])]
        for n, (br, kt) in enumerate(parts_):
            pairs.append((heads[:, kt, (14, 18)[br] + g, :], pT[j][:, n * P:n * P + P]))
        pT_free[j] = group(O[r:r + 64, h // 2, :], pairs, k, k_vc, kcT, ofree)
        return pT_free[j]

    def evac_pair(dst, c0, t, b, k):
        v = psum[:, b, :].rearrange("p (c n) -> p c n", c=4)
        k = divide(v, dst[0][:, c0:c0 + 4, t * P:t * P + P], dst[1][:, c0:c0 + 4, t * P:t * P + P], k)
        give(b, k)
        return k

    rqT, rkT = (take(1024).rearrange("p (h n) -> p h n", h=4) for _ in range(2))

    def turn(dst, src, name, t):
        b, free = bank()
        k = transposes(psum[:, b, :], [src[:, t, h * P:h * P + P] for h in range(4)], kr[name], free)
        k = copy_act(dst[:, :, t * P:t * P + P], psum[:, b, :].rearrange("p (h n) -> p h n", h=4), k)
        give(b, k)
        return k

    RS = rqk_all[:, 0:1536].rearrange("p (h n) -> p h n", h=4)
    decay = const("decay").rearrange("p (h n) -> p h n", h=4)
    rss, rrs = stat(8), stat(8)

    def ret_scores(h):
        b, free = bank()
        group(psum[:, b, 0:256], [(rkT[:, h, 0:P], rqT[:, h, :])], k_rT, free)
        k = group(psum[:, b, 256:384], [(rkT[:, h, P:256], rqT[:, h, P:256])])
        tt(dve, RS[:, h, 0:256], psum[:, b, 0:256], decay[:, h, :], ALU.mult, k, in_consts)
        k = tt(dve, RS[:, h, 256:384], psum[:, b, 256:384], decay[:, h, 0:P], ALU.mult)
        give(b, k)
        return k

    def ret_out(t):
        b, free = bank()
        O = psum[:, b, :].rearrange("p (h n) -> p h n", h=4)
        for h in range(4):
            pairs = [(RS[:, h, t * P:t * P + P], rv[:, 0, h * P:h * P + P])]
            if t:
                pairs.append((RS[:, h, 256:384], rv[:, 1, h * P:h * P + P]))
            k = group(O[:, h, :], pairs, k_RS, kr["rv"], free)
        for h in range(4):
            k2 = sum_sq(rss[:, 4 * t + h:4 * t + h + 1], O[:, h, :], k)
        k_sq = k2
        k2 = rsqrt_mean(rrs[:, 4 * t:4 * t + 4], rss[:, 4 * t:4 * t + 4], P, k2)
        ro = rg[:, t, :].rearrange("p (h n) -> p h n", h=4)
        k = tt(dve, ro, O, ro, ALU.mult, k_sq, kr["rg"])
        give(b, [k, k2])
        return [k, k2]

    def ret_scale(t, k):
        ro = rg[:, t, :].rearrange("p (h n) -> p h n", h=4)
        return tt(dve, ro, ro, bc(rrs[:, 4 * t:4 * t + 4], 2, [P, 4, P]), ALU.mult, k)

    def ret_T(t, k):
        b, free = bank()
        k = transposes(psum[:, b, :], [rg[:, t, h * P:h * P + P] for h in range(4)], k, free)
        return evac_pair(retT, 0, t, b, k)

    done = None
    got = {}
    got[0] = scores(0)
    got[1] = scores(1)
    weighed = weigh(0, *got.pop(0))
    got[2] = scores(2)
    k_rT = [turn(rqT, rq, "rq", 0), turn(rkT, rk, "rk", 0)]
    kcT = {0: cmp_T(0)}
    flipped = {0: probs_T(0, *weighed)}
    for i in range(16):
        if i % 8 == 0:
            ob, ofree = bank()
            O = psum[:, ob, :].rearrange("p (c n) -> p c n", c=4)
        if i < 15:
            weighed = weigh(i + 1, *got.pop(i + 1))
        if i + 3 < 16:
            got[i + 3] = scores(i + 3)
        step()
        if i == 2:
            k_rT += [turn(rqT, rq, "rq", 1), turn(rkT, rk, "rk", 1)]
        if i == 3:
            kcT[1] = cmp_T(1)
        if 4 <= i < 8:
            k_RS = ret_scores(i - 4)
        if i in (9, 12):
            k_ro = ret_out((i - 9) // 3)
        if i in (10, 13):
            k_ro = ret_scale((i - 10) // 3, k_ro)
        if i in (11, 14):
            k_retT = ret_T((i - 11) // 3, k_ro)
        if i < 15:
            flipped[i + 1] = probs_T(i + 1, *weighed)
        done = pv(i, *flipped.pop(i), O, kcT[i // 8], ofree)
        if i % 8 == 7:
            k_nsaT = evac_pair(nsaT, 0, i // 8, ob, done)
    step(99)
    gates(sig, k_sig)

    def merge(wa, aT, ka, wb, bT, kb, sig, ksig, dst):
        got = {}

        def first(q, ps, tok):
            g = sig[:, 2 * q:2 * q + 2, :]
            got[q] = tt(dve, g, ps, g, ALU.mult, tok, ksig["g", q])
            return got[q]

        def second(q, ps, tok):
            g, f = sig[:, 8 + 2 * q:10 + 2 * q, :], sig[:, 2 * q:2 * q + 2, :]
            free = tt(dve, g, ps, g, ALU.mult, tok, ksig["g", 4 + q])
            k = tt(dve, g, g, f, ALU.add, free, got[q])
            done.extend([divide(g, dst[0][:, 2 * q:2 * q + 2, :], dst[1][:, 2 * q:2 * q + 2, :], k)] * 2)
            return free
        done = []
        run(fm(wa, 0, D, aT, ka, first), fm(wb, 0, D, bT, kb, second))
        return done

    k_mix = merge(a["w_proj_a"][0], nsaT, k_nsaT, a["w_proj_b"][0], retT, k_retT, sig, k_sig, xT)
    k_x = {}

    run(tm(a["w_out"][0], 0, D, xT, k_mix, to_residual))

    def mlp(pairs, up, w_down):
        bufs = [pair(4096 + 1024 * i, 2) for i in range(4)]
        banks = [bank() for _ in range(4)]
        for _, free in banks:
            pe.wait(free)
        done = [None] * 4
        ready = {}
        for q in range(pairs + 2):
            if q < pairs:
                ready[q] = up(q, bufs[q % 4], done[q % 4])
            if q < 2:
                continue
            q -= 2
            u = bufs[q % 4]
            pe.wait(ready[q])
            for h in range(2):
                tile = weight(w_down[256 * q:256 * q + 256, 512 * h:512 * h + 512], 2, 512)
                wh, wl, tok, _ = tile
                pe.wait(tok)
                for t in range(2):
                    ps = psum[:, banks[2 * h + t][0], :]
                    c = slice(t * P, t * P + P)
                    for k in range(2):
                        pe.part(mm(ps, u[0][:, k, c], wh[:, k, :], q == 0 and k == 0, False))
                        pe.part(mm(ps, u[0][:, k, c], wl[:, k, :], False, False))
                        f = mm(ps, u[1][:, k, c], wh[:, k, :], False, q == pairs - 1 and k == 1)
                        if k:
                            tok = pe.do(f)
                        else:
                            pe.part(f)
                    if q == pairs - 1:
                        b = banks[2 * h + t][0]
                        give(b, to_residual(h, t, psum[:, b, :], tok))
                used(tile, tok)
            done[q % 4] = tok

    h_ready = norm_T(lambda t: x[:, t, :], [k_x[0], k_x[1]], col("norm_mlp"), xT, shares=shares)
    tmps = [f32(8192 + 512 * i, 512).rearrange("p (c n) -> p c n", c=2) for i in range(4)]
    gens = fm(a["w_up"][0], 0, 4096, xT, h_ready, lambda q, ps, tok: up_evac(q, ps, tok))
    state = {}

    def up_evac(q, ps, tok):
        r = tmps[q % 4]
        k = fn(r, ps, ACT.Relu, tok)
        k = stt(r, ps, 0.0, r, ALU.max, ALU.mult, k)
        dst, free = state["dst"]
        state["k"] = divide(r, dst[0], dst[1], k, free)
        return k

    def up_relu2(q, dst, free):
        state["dst"] = dst, free
        next(gens)
        next(gens)
        return state["k"]

    twice[0] = True
    mlp(16, up_relu2, a["w_down"][0])
    twice[0] = False

    def last_norm(name):
        out_ = []
        for t in range(2):
            r, k = rsqrt_of(shares[t])
            out_.append(stt(x[:, t, :], x[:, t, :], r, row(name), ALU.mult, ALU.mult, k, k_x[t], in_rows))
        return out_
    at[0] = 8192
    w2 = a["w_in_2"][0]
    rs = [twice_rsqrt(t) for t in range(2)]
    h_ready = norm_T(lambda t: z[:, t, :], k_z, col("norm_mix_2"), xT, rs=[v[2:] for v in rs])
    k_y = [fn(x[:, t, :], z[:, t, :], ACT.Copy, rs[t][1], k_z[t], scale=rs[t][0]) for t in range(2)]
    dve.wait(k_y)
    raw = take(3108).rearrange("p (c n) -> p c n", c=12)
    cv = take(3072).rearrange("p (c n) -> p c n", c=12)
    k_pad = pool.do(lambda e: e.memset(raw[:, :, 0:3], 0.0), h_ready)
    cw = col("conv_w").rearrange("p (c k) -> p c k", k=4)
    k_cv = {}

    def to_conv(q, ps, tok):
        c = 2 * q
        k = copy_act(raw[:, c:c + 2, 3:259], ps, tok, free=True)
        dve.wait(k, k_pad)
        ks = [ts(dve, cv[:, i, :], raw[:, i, 0:256], cw[:, i, 0:1], col("conv_b")[:, i:i + 1], ALU.mult, ALU.add, free=True)
              for i in (c, c + 1)]
        for j in range(1, 4):
            for i in (c, c + 1):
                ks[i - c] = stt(cv[:, i, :], raw[:, i, j:j + 256], cw[:, i, j:j + 1], cv[:, i, :], ALU.mult, ALU.add,
                                ks[i - c], free=True)
        k_conv.append(ks)
        return k

    k_conv = []

    def silu_conv():
        q = len(k_cv)
        k_cv[q] = fn(cv[:, 2 * q:2 * q + 2, :], cv[:, 2 * q:2 * q + 2, :], ACT.Silu, k_conv[q], free=True)


    small = take(256)
    dt_, e_, s_, s2_, p_, aa = (small[:, 32 * i:32 * i + 32] for i in range(6))
    Aexp, e1, d0 = (small[:, 192 + 16 * i:208 + 16 * i] for i in range(3))
    k_Ae = fn(Aexp, row("ssd_A_log_2"), ACT.Exp, in_rows, h_ready)
    kdt = {}

    def to_dt(blk, t, ps, tok):
        kdt[t] = tt(dve, dt_[:, 16 * t:16 * t + 16], ps, row("ssd_dt_bias_2"), ALU.add, tok)
        return kdt[t]

    run(tm(w2, 2560, 16, xT, h_ready, to_dt))
    convs = fm(w2, 1024, 1536, xT, h_ready, to_conv)
    for _ in range(4):
        next(convs)
    dt3 = dt_.rearrange("p (t h) -> p t h", t=2)
    a3 = aa.rearrange("p (t h) -> p t h", t=2)

    def softplus():
        k = stt(e_, dt_, -1.0, dt_, ALU.mult, ALU.min, kdt[1])
        k = fn(e_, e_, ACT.Exp, k)
        k = ts(dve, s_, e_, 2.0, None, ALU.add, None, k)
        yield
        k = dve.do(lambda e: e.reciprocal(s_, s_), k)
        k = tt(dve, s_, s_, e_, ALU.mult, k)
        k = tt(dve, s2_, s_, s_, ALU.mult, k)
        yield
        k = ts(dve, p_, s2_, 1 / 17, None, ALU.mult, None, k)
        for c in (15, 13, 11, 9, 7, 5, 3):
            k = stt(p_, p_, 1 / c, s2_, ALU.add, ALU.mult, k)
            if c in (9, 3):
                yield
        k = stt(p_, p_, 1.0, s_, ALU.add, ALU.mult, k)
        k = ts(dve, p_, p_, 2.0, None, ALU.mult, None, k)
        k = kdt["dt"] = stt(dt_, dt_, 0.0, p_, ALU.max, ALU.add, k)
        kdt["a"] = stt(a3, dt3, -1.0, bc(Aexp, 1, [P, 2, 16]), ALU.mult, ALU.mult, k, k_Ae)
        yield

    parts_of = softplus()
    next(parts_of)
    while len(k_conv) < 6:
        next(convs)
        next(parts_of, None)
        next(convs)
        if len(k_conv) > 4:
            silu_conv()
    run(convs)
    for _ in parts_of:
        pass
    k_dt, k_a = kdt["dt"], kdt["a"]
    upper, after = const("upper"), const("after")
    flat = {}
    flat["at_zs"] = at[0]
    flat["zs"] = take(2048)
    zs = flat["zs"].rearrange("p (t n) -> p t n", t=2)
    gq = take(1024).rearrange("p (h n) -> p h n", h=4)
    flat["gk"] = take(1024)
    gk = flat["gk"].rearrange("p (h n) -> p h n", h=4)
    flat["gv"] = at[0]
    gv = take(2048).rearrange("p (t n) -> p t n", t=2)
    a1T = take(256)
    kg = {}

    def keep_a1(q, ps, tok):
        kg["a1"] = copy_act(a1T[0:16, :], ps[0:16, 0, :], tok)
        return kg["a1"]

    fill[0] = chain(tm(w2, 0, 1024, xT, h_ready, keep_tm(zs, kg, "z", ACT.Silu)),
                    fm(w2, 2576, 512, xT, h_ready, keep_fm(gq, kg, "q")),
                    fm(w2, 3088, 512, xT, h_ready, keep_fm(gk, kg, "k")),
                    fm(w2, 5648, 128, xT, h_ready, keep_a1),
                    tm(w2, 3600, 1024, xT, h_ready, keep_tm(gv, kg, "v", ACT.Copy)))

    flat["xs"] = take(2048)
    flat["sig"] = at[0] - 1024
    xs = flat["xs"].rearrange("p (t n) -> p t n", t=2)
    X = take(2048).rearrange("p (t n) -> p t n", t=2)
    Xd = take(1024)
    flat["CB"] = take(768)
    CB = flat["CB"].rearrange("p (g n) -> p g n", g=2)
    rot = [raw.rearrange("p c n -> p (c n)")[:, 512 * i:512 * i + 512].rearrange("p (h n) -> p h n", h=4)
           for i in range(6)]
    La, E = rot[0:3], rot[3:6]
    k_La, k_E, E_free, La_free = {}, {}, [None] * 3, [None] * 3
    quads = [(t, q) for t in range(2) for q in range(4)]

    def seg_in(i):
        t, q = quads[i]
        v = La[i % 3]
        k_La[i] = tt(dve, v, bc(after, 1, [P, 4, P]), bc(a3[:, t, 4 * q:4 * q + 4], 2, [P, 4, P]), ALU.mult,
               k_a, La_free[i % 3], free=i > 2)

    seg_in(0)
    seg_in(1)
    while len(k_cv) < 6:
        silu_conv()
    step(2)
    for t in range(2):
        for q in range(2):
            b, free = bank()
            k = transposes(psum[:, b, :], [cv[:, 4 * q + j, t * P:t * P + P] for j in range(4)],
                           k_cv[2 * q], k_cv[2 * q + 1], free)
            k_xs = copy_act(xs[:, t, 512 * q:512 * q + 512], psum[:, b, :], k)
            give(b, k_xs)
        k_X = tt(dve, X[:, t, :].rearrange("p (h d) -> p h d", h=16), xs[:, t, :].rearrange("p (h d) -> p h d", h=16),
                 bc(dt3[:, t, :], 2, [P, 16, 64]), ALU.mult, k_xs, k_dt)
    b, free = bank()
    group(psum[:, b, 0:16], [(upper, a3[:, 1, :])], k_a, free)
    k = group(psum[:, b, 16:32], [(after, a3[:, 0, :])])
    fn(e1, psum[:, b, 0:16], ACT.Exp, k)
    k_dec = fn(d0, psum[:, b, 16:32], ACT.Exp, k)
    give(b, k_dec)
    k_Xd = tt(dve, Xd.rearrange("p (h d) -> p h d", h=16), X[:, 0, :].rearrange("p (h d) -> p h d", h=16),
              bc(d0, 2, [P, 16, 64]), ALU.mult, k_X, k_dec)
    step()
    for g in range(2):
        b, free = bank()
        group(psum[:, b, 0:256], [(cv[:, 8 + g, 0:P], cv[:, 10 + g, :])], k_cv[4], k_cv[5], free)
        k = group(psum[:, b, 256:384], [(cv[:, 8 + g, P:256], cv[:, 10 + g, P:256])])
        v = psum[:, b, 0:384]
        dve.wait(k)
        tt(dve, CB[:, g, 0:P], v[:, 0:P], upper, ALU.mult)
        tt(dve, CB[:, g, 256:384], v[:, 256:384], upper, ALU.mult)
        k_CB = copy_dve(CB[:, g, P:256], v[:, P:256])
        give(b, k_CB)

    def seg(i):
        t, q = quads[i]
        v, k = La[i % 3], k_La[i]
        b, free = bank()
        for h in range(4):
            k = group(psum[:, b, h * P:h * P + P], [(v[:, h, :], upper)], k, free)
        La_free[i % 3] = k
        o = E[i % 3]
        k = fn(o, psum[:, b, :].rearrange("p (h n) -> p h n", h=4), ACT.Exp, k, E_free[i % 3])
        give(b, k)
        k_E[i] = tt(dve, o, o, bc(CB[:, q // 2, 256 * t:256 * t + P], 1, [P, 4, P]), ALU.mult, k, k_CB)

    yss, yrs = stat(4), stat(4)
    yT = pair(4096, 8)
    k_yT = None
    ybank = {}

    def diag(i):
        t, q = quads[i]
        g = q // 2
        if q % 2 == 0:
            ybank[t, g] = bank()
        b, free = ybank[t, g]
        for h in range(4):
            o = 256 * (q % 2) + 64 * h
            k = group(psum[:, b, o:o + 64], [(E[i % 3][:, h, :], X[:, t, 256 * q + 64 * h:256 * q + 64 * h + 64])],
                      k_E[i], k_X, free)
        E_free[i % 3] = k
        if q % 2 == 0:
            return
        c = slice(512 * g, 512 * g + 512)
        by_head = lambda v: v.rearrange("p (h d) -> p h d", h=8)
        Dr = bc(row("ssd_D_2")[:, 8 * g:8 * g + 8], 2, [P, 8, 64])
        y = xs[:, t, c]
        k2 = tt(dve, by_head(y), by_head(y), Dr, ALU.mult, in_rows)
        k2 = tt(dve, y, psum[:, b, :], y, ALU.add, k2, k)
        give(b, k2)
        if t:
            b, free = bank()
            k = group(psum[:, b, :], [(CB[:, g, P:256], Xd[:, c])], k_CB, k_Xd, free)
            x1 = X[:, 1, c]
            k = tt(dve, by_head(x1), by_head(psum[:, b, :]), bc(e1[:, 8 * g:8 * g + 8], 2, [P, 8, 64]), ALU.mult,
                   k, k_dec)
            give(b, k)
            k2 = tt(dve, y, y, x1, ALU.add, k, k2)
        k2 = tt(dve, y, y, zs[:, t, c], ALU.mult, k2, kg["z"])
        j = 2 * t + g
        k = sum_sq(yss[:, j:j + 1], y, k2)
        k = rsqrt_mean(yrs[:, j:j + 1], yss[:, j:j + 1], 512, k)
        k = ts(dve, y, y, yrs[:, j:j + 1], None, ALU.mult, None, k)
        k_y2[t, g] = k

    def y_out(t, g):
        y = xs[:, t, 512 * g:512 * g + 512]
        return gain_T(y, yT, 4 * g, t, bc(col("ssd_norm_2")[:, 4 * g:4 * g + 4], 2, [P, 4, P]), k_y2[t, g])

    k_y2 = {}
    seg_in(2)
    seg(0)
    seg(1)
    step(5)
    for i in range(8):
        if i + 3 < 8:
            seg_in(i + 3)
        if i + 2 < 8:
            seg(i + 2)
        step()
        diag(i)
        if i < 6:
            step()
        if i in (2, 4, 6):
            k_yT = y_out(*((0, 0), (0, 1), (1, 0))[i // 2 - 1])
    step(99)
    k_yT = y_out(1, 1)

    oT = pair(8192, 8)
    gr = f32(12288, 2048).rearrange("p (t n) -> p t n", t=2)

    la, bcum = (flat["zs"][:, i:i + 1024].rearrange("p (h n) -> p h n", h=4) for i in (0, 1024))
    kt_ = la
    kh = flat["xs"][:, 0:1024].rearrange("p (h n) -> p h n", h=4)
    sig = f32(flat["sig"], 4096).rearrange("p (c n) -> p c n", c=16)
    ST = [flat["gk"][:, 0:512], flat["gk"][:, 512:1024], flat["CB"][:, 0:512]]
    ST = [v.rearrange("p (h n) -> p h n", h=4) for v in ST]
    ke, qe = (take(512).rearrange("p (h n) -> p h n", h=4) for _ in range(2))
    dec = take(16)
    tmpg = big[:, 0, :].rearrange("p (h n) -> p h n", h=4)
    k_sig = {}
    fill[0] = chain(tm(w2, 4624, 1024, xT, h_ready, keep_tm(gr, kg, "r", ACT.Copy)),
                    fm(w2, 5664, 2048, xT, h_ready, keep_fm(sig, k_sig, "g")))
    act.wait(k_yT)
    step(4)

    for i in range(2):
        b, free = bank()
        for s in range(2):
            h = 2 * i + s
            k = group(psum[:, b, 256 * s:256 * s + 256], [(wa2[:, h * P:h * P + P], a1T[0:16, :])],
                      kg["a1"], in_wa2, free)
        for s in range(2):
            h = 2 * i + s
            k_la = ts(dve, la[:, h, :], psum[:, b, 256 * s:256 * s + 256], col("gla_b")[:, h:h + 1], None,
                      ALU.add, None, k, k_yT)
        give(b, k_la)
    k = stt(tmpg, la, -1.0, la, ALU.mult, ALU.min, k_la)
    k = fn(tmpg, tmpg, ACT.Exp, k)
    k = fn(tmpg, tmpg, ACT.Ln, k, bias=1.0)
    k = stt(la, la, 0.0, tmpg, ALU.min, ALU.subtract, k)
    for h in range(4):
        k_b = dve.do(lambda e, h=h: e.tensor_tensor_scan(bcum[:, h, :], const("keep"), la[:, h, :], 0.0,
                                                         ALU.mult, ALU.add), k)
    step()
    k = fn(tmpg, bcum, ACT.Exp, k_b, scale=1 / 16)
    k_qt = stt(gq, gq, P ** -0.5, tmpg, ALU.mult, ALU.mult, k, kg["q"])
    k = fn(kt_, bcum, ACT.Exp, k_b, scale=-1 / 16)
    k_kt = tt(dve, kt_, kt_, gk, ALU.mult, k, kg["k"])
    step(4)
    by_chunk = lambda v: v.rearrange("p h (c n) -> p (h c) n", c=4)
    last = by_chunk(bcum)[:, :, 63:64]
    k = tt(dve, by_chunk(kh), last.to_broadcast([P, 16, 64]), by_chunk(bcum), ALU.subtract, k_b)
    k = fn(kh, kh, ACT.Exp, k, scale=1 / 16)
    k_kh = tt(dve, kh, kh, gk, ALU.mult, k)
    k_dec = fn(dec.unsqueeze(2), last, ACT.Exp, k_b, scale=1 / 16)
    step(2)
    dec3 = dec.rearrange("p (h c) -> p h c", c=4)
    dve.wait(k_dec)
    tt(dve, ke[:, :, 0:64], kh[:, :, 0:64], dec3[:, :, 1:2].to_broadcast([P, 4, 64]), ALU.mult)
    copy_dve(ke[:, :, 64:P], kh[:, :, 64:P])
    tt(dve, qe[:, :, 64:P], gq[:, :, 192:256], dec3[:, :, 2:3].to_broadcast([P, 4, 64]), ALU.mult)
    k_e2 = copy_dve(qe[:, :, 0:64], gq[:, :, P:192])
    step()

    step(4)
    for t in range(2):
        b, free = bank()
        c0, c1 = 2 * t * 64, 2 * t * 64 + 64
        for h in range(4):
            o = psum[:, b, h * P:h * P + P]
            group(o[0:64, 0:64], [(kt_[:, h, c0:c1], gq[:, h, c0:c1])], k_qt, k_kt, k_kh, free)
            group(o[0:64, 64:P], [(kh[:, h, c0:c1], gq[:, h, c1:c1 + 64])])
            k = group(o[64:P, :], [(kt_[:, h, c1:c1 + 64], gq[:, h, c0:c1 + 64])])
        k_ST = tt(dve, ST[t], psum[:, b, :].rearrange("p (h n) -> p h n", h=4), bc(upper, 1, [P, 4, P]),
                  ALU.mult, k)
        give(b, k_ST)
        step()
    b, free = bank()
    for h in range(4):
        k = group(psum[:, b, h * P:h * P + P], [(ke[:, h, :], qe[:, h, :])], k_e2, free)
    k_ST = copy_dve(ST[2], psum[:, b, :].rearrange("p (h n) -> p h n", h=4), k)
    give(b, k_ST)
    mem = flat["zs"].rearrange("p (t n) -> p t n", t=2)
    in_mem = sp.dma(m["s_mem"], 16, mem, a["mem_2"].rearrange("b (t p) d -> p (b t) d", p=P), k_ST)
    step()
    kg["r"] = fn(gr, gr, ACT.Silu, kg["r"])
    outs = []

    def gain_out():
        o, j, k = outs.pop(0)
        t, c0 = j // 4, 2 * (j % 4)
        o2 = o.rearrange("p (h n) -> p h n", h=2)
        k = tt(dve, o2, o2, bc(grs[:, j:j + 2], 2, [P, 2, 256]), ALU.mult, k)
        step()
        return gain_T(o, oT, c0, t, col("gla_norm_2").unsqueeze(1).unsqueeze(3).to_broadcast([P, 2, 2, P]), k)

    gss, grs = stat(8), stat(8)
    for t in range(2):
        for i in range(2):
            b, free = bank()
            for s in range(2):
                h = 2 * i + s
                pairs = [(ST[t][:, h, :], gv[:, t, 256 * h:256 * h + 256])]
                if t:
                    pairs.append((ST[2][:, h, :], gv[:, 0, 256 * h:256 * h + 256]))
                k = group(psum[:, b, 256 * s:256 * s + 256], pairs, k_ST, kg["v"], free)
            j = 4 * t + 2 * i
            for s in range(2):
                k2 = sum_sq(gss[:, j + s:j + s + 1], psum[:, b, 256 * s:256 * s + 256], k)
            k_sq = k2
            k2 = rsqrt_mean(grs[:, j:j + 2], gss[:, j:j + 2], 256, k2)
            o = gr[:, t, 512 * i:512 * i + 512]
            k = tt(dve, o, psum[:, b, :], o, ALU.mult, k_sq, kg["r"])
            give(b, [k, k2])
            outs.append((o, j, [k, k2]))
            if len(outs) > 1:
                gain_out()
    k_oT = gain_out()
    memT = pair(flat["at_zs"] + 2048, 8)
    k_mem = norm_T(lambda t: mem[:, t, :], [in_mem, in_mem], col("norm_mem_2"), memT, [k, k_oT])
    step(99)
    gates(sig, k_sig)
    k_mix = merge(a["w_up_ssd_2"][0], yT, k_yT, a["w_up_gla_2"][0], oT, k_oT, sig, k_sig, xT)
    run(tm(a["w_o_2"][0], 0, D, xT, k_mix, to_residual))

    kx = [k_x[0], k_x[1]]
    mkT = f32(10240, 2048).rearrange("p (c n) -> p c n", c=8)
    mv = f32(flat["sig"], 2048).rearrange("p (t n) -> p t n", t=2)
    qx = f32(flat["sig"] + 2048, 2048).rearrange("p (c n) -> p c n", c=8)
    px = f32(flat["sig"] + 4096, 2048).rearrange("p (t h n) -> p t h n", t=2, h=4)
    pxT = f32(8192, 2048).rearrange("p (h m n) -> p h m n", h=4, m=2)
    oxT = pair(4096, 8)
    wkv = a["w_xkv_2"][0]
    fill[0] = chain(fm(wkv, 0, D, memT, k_mem, keep_fm(mkT, kg, "mk")),
                    tm(wkv, D, D, memT, k_mem, keep_tm(mv, kg, "mv", ACT.Copy)))
    step()
    h_ready = norm_T(lambda t: x[:, t, :], kx, col("norm_xattn_2"), xT, shares=shares)
    step(2)
    run(fm(a["w_xq_2"][0], 0, D, xT, h_ready, keep_fm(qx, kg, "qx")))
    xm, xden = stat(8), stat(8)

    def x_scores(h):
        b, free = bank()
        S = psum[:, b, :].rearrange("p (t n) -> p t n", t=2)
        for t in range(2):
            k = group(S[:, t, :], [(qx[:, 2 * h + c, t * P:t * P + P], mkT[:, 2 * h + c, :]) for c in range(2)],
                      kg["qx", h], kg["mk", h], free)
        mx, d = xm[:, 2 * h:2 * h + 2], xden[:, 2 * h:2 * h + 2]
        k = dve.do(lambda e: e.tensor_reduce(mx, S, AX.X, ALU.max), k)
        k = ts(dve, mx, mx, -1 / 16, None, ALU.mult, None, k)
        for t in range(2):
            k2 = fn(px[:, t, h, :], S[:, t, :], ACT.Exp, k, bias=mx[:, t:t + 1], scale=1 / 16, accum_out=d[:, t:t + 1])
        give(b, k2)
        k = dve.do(lambda e: e.reciprocal(d, d), k2)
        return tt(dve, px[:, :, h, :], px[:, :, h, :], bc(d, 2, [P, 2, 256]), ALU.mult, k)

    def x_out(h, k):
        b, free = bank()
        k = transposes(psum[:, b, :], [px[:, t, h, c * P:c * P + P] for c in range(2) for t in range(2)], k, free)
        k = copy_act(pxT[:, h, :, :], psum[:, b, :].rearrange("p (m n) -> p m n", m=2), k)
        give(b, k)
        b, free = bank()
        pe.wait(k)
        for c in range(2):
            f = 256 * h + 128 * c
            k = group(psum[:, b, 256 * c:256 * c + 256], [(mv[:, i, f:f + P], pxT[:, h, i, :]) for i in range(2)],
                      kg["mv"], free)
        v = psum[:, b, :].rearrange("p (c n) -> p c n", c=2)
        k = divide(v, oxT[0][:, 2 * h:2 * h + 2, :], oxT[1][:, 2 * h:2 * h + 2, :], k)
        give(b, k)
        return k

    k_px = []
    for h in range(4):
        k_px.append(x_scores(h))
        step(2)
    step(99)
    k_ox = []
    for h in range(4):
        k_ox.extend([x_out(h, k_px[h])] * 2)
    run(tm(a["w_xo_2"][0], 0, D, oxT, k_ox, to_residual))

    kx = [k_x[0], k_x[1]]
    h_ready = norm_T(lambda t: x[:, t, :], kx, col("norm_ffn_2"), xT, shares=shares)
    wf = a["w_ffn_in_2"][0]

    def gate_evac(q, ps, tok):
        state["gate"] = fn(tmps[q % 4], ps, ACT.Silu, tok)
        return state["gate"]

    def prod_evac(q, ps, tok):
        r = tmps[q % 4]
        k = tt(dve, r, ps, r, ALU.mult, tok, state["gate"])
        dst, free = state["dst"]
        state["k"] = divide(r, dst[0], dst[1], k, free)
        return k

    gates = fm(wf, 0, 2816, xT, h_ready, gate_evac)
    prods = fm(wf, 2816, 2816, xT, h_ready, prod_evac)

    def up_swiglu(q, dst, free):
        state["dst"] = dst, free
        for g in (gates, gates, prods, prods):
            next(g)
        return state["k"]

    mlp(11, up_swiglu, a["w_ffn_out_2"][0])
    k_y = last_norm("norm_final_2")
    sp.dma(m["s_out"], 16, out.rearrange("b (t p) d -> p (b t) d", p=P), x[:, :, :], *k_y)
    sp.wait((m["s_out"], 16))
    settle()
    return (pe, act, dve, pool, sp), wanted


def shape_constants():
    i = np.arange(P)
    v = {}
    v["upper"] = i[:, None] <= i[None, :]
    v["after"] = i[:, None] > i[None, :]
    v["causal"] = np.where(i[None, :] <= i[:, None], 0.0, NEG)
    end = 16 * np.arange(15) + 31
    tok = i[:, None] + P * np.arange(2)[None, :]
    v["cmask"] = np.where(end[None, None, :] <= tok[:, :, None], 0.0, NEG).reshape(P, 30)
    v["crow"] = tok >= 31
    lg = np.log(1.0 - np.exp2(-5.0 - np.arange(4)))
    rel = np.arange(256)[None, :] - i[:, None]
    v["decay"] = np.concatenate([np.where(rel >= 0, np.exp(g * np.maximum(rel, 0)), 0.0) * P ** -0.5 for g in lg], 1)
    v["inv"] = np.tile(np.array(INV_BITS, np.uint32).view(np.float32)[None, :], (P, 1))
    v["keep"] = np.tile((np.arange(256) % 64 != 0)[None, :], (P, 1))
    return np.ascontiguousarray(np.concatenate([np.asarray(v[n], np.float32) for n in CONSTS], 1))


INV_BITS = [
    0x3f800000, 0x3e4693b0, 0x3d1a08c9, 0x3beef752, 0x3ab95d24, 0x398fc8f8, 0x385f10cb, 0x372d07a6, 0x3f800000,
    0x3f5dafd6, 0x3f3ff911, 0x3f263de0, 0x3f0ff59a, 0x3ef953ce, 0x3ed7e89a, 0x3ebaf81a, 0x3ea1e89b, 0x3e8c3503,
    0x3e72d422, 0x3e5247ed, 0x3e361887, 0x3e1db040, 0x3e088d77, 0x3dec7fd5, 0x3dcccccc, 0x3db15978, 0x3d99940d,
    0x3d84fe4c, 0x3d6655c1, 0x3d477640, 0x3d2cba16, 0x3d159348, 0x3d0186e2, 0x3ce054d1, 0x3cc2434e, 0x3ca83989,
    0x3c91ad3a, 0x3c7c4d30, 0x3c5a7bf1, 0x3c3d330e, 0x3c23d70a, 0x3c0de12e, 0x3bf5b9ad, 0x3bd4ca16, 0x3bb8449a,
    0x3b9f91cc, 0x3b8a2e75, 0x3b6f520d, 0x3b4f3e33, 0x3b33770d, 0x3b1b690e, 0x3b06946d, 0x3ae91528, 0x3ac9d759,
    0x3aaec98d, 0x3a975c0b, 0x3a83126e, 0x3a6301e3, 0x3a44948a, 0x3a2a3b44, 0x3a136a14, 0x39ff4fac, 0x39dd1722,
    0x39bf74d6, 0x39a5cb60, 0x398f9275, 0x3978a80d, 0x395753e2, 0x393a7753, 0x39217918, 0x390bd46d, 0x38f22cdd]


WEIGHTS = ["x", "w_in", "cmp_k_w1", "cmp_k_w2", "cmp_v_w1", "cmp_v_w2", "w_proj_a", "w_proj_b", "w_out", "w_up",
           "w_down", "norm_final", "mem_2", "w_in_2", "ssd_dt_bias_2", "ssd_A_log_2", "ssd_D_2", "gla_w_a2_2",
           "w_up_ssd_2", "w_up_gla_2", "w_o_2", "w_xq_2", "w_xkv_2", "w_xo_2", "w_ffn_in_2", "w_ffn_out_2",
           "norm_final_2"]


def kernel(**inputs):
    import concourse.bacc as bacc
    from concourse.bass_utils import run_bass_kernel_spmd

    get = {n: np.asarray(v) for n, v in inputs.items()}

    def by_column(v):
        return v.reshape(-1, P).T

    cols = {n: by_column(get[n]) for n in ("norm_mix", "norm_mlp", "norm_mix_2", "ssd_norm_2", "gla_norm_2",
                                            "norm_xattn_2", "norm_mem_2", "norm_ffn_2")}
    cols["conv_w"] = get["ssd_conv_w_2"].reshape(4, 12, P).transpose(2, 1, 0).reshape(P, 48)
    cols["conv_b"] = by_column(get["ssd_conv_b_2"])
    cols["gla_b"] = by_column(get["gla_b_a_2"])
    cols["pe_k"] = by_column(get["cmp_pos_k"])
    cols["pe_v"] = by_column(get["cmp_pos_v"])
    arrays = {n: np.ascontiguousarray(get[n]) for n in WEIGHTS}
    arrays["cols"] = np.ascontiguousarray(np.concatenate([cols[n] for n in COLS], 1))
    arrays["pos"] = np.ascontiguousarray(get["positions"].reshape(2, P).T)
    arrays["consts"] = shape_constants()
    arrays["ident"] = np.eye(P, dtype=np.float32)

    nc = bacc.Bacc("TRN2", target_bir_lowering=False, num_devices=1)
    aps = {n: nc.dram_tensor(f"in_{n}", v.shape, mybir.dt.from_np(v.dtype), kind="ExternalInput").ap()
           for n, v in arrays.items()}
    out = nc.dram_tensor("out_0", (1, 256, D), F32, kind="ExternalOutput").ap()
    build(nc, aps, out)
    r = run_bass_kernel_spmd(nc, [{f"in_{n}": v for n, v in arrays.items()}], core_ids=[0])
    return r.results[0]["out_0"]
```
